# Optimizing a Trainium2 kernel written in Bass

```python
import jax
import jax.numpy as jnp
from jax import lax
import numpy as np

D_MODEL = 1024
BATCH = 1
SEQ = 512
DEPTH = 1

RWKV_HEAD = 64
RWKV_WIDTH = D_MODEL
RWKV_HEADS = RWKV_WIDTH // RWKV_HEAD
DECAY_LORA = 64
ICLR_LORA = 64
VALUE_LORA = 32
GATE_LORA = 128
RWKV_GN_EPS = 64e-5
MAMBA_EXPAND = 2
MAMBA_INNER = MAMBA_EXPAND * D_MODEL
MAMBA_HEAD = 64
MAMBA_HEADS = MAMBA_INNER // MAMBA_HEAD
MAMBA_GROUPS = 4
MAMBA_STATE = 128
MAMBA_CONV = 4
SSD_CHUNK = 128
MAMBA_XBC = MAMBA_INNER + 2 * MAMBA_GROUPS * MAMBA_STATE
RWKV_COLS = 3 * RWKV_WIDTH + DECAY_LORA + ICLR_LORA + GATE_LORA
MAMBA_COLS = MAMBA_INNER + MAMBA_XBC + MAMBA_HEADS
GATE_COLS = 2 * D_MODEL
IN_COLS = RWKV_COLS + MAMBA_COLS + GATE_COLS
N_EXPERT_GROUPS = 4
EXPERTS_PER_GROUP = 8
N_EXPERTS = N_EXPERT_GROUPS * EXPERTS_PER_GROUP
TOP_K_INNER = 2
EXPERT_FF = D_MODEL // 2
EXPERT_BLOCK = 256
NORM_EPS = 1e-6

kernel_name = 'hybrid_rwkv7_mamba2_hmoe_block'

def _rmsnorm(x, g):
    xf = x.astype(jnp.float32)
    y = xf * lax.rsqrt(jnp.mean(xf * xf, axis=-1, keepdims=True) + NORM_EPS)
    return (y * g.astype(jnp.float32)).astype(x.dtype)

def _token_shift(u):
    return jnp.pad(u[:, :-1], ((0, 0), (1, 0), (0, 0)))

def _wkv7(r, decay, k, v, a_vec, b_vec):
    bsz, _, nh, n = r.shape

    def step(state, inp):
        r_t, w_t, k_t, v_t, a_t, b_t = inp
        sa = jnp.einsum('bhvk,bhk->bhv', state, a_t)
        state = (state * w_t[:, :, None, :] + sa[..., None] * b_t[:, :, None, :]
                 + v_t[..., None] * k_t[:, :, None, :])
        return state, jnp.einsum('bhvk,bhk->bhv', state, r_t)

    xs = tuple(jnp.swapaxes(t, 0, 1) for t in (r, decay, k, v, a_vec, b_vec))
    state0 = jnp.zeros((bsz, nh, n, n), jnp.float32)
    _, y = lax.scan(step, state0, xs)
    return jnp.swapaxes(y, 0, 1)

def _rwkv7_branch(u, h, v_first, v_res, mu, w0, w_decay2, a0, w_iclr2, w_gate2,
                  k_k, k_a, r_k, lnx_g, lnx_b, w_o):
    bsz, s, _ = u.shape
    u = u.astype(jnp.float32)
    u = u + (_token_shift(u) - u) * mu
    splits = [RWKV_WIDTH, 2 * RWKV_WIDTH, 3 * RWKV_WIDTH,
              3 * RWKV_WIDTH + DECAY_LORA, 3 * RWKV_WIDTH + DECAY_LORA + ICLR_LORA]
    r, k, v, w_lo, a_lo, g_lo = jnp.split(u, splits, axis=-1)
    w = -jax.nn.softplus(-(w0 + jnp.tanh(w_lo) @ w_decay2)) - 0.5
    decay = jnp.exp(-jnp.exp(w))
    a = jax.nn.sigmoid(a0 + a_lo @ w_iclr2)
    g = jax.nn.sigmoid(g_lo) @ w_gate2
    if v_res is not None:
        w_v1, mu_v, v0, w_v2 = v_res
        v_lo = (h @ w_v1).astype(jnp.float32)
        v_lo = v_lo + (_token_shift(v_lo) - v_lo) * mu_v
        v = v + (v_first - v) * jax.nn.sigmoid(v0 + v_lo @ w_v2)
    heads = lambda t: t.reshape(bsz, s, RWKV_HEADS, RWKV_HEAD)
    kk = heads(k * k_k)
    kk = kk / jnp.maximum(jnp.linalg.norm(kk, axis=-1, keepdims=True), 1e-12)
    k = k * (1.0 + (a - 1.0) * k_a)
    r_h, k_h, v_h, a_h, d_h = heads(r), heads(k), heads(v), heads(a), heads(decay)
    y = _wkv7(r_h, d_h, k_h, v_h, -kk, kk * a_h)
    mean = jnp.mean(y, axis=-1, keepdims=True)
    var = jnp.mean(jnp.square(y - mean), axis=-1, keepdims=True)
    y = ((y - mean) * lax.rsqrt(var + RWKV_GN_EPS)).reshape(bsz, s, RWKV_WIDTH) * lnx_g + lnx_b
    bonus = jnp.sum(r_h * k_h * r_k, axis=-1, keepdims=True) * v_h
    y = y + bonus.reshape(bsz, s, RWKV_WIDTH)
    return (y * g) @ w_o, v

def _causal_dwconv(u, w, b):
    kw, c = w.shape
    out = lax.conv_general_dilated(u, w[:, None, :].astype(u.dtype), window_strides=(1,),
                                   padding=[(kw - 1, 0)], dimension_numbers=('NWC', 'WIO', 'NWC'),
                                   feature_group_count=c)
    return out + b

def _ssd(xh, dt, a_head, bm, cm):
    b, s, nh, p = xh.shape
    g, n = bm.shape[2], bm.shape[3]
    hg = nh // g
    nc = s // SSD_CHUNK
    ln = SSD_CHUNK
    xdt = jnp.moveaxis((xh * dt[..., None]).reshape(b, nc, ln, g, hg, p), 1, 0)
    adt = jnp.moveaxis((dt * a_head).reshape(b, nc, ln, g, hg), 1, 0)
    bc = jnp.moveaxis(bm.reshape(b, nc, ln, g, n), 1, 0)
    cc = jnp.moveaxis(cm.reshape(b, nc, ln, g, n), 1, 0)
    causal = jnp.tril(jnp.ones((ln, ln), bool))[None, :, :, None, None]

    def chunk_step(state, inp):
        x_c, a_c, b_c, c_c = inp
        a_cs = jnp.cumsum(a_c, axis=1)
        seg = a_cs[:, :, None] - a_cs[:, None, :]
        decay_ls = jnp.exp(jnp.where(causal, seg, -jnp.inf))
        cb = jnp.einsum('blgn,bsgn->blsg', c_c, b_c)
        y_diag = jnp.einsum('blsg,blsgj,bsgjp->blgjp', cb, decay_ls, x_c)
        y_off = jnp.einsum('blgn,bgjpn,blgj->blgjp', c_c, state, jnp.exp(a_cs))
        a_last = a_cs[:, -1]
        to_end = jnp.exp(a_last[:, None] - a_cs)
        new_state = (state * jnp.exp(a_last)[..., None, None]
                     + jnp.einsum('blgn,blgj,blgjp->bgjpn', b_c, to_end, x_c))
        return new_state, y_diag + y_off

    state0 = jnp.zeros((b, g, hg, p, n), jnp.float32)
    _, y = lax.scan(chunk_step, state0, (xdt, adt, bc, cc))
    return jnp.moveaxis(y, 0, 1).reshape(b, s, nh, p)

def _mamba2_branch(m, conv_w, conv_b, dt_bias, a_log, d_skip, mnorm_g, w_o):
    bsz, s, _ = m.shape
    z, xbc, dt_raw = jnp.split(m.astype(jnp.float32), [MAMBA_INNER, MAMBA_INNER + MAMBA_XBC], axis=-1)
    xbc = jax.nn.silu(_causal_dwconv(xbc, conv_w.astype(jnp.float32), conv_b))
    xs, bm, cm = jnp.split(xbc, [MAMBA_INNER, MAMBA_INNER + MAMBA_GROUPS * MAMBA_STATE], axis=-1)
    xh = xs.reshape(bsz, s, MAMBA_HEADS, MAMBA_HEAD)
    bm = bm.reshape(bsz, s, MAMBA_GROUPS, MAMBA_STATE)
    cm = cm.reshape(bsz, s, MAMBA_GROUPS, MAMBA_STATE)
    dt = jax.nn.softplus(dt_raw + dt_bias)
    a_head = -jnp.exp(a_log.astype(jnp.float32))
    y = _ssd(xh, dt, a_head, bm, cm) + xh * d_skip[:, None]
    y = y.reshape(bsz, s, MAMBA_INNER) * jax.nn.silu(z)
    yg = y.reshape(bsz, s, MAMBA_GROUPS, MAMBA_INNER // MAMBA_GROUPS)
    yg = yg * lax.rsqrt(jnp.mean(yg * yg, axis=-1, keepdims=True) + 1e-5)
    y = yg.reshape(bsz, s, MAMBA_INNER) * mnorm_g
    return y @ w_o

def _hier_moe(h, w_rg, b_rg, w_re, b_re, w_e1, w_e3, w_e2):
    bsz, s, d = h.shape
    t = bsz * s
    hf = h.reshape(t, d)
    g_prob = jax.nn.softmax((hf @ w_rg).astype(jnp.float32) + b_rg, axis=-1)
    g_p, g_idx = lax.top_k(g_prob, 1)
    e_logits = ((hf @ w_re).astype(jnp.float32) + b_re).reshape(t, N_EXPERT_GROUPS, EXPERTS_PER_GROUP)
    e_sel = jnp.take_along_axis(e_logits, g_idx[:, :, None], axis=1)[:, 0]
    e_p, e_idx = lax.top_k(jax.nn.softmax(e_sel, axis=-1), TOP_K_INNER)
    e_p = e_p / jnp.sum(e_p, axis=-1, keepdims=True)
    weights = (g_p * e_p).reshape(-1)
    eid = (g_idx * EXPERTS_PER_GROUP + e_idx).reshape(-1).astype(jnp.int32)
    tok = jnp.repeat(jnp.arange(t, dtype=jnp.int32), TOP_K_INNER)
    n_assign = t * TOP_K_INNER
    order = jnp.argsort(eid)
    se, stok, sw = eid[order], tok[order], weights[order]
    counts = jnp.bincount(eid, length=N_EXPERTS)
    offsets = jnp.cumsum(counts) - counts
    pcounts = (counts + EXPERT_BLOCK - 1) // EXPERT_BLOCK * EXPERT_BLOCK
    pends = jnp.cumsum(pcounts)
    poffsets = pends - pcounts
    pos = poffsets[se] + (jnp.arange(n_assign, dtype=jnp.int32) - offsets[se])
    n_blocks = -(-(n_assign + N_EXPERTS * (EXPERT_BLOCK - 1)) // EXPERT_BLOCK)
    n_rows = n_blocks * EXPERT_BLOCK
    buf_tok = jnp.zeros((n_rows,), jnp.int32).at[pos].set(stok)
    buf_w = jnp.zeros((n_rows,), jnp.float32).at[pos].set(sw)
    block_start = jnp.arange(n_blocks, dtype=jnp.int32) * EXPERT_BLOCK
    block_e = jnp.minimum(jnp.searchsorted(pends, block_start, side='right'), N_EXPERTS - 1)
    xb = hf[buf_tok].reshape(n_blocks, EXPERT_BLOCK, d)

    def expert_block(args):
        xblk, e = args
        hid = jax.nn.silu(xblk @ w_e1[e]) * (xblk @ w_e3[e])
        return hid @ w_e2[e]

    yb = lax.map(expert_block, (xb, block_e)).reshape(n_rows, d)
    y = jax.ops.segment_sum(yb * buf_w[:, None].astype(yb.dtype), buf_tok, num_segments=t)
    return y.reshape(bsz, s, d).astype(h.dtype)

def setup_inputs(seed: int = 0) -> dict:
    key = jax.random.key(seed)
    ks = jax.random.split(key, 40)
    f32 = jnp.float32
    nrm = lambda k, shape, scale: jax.random.normal(k, shape, f32) * scale
    uni = lambda k, shape, lo, hi: jax.random.uniform(k, shape, f32, minval=lo, maxval=hi)
    nv = DEPTH - 1
    dt = jnp.exp(uni(ks[21], (DEPTH, MAMBA_HEADS), float(np.log(1e-3)), float(np.log(1e-1))))
    return {
        'x': nrm(ks[0], (BATCH, SEQ, D_MODEL), 1.0),
        'norm1_g': 1.0 + nrm(ks[1], (DEPTH, D_MODEL), 0.02),
        'w_in': nrm(ks[2], (DEPTH, D_MODEL, IN_COLS), D_MODEL ** -0.5),
        'mu_rwkv': uni(ks[3], (DEPTH, RWKV_COLS), 0.0, 1.0),
        'w0': uni(ks[4], (DEPTH, RWKV_WIDTH), -5.0, 1.0),
        'w_decay2': nrm(ks[5], (DEPTH, DECAY_LORA, RWKV_WIDTH), 0.1 * DECAY_LORA ** -0.5),
        'a0': nrm(ks[6], (DEPTH, RWKV_WIDTH), 0.1),
        'w_iclr2': nrm(ks[7], (DEPTH, ICLR_LORA, RWKV_WIDTH), 0.1 * ICLR_LORA ** -0.5),
        'w_gate2': nrm(ks[8], (DEPTH, GATE_LORA, RWKV_WIDTH), GATE_LORA ** -0.5),
        'k_k': 0.85 + nrm(ks[9], (DEPTH, RWKV_WIDTH), 0.02),
        'k_a': 1.0 + nrm(ks[10], (DEPTH, RWKV_WIDTH), 0.02),
        'r_k': nrm(ks[11], (DEPTH, RWKV_HEADS, RWKV_HEAD), 0.1),
        'lnx_g': 1.0 + nrm(ks[12], (DEPTH, RWKV_WIDTH), 0.02),
        'lnx_b': nrm(ks[13], (DEPTH, RWKV_WIDTH), 0.01),
        'w_rwkv_o': nrm(ks[14], (DEPTH, RWKV_WIDTH, D_MODEL), RWKV_WIDTH ** -0.5),
        'w_v1': nrm(ks[15], (nv, D_MODEL, VALUE_LORA), D_MODEL ** -0.5),
        'mu_v': uni(ks[16], (nv, VALUE_LORA), 0.0, 1.0),
        'v0': nrm(ks[17], (nv, RWKV_WIDTH), 0.1),
        'w_v2': nrm(ks[18], (nv, VALUE_LORA, RWKV_WIDTH), 0.1 * VALUE_LORA ** -0.5),
        'conv_w': nrm(ks[19], (DEPTH, MAMBA_CONV, MAMBA_XBC), MAMBA_CONV ** -0.5),
        'conv_b': nrm(ks[20], (DEPTH, MAMBA_XBC), 0.01),
        'dt_bias': dt + jnp.log(-jnp.expm1(-dt)),
        'a_log': jnp.log(uni(ks[22], (DEPTH, MAMBA_HEADS), 1.0, 16.0)),
        'd_skip': 1.0 + nrm(ks[23], (DEPTH, MAMBA_HEADS), 0.02),
        'mnorm_g': 1.0 + nrm(ks[24], (DEPTH, MAMBA_INNER), 0.02),
        'w_mamba_o': nrm(ks[25], (DEPTH, MAMBA_INNER, D_MODEL), MAMBA_INNER ** -0.5),
        'w_out': nrm(ks[26], (DEPTH, D_MODEL, D_MODEL), D_MODEL ** -0.5),
        'norm2_g': 1.0 + nrm(ks[27], (DEPTH, D_MODEL), 0.02),
        'w_rg': nrm(ks[28], (DEPTH, D_MODEL, N_EXPERT_GROUPS), D_MODEL ** -0.5),
        'b_rg': nrm(ks[29], (DEPTH, N_EXPERT_GROUPS), 0.01),
        'w_re': nrm(ks[30], (DEPTH, D_MODEL, N_EXPERTS), D_MODEL ** -0.5),
        'b_re': nrm(ks[31], (DEPTH, N_EXPERTS), 0.01),
        'w_e1': nrm(ks[32], (DEPTH, N_EXPERTS, D_MODEL, EXPERT_FF), D_MODEL ** -0.5),
        'w_e3': nrm(ks[33], (DEPTH, N_EXPERTS, D_MODEL, EXPERT_FF), D_MODEL ** -0.5),
        'w_e2': nrm(ks[34], (DEPTH, N_EXPERTS, EXPERT_FF, D_MODEL), EXPERT_FF ** -0.5),
        'final_g': 1.0 + nrm(ks[35], (D_MODEL,), 0.02),
    }

def reference(x, norm1_g, w_in, mu_rwkv, w0, w_decay2, a0, w_iclr2, w_gate2, k_k, k_a, r_k,
              lnx_g, lnx_b, w_rwkv_o, w_v1, mu_v, v0, w_v2, conv_w, conv_b, dt_bias, a_log,
              d_skip, mnorm_g, w_mamba_o, w_out, norm2_g, w_rg, b_rg, w_re, b_re, w_e1, w_e3,
              w_e2, final_g):
    v_first = None
    for l in range(DEPTH):
        h = _rmsnorm(x, norm1_g[l])
        proj = h @ w_in[l]
        u_rwkv, u_mamba, u_gate = jnp.split(proj, [RWKV_COLS, RWKV_COLS + MAMBA_COLS], axis=-1)
        v_res = None if l == 0 else (w_v1[l - 1], mu_v[l - 1], v0[l - 1], w_v2[l - 1])
        o_a, v_l = _rwkv7_branch(u_rwkv, h, v_first, v_res, mu_rwkv[l], w0[l], w_decay2[l], a0[l],
                                 w_iclr2[l], w_gate2[l], k_k[l], k_a[l], r_k[l], lnx_g[l],
                                 lnx_b[l], w_rwkv_o[l])
        if l == 0:
            v_first = v_l
        o_b = _mamba2_branch(u_mamba, conv_w[l], conv_b[l], dt_bias[l], a_log[l], d_skip[l],
                             mnorm_g[l], w_mamba_o[l])
        g_a, g_b = jnp.split(jax.nn.sigmoid(u_gate.astype(jnp.float32)), 2, axis=-1)
        merged = (g_a * o_a + g_b * o_b).astype(x.dtype)
        x = x + (merged @ w_out[l]).astype(x.dtype)
        h2 = _rmsnorm(x, norm2_g[l])
        x = x + _hier_moe(h2, w_rg[l], b_rg[l], w_re[l], b_re[l], w_e1[l], w_e3[l], w_e2[l])
    return _rmsnorm(x, final_g)


_drawn_inputs = setup_inputs


def setup_inputs(seed=0):
    import zlib

    import numpy as np

    out = dict(_drawn_inputs(seed))
    spreads = {}
    factors = {'w_decay2': 6.808,
     'a0': 2.849,
     'k_k': 16.133,
     'k_a': 4.333,
     'lnx_g': 5.669,
     'lnx_b': 21.503,
     'conv_b': 12.53,
     'd_skip': 28.475,
     'b_rg': 8.0,
     'b_re': 16.104,
     'final_g': 25.595,
     'dt_bias': 22.056,
     'mnorm_g': 5.466,
     'norm2_g': 3.299,
     'a_log': 8.0}
    for name, (base, spread) in spreads.items():
        noise = np.random.default_rng([zlib.crc32(name.encode()), seed]).standard_normal(out[name].shape)
        drawn = base * np.exp(spread * noise) if base else spread * noise
        out[name] = jnp.asarray(drawn.astype(out[name].dtype))
    for name, factor in factors.items():
        out[name] = (out[name] * factor).astype(out[name].dtype)
    return out
```

```python
import concourse.bass as bass
from concourse import mybir
from contextlib import ExitStack

F32 = mybir.dt.float32
I32 = mybir.dt.int32
ALU = mybir.AluOpType
ACT = mybir.ActivationFunctionType
AX = mybir.AxisListType

P = 128
D_MODEL = 1024
SEQ = 512
TILES = SEQ // P
KT = D_MODEL // P
RWKV_HEAD = 64
PAIRS = D_MODEL // P
DECAY_LORA = 64
RWKV_COLS = 3 * D_MODEL + 256
MAMBA_INNER = 2048
GROUPS = 4
HEADS_PER_GROUP = 8
MAMBA_HEADS = GROUPS * HEADS_PER_GROUP
XBC_TILES = (MAMBA_INNER + 2 * GROUPS * P) // P
TAPS = 4
Z_COL = RWKV_COLS
XS_COL = Z_COL + MAMBA_INNER
B_COL = XS_COL + MAMBA_INNER
C_COL = B_COL + GROUPS * P
DT_COL = C_COL + GROUPS * P
GATE_COL = DT_COL + MAMBA_HEADS
N_GROUPS = 4
N_EXPERTS = 32
EXPERT_FF = 512
FT = EXPERT_FF // P
BLOCK = 64
MAX_EXTRA = 2 * SEQ // BLOCK
MAX_BLOCKS = N_EXPERTS + MAX_EXTRA
XS_ROWS = (MAX_BLOCKS + 2) * BLOCK
KAPPA = 0.6065306597126334
BIG = 1.0e30
LEVELS = 6


def hybrid_block_kernel(nc, a, out):
    ctx = ExitStack()
    with ctx:
        def sem(name):
            return ctx.enter_context(nc.semaphore(name))

        def sb(name, cols):
            return ctx.enter_context(nc.sbuf_tensor(name, [P, cols], F32))

        hT_t = sb("hT", KT * SEQ)
        ygT_t = sb("ygT", PAIRS * SEQ)
        ymT_t = sb("ymT", 16 * SEQ)
        ring_t = sb("ring", 5 * KT * P)
        arena = sb("arena", 26240)
        const = sb("const", 3600)
        hT = hT_t[:, :].rearrange("p (k t) -> p k t", k=KT)
        ygT = ygT_t[:, :].rearrange("p (k t) -> p k t", k=PAIRS)
        ymT = ymT_t[:, :].rearrange("p (k t) -> p k t", k=16)
        ring = [ring_t[:, s * KT * P:(s + 1) * KT * P].rearrange("p (k m) -> p k m", k=KT) for s in range(5)]

        def taker(t):
            at = [0]

            def take(n):
                at[0] += n
                assert at[0] <= t[:, :].shape[1], (at[0], t[:, :].shape)
                return t[:, at[0] - n:at[0]]
            return take

        kc = taker(const)
        ident, head_ones, ones = kc(P), kc(P), kc(P)
        tri2 = kc(2 * P)
        neg_tri = kc(P)
        level_mask = [kc(P) for _ in range(LEVELS + 1)]
        not_start = kc(SEQ)
        pair_prm = kc(PAIRS * 14)
        norm1_c = kc(KT)
        lora_mu = kc(4)
        conv_prm = kc(GROUPS * 6 * 5)
        out_prm = kc(GROUPS * 8)
        prm = kc(14)
        cprm = kc(30)
        oprm = kc(8)
        dt_tok = kc(TILES * MAMBA_HEADS)
        acs_tok = kc(TILES * MAMBA_HEADS)
        s_small = kc(64)
        dtp = kc(4)
        pp3 = pair_prm.rearrange("p (c n) -> p c n", c=PAIRS)
        cp4 = conv_prm.rearrange("p (g s n) -> p g s n", g=GROUPS, s=6)
        op3 = out_prm.rearrange("p (g n) -> p g n", g=GROUPS)

        bank = [ctx.enter_context(nc.psum_tensor(f"bank{i}", [P, 512], F32)) for i in range(8)]
        bk = [b[:, :] for b in bank]

        acs_d = nc.dram_tensor("acs_d", [MAMBA_HEADS, SEQ], F32, kind="Internal").ap()
        xs_d = nc.dram_tensor("xs_d", [XS_ROWS, D_MODEL], F32, kind="Internal").ap()

        w_in = a["w_in"][0]

        def w_cols(mat, kt0, col):
            return mat[kt0 * P:(kt0 + KT) * P, bass.ds(col, P)].rearrange("(k p) m -> p k m", p=P)

        ks = taker(arena)
        ks(3 * D_MODEL + 2 * SEQ)
        x_tok = ks(TILES * D_MODEL).rearrange("p (t d) -> p t d", t=TILES)
        xn_tok = ks(TILES * D_MODEL).rearrange("p (t d) -> p t d", t=TILES)
        rows = [ks(P), ks(P), ks(P), ks(P)]
        dskip_in = ks(2)
        row_f, row_sh, eq_tmp = ks(P), ks(P), ks(P)
        col_f, col_sh = ks(1), ks(1)
        eq_blocks = [ks(P) for _ in range(LEVELS + 2)]
        idx_i = ctx.enter_context(nc.sbuf_tensor("idx_i", [P, 2 * (P + 1)], I32))
        sq_scr = ks(D_MODEL)
        dtw = [ks(SEQ)[0:MAMBA_HEADS] for _ in range(8)]
        dt_w = ks(KT * MAMBA_HEADS).rearrange("p (k m) -> p k m", k=KT)

        kr = taker(arena)
        lw_w = kr(D_MODEL)
        lw_a = kr(D_MODEL)
        lw_g = kr(D_MODEL)
        lo_wa, lo_g = kr(SEQ), kr(SEQ)
        rkv = [kr(SEQ) for _ in range(3)]
        sigw, iclr, gate = kr(SEQ), kr(SEQ), kr(SEQ)
        ccum, cc, cp = kr(SEQ), kr(SEQ), kr(SEQ)
        e_a, e_r, e_b = kr(SEQ), kr(SEQ), kr(SEQ)
        kkr, ksq, rnorm, kscale, k2, rk = kr(SEQ), kr(SEQ), kr(SEQ), kr(SEQ), kr(SEQ), kr(SEQ)
        kb, bonus = kr(SEQ), kr(SEQ)
        a_t, r_t, b_t, k_t = kr(SEQ), kr(SEQ), kr(SEQ), kr(SEQ)
        ar = kr(TILES * 4 * P).rearrange("p (j f t) -> p j f t", j=TILES, f=4)
        v_tok, b_tok, k_tok = kr(SEQ), kr(SEQ), kr(SEQ)
        x1, u_sb, fs = kr(P), kr(P), kr(P)
        st = [kr(P), kr(P)]
        r_ones = kr(P)
        lora_c = [kr(P) for _ in range(3)]
        y_c, y_sq, y_3 = kr(SEQ), kr(SEQ), kr(SEQ)
        km = taker(ymT_t)
        gb = km(TILES * 512).rearrange("p (j f t) -> p j f t", j=TILES, f=4)
        gk = km(TILES * 512).rearrange("p (j f t) -> p j f t", j=TILES, f=4)
        bm = [km(8 * P).rearrange("p (j f t) -> p j f t", j=TILES, f=2) for _ in range(2)]
        xt, gi, hi = km(8 * P), km(8 * P), kr(8 * P)
        lev8 = [m.unsqueeze(1).unsqueeze(1).broadcast_to([P, TILES, 2, P]) for m in level_mask]
        ident8 = ident.unsqueeze(1).unsqueeze(1).broadcast_to([P, TILES, 2, P])
        gi4 = gi.rearrange("p (j f t) -> p j f t", j=TILES, f=2)
        zero_tile = ygT_t[:, 6 * SEQ:8 * SEQ]

        kb2 = taker(arena)
        zs = kb2(4 * SEQ).rearrange("p (m t) -> p m t", m=4)
        xbcT = kb2(6 * SEQ).rearrange("p (m t) -> p m t", m=6)
        b_tk = kb2(SEQ)
        xdt = kb2(TILES * 512).rearrange("p (j n) -> p j n", j=TILES)
        xe = [kb2(512) for _ in range(2)]
        m_sb = [kb2(1024).rearrange("p (h t) -> p h t", h=8) for _ in range(2)]
        c_sb = [kb2(1024).rearrange("p (h t) -> p h t", h=8) for _ in range(2)]
        acs_bc = kb2(8 * SEQ).rearrange("p (h t) -> p h t", h=8)
        e_bc = kb2(8 * SEQ).rearrange("p (h t) -> p h t", h=8)
        state = [kb2(512) for _ in range(2)]
        s_dec = kb2(512)
        y_m, y_m_b = kb2(512), kb2(512)
        y_g = kb2(4 * SEQ).rearrange("p (m t) -> p m t", m=4)
        ysq2 = e_bc.rearrange("p h t -> p (h t)")[:, 0:4 * SEQ]
        rstd2 = kb2(SEQ)
        te = [kb2(8) for _ in range(2)]


        SLOT = 12288
        w1_sb = [arena[:, s_ * SLOT:s_ * SLOT + 4096].rearrange("p (k n) -> p k n", k=KT) for s_ in range(2)]
        w3_sb = [arena[:, s_ * SLOT + 4096:s_ * SLOT + 8192].rearrange("p (k n) -> p k n", k=KT) for s_ in range(2)]
        w2_sb = [arena[:, s_ * SLOT + 8192:s_ * SLOT + 12288].rearrange("p (k n) -> p k n", k=FT) for s_ in range(2)]
        merged = arena[:, SLOT + 8192:SLOT + 12288].rearrange("p (k t) -> p k t", k=KT)
        w_out_sb = arena[:, SLOT:SLOT + 8192].rearrange("p (k n) -> p k n", k=KT)
        mg = taker(arena)
        mg(8192)
        sg_a = [mg(SEQ), mg(SEQ)]
        sg_b = [mg(SEQ), mg(SEQ)]
        t_a = [mg(SEQ), mg(SEQ)]
        t_b = [mg(SEQ), mg(SEQ)]
        x1_tok = ygT_t[:, :].rearrange("p (t d) -> p t d", t=TILES)
        k5 = taker(ymT_t)
        h2T = k5(KT * SEQ).rearrange("p (k t) -> p k t", k=KT)
        h2_tok = k5(TILES * D_MODEL).rearrange("p (t d) -> p t d", t=TILES)
        k6 = taker(hT_t)
        g2_bc, gf_bc = k6(D_MODEL), k6(D_MODEL)
        wr_sb = k6(KT * 36).rearrange("p (k n) -> p k n", k=KT)
        br_bc = k6(36)
        sq_row = k6(D_MODEL)
        k8 = taker(ring_t)
        lg = k8(TILES * 36).rearrange("p (t n) -> p t n", t=TILES)
        g_l = lg[:, :, 0:4]
        e_l = lg[:, :, 4:36]
        rt = [k8(TILES * 32).rearrange("p (t n) -> p t n", t=TILES) for _ in range(7)]
        gs = [k8(TILES * 4).rearrange("p (t n) -> p t n", t=TILES) for _ in range(3)]
        sm = [k8(TILES) for _ in range(12)]
        thr = k8(32 * 8).rearrange("p (n b) -> p n b", n=32)
        over = k8(32 * 8).rearrange("p (n b) -> p n b", n=32)
        pri = k8(32)
        extra, incl, away, home = k8(32), k8(32), k8(32), k8(32)
        ones32 = k8(32)
        r_f = [k8(TILES), k8(TILES)]
        item_w = k8(MAX_EXTRA)
        item_f = k8(MAX_BLOCKS + 2)
        item_c = k8(MAX_EXTRA * 32).rearrange("p (w n) -> p w n", w=MAX_EXTRA)
        r_i = ctx.enter_context(nc.sbuf_tensor("r_i", [P, 2 * TILES], I32))
        item_i = ctx.enter_context(nc.sbuf_tensor("item_i", [P, MAX_BLOCKS + 2], I32))
        k7 = taker(ymT_t)
        xs_sb = [k7(D_MODEL)[0:BLOCK] for _ in range(2)]
        xgT = k7(KT * BLOCK).rearrange("p (k s) -> p k s", k=KT)
        silu_hi = k7(EXPERT_FF)[BLOCK:2 * BLOCK]
        hid = k7(EXPERT_FF)[0:BLOCK]
        hidT = k7(FT * BLOCK).rearrange("p (k s) -> p k s", k=FT)
        y_out = [k7(D_MODEL)[0:BLOCK] for _ in range(2)]
        y_rows = [k7(D_MODEL) for _ in range(2)]

        (head_norm, head_act, terms, kb_rk, lorac_ready, dve_done_e, ginit_ready, x_in) = (
            sem(n) for n in "head_norm head_act terms kb_rk lorac_ready dve_done_e ginit_ready x_in".split())
        (rows_in, dtw_in, zeros_ready, xs_zeroed, idx_ready, masks_ready, sumsq_ready, ms_ready) = (
            sem(n) for n in "rows_in dtw_in zeros_ready xs_zeroed idx_ready masks_ready sumsq_ready ms_ready".split())
        (rms_ready, rstd_ready, xn_ready, norm_tr, hT_ready, rows_tr, prm_ready, lora_in) = (
            sem(n) for n in "rms_ready rstd_ready xn_ready norm_tr hT_ready rows_tr prm_ready lora_in".split())
        (lo_scaled, lo_shifted, lo_ready, dt_proj, dt_act, dt_dve, dt_tr, dt_tok_ready) = (
            sem(n) for n in "lo_scaled lo_shifted lo_ready dt_proj dt_act dt_dve dt_tr dt_tok_ready".split())
        (acs_stored, rkv_scaled, shifted, pair_prm_ready, lora_mm, lora_read, ksq_ready, norm_mm) = (
            sem(n) for n in "acs_stored rkv_scaled shifted pair_prm_ready lora_mm lora_read ksq_ready norm_mm".split())
        (nrm_ready, kscale_ready, centered, exps_ready, ar_ready, bonus_mm, bonus_ready, tok_tr) = (
            sem(n) for n in "nrm_ready kscale_ready centered exps_ready ar_ready bonus_mm bonus_ready tok_tr".split())
        (tok_ready, gram_mm, gram_ready, bm_ready, g_ready, h_ready, h_tr, xt_mm) = (
            sem(n) for n in "tok_ready gram_mm gram_ready bm_ready g_ready h_ready h_tr xt_mm".split())
        (xt_ready, g_mm, x1_mm, x1_ready, u_mm, u_ready, d_mm, s_ready) = (
            sem(n) for n in "xt_ready g_mm x1_mm x1_ready u_mm u_ready d_mm s_ready".split())
        (fs_ready, f_ready, s_zero, y_mm, pe_pair, act_pair, dve_pair, dve_step) = (
            sem(n) for n in "fs_ready f_ready s_zero y_mm pe_pair act_pair dve_pair dve_step".split())
        (pool_step, z_ready, taps_act, taps_done, xbc_ready, acs_bc_in, e_bc_ready, bt_tr) = (
            sem(n) for n in "pool_step z_ready taps_act taps_done xbc_ready acs_bc_in e_bc_ready bt_tr".split())
        (bt_tok_ready, xt_tr, xdt_ready, cprm_ready, d_ready, m_exp, m_ready, cb_mm) = (
            sem(n) for n in "bt_tok_ready xt_tr xdt_ready cprm_ready d_ready m_exp m_ready cb_mm".split())
        (c_ready, ym_mm, st_mm, te_in, te_ready, xe_ready, st_ready, yskip_ready) = (
            sem(n) for n in "c_ready ym_mm st_mm te_in te_ready xe_ready st_ready yskip_ready".split())
        (yg_ready, ysq_ready, gn_mm, gn_ready, act_group, dve_group, sig_ready, merged_ready) = (
            sem(n) for n in "yg_ready ysq_ready gn_mm gn_ready act_group dve_group sig_ready merged_ready".split())
        (w_out_in, router_in, out_mm, x1_done, h2_ready, h2T_ready, logit_mm, r_exp_in) = (
            sem(n) for n in "w_out_in router_in out_mm x1_done h2_ready h2T_ready logit_mm r_exp_in".split())
        (r_exp, sel_ready, pos_mm, scattered, rows_out, items_out, w1_in0, w1_in1, w3_in0) = (
            sem(n) for n in "r_exp sel_ready pos_mm scattered rows_out items_out w1_in0 w1_in1 w3_in0".split())
        (w3_in1, w2_in0, w2_in1, xb_in0, xb_in1, xg_tr, xg_ready, h13_mm) = (
            sem(n) for n in "w3_in1 w2_in0 w2_in1 xb_in0 xb_in1 xg_tr xg_ready h13_mm".split())
        (silu_ready, hid_ready, hid_tr, hidT_ready, y2_mm, ycopy_a, ycopy_b, yst0) = (
            sem(n) for n in "silu_ready hid_ready hid_tr hidT_ready y2_mm ycopy_a ycopy_b yst0".split())
        (yst1, yg_in0, yg_in1, experts_done, ysum, final_ready, out_stored) = (
            sem(n) for n in "yst1 yg_in0 yg_in1 experts_done ysum final_ready out_stored".split())
        w_loaded = [sem(f"w_loaded{i}") for i in range(5)]
        slot_done = [sem(f"slot_done{i}") for i in range(5)]

        def chain(eng, step, base):
            count = [0]

            def link(ins):
                ins.then_inc(step, 1)
                count[0] += 1
                eng.wait_ge(step, base + count[0])
            link.count = count
            return link

        def done(eng, ins, what, value):
            ins.then_inc(what, 1)
            eng.wait_ge(what, value)

        BASE_PAIR = [1, 1, 0, 0, 0]
        BASE_GROUP = [BASE_PAIR[i] + (PAIRS if i < 3 else 0) for i in range(5)]
        BASE_MERGE = [BASE_GROUP[i] + 2 * GROUPS for i in range(5)]
        MERGE_MATS = [("w_rwkv_o", 0, 0), ("w_in", 0, GATE_COL), ("w_in", 0, GATE_COL + D_MODEL),
                      ("w_mamba_o", 0, 0), ("w_mamba_o", KT, 0)]
        GROUP_COLS = [(XS_COL + m * P, 4 * P) for m in range(4)] + [(B_COL, P), (C_COL, P)] \
            + [(Z_COL + m * P, 4 * P) for m in range(4)]

        def wait_pair(eng, i, c):
            eng.wait_ge(slot_done[i], c + BASE_PAIR[i] + 1)

        def wait_group(eng, t, g):
            eng.wait_ge(slot_done[t % 5], g * 2 + BASE_GROUP[t % 5] + t // 5 + 1)

        def wait_merge(eng, s, j):
            eng.wait_ge(slot_done[s], j + BASE_MERGE[s] + 1)

        GRAM_BANKS = [7, 4, 5, 3]
        E_W1, E_W3, E_W2 = a["w_e1"][0], a["w_e3"][0], a["w_e2"][0]

        block = ctx.enter_context(nc.Block())

        @block.sync
        def _(sp):
            for t in range(TILES):
                sp.dma_start(x_tok[:, t, :], a["x"][0, t * P:(t + 1) * P, :]).then_inc(x_in, 16)

            def row(dst, src, n):
                sp.dma_start(dst[0:n, :], src.rearrange("(n m) -> n m", m=P)).then_inc(rows_in, 16)

            row(rows[0][0:24], a["mu_rwkv"][0, 0:3 * D_MODEL], 24)
            for i, name in enumerate(["w0", "a0", "k_k", "k_a"]):
                row(rows[0][24 + 8 * i:32 + 8 * i], a[name][0], 8)
            row(rows[0][56:64], a["r_k"][0].rearrange("h n -> (h n)"), 8)
            row(rows[0][64:72], a["lnx_g"][0], 8)
            row(rows[0][72:80], a["lnx_b"][0], 8)
            row(rows[0][80:88], a["norm1_g"][0], 8)
            row(rows[0][88:90], a["mu_rwkv"][0, 3 * D_MODEL:RWKV_COLS], 2)
            row(rows[1][0:96], a["conv_w"][0].rearrange("a b -> (a b)"), 96)
            row(rows[1][96:120], a["conv_b"][0], 24)
            row(rows[2][0:16], a["mnorm_g"][0], 16)
            sp.dma_start(dskip_in[0:16], a["d_skip"][0].rearrange("(a b) -> a b", b=2)).then_inc(rows_in, 16)
            sp.dma_start(dtp[0:MAMBA_HEADS, 0:1], a["dt_bias"].rearrange("a b -> b a")).then_inc(rows_in, 16)
            sp.dma_start(dtp[0:MAMBA_HEADS, 1:2], a["a_log"].rearrange("a b -> b a")).then_inc(rows_in, 16)
            sp.dma_start(ring[0], w_cols(w_in, 0, 3 * D_MODEL)).then_inc(w_loaded[0], 16)
            sp.dma_start(ring[1], w_cols(w_in, 0, 3 * D_MODEL + P)).then_inc(w_loaded[1], 16)
            sp.dma_start(dt_w, w_in[:, DT_COL:DT_COL + MAMBA_HEADS].rearrange("(k p) m -> p k m", p=P)
                         ).then_inc(dtw_in, 16)
            sp.dma_start(lw_g, a["w_gate2"][0]).then_inc(lora_in, 16)
            sp.dma_start(lw_w[0:DECAY_LORA], a["w_decay2"][0]).then_inc(lora_in, 16)
            sp.dma_start(lw_a[DECAY_LORA:P], a["w_iclr2"][0]).then_inc(lora_in, 16)
            for s in range(3):
                if s < 2:
                    sp.wait_ge(slot_done[s], BASE_PAIR[s])
                sp.dma_start(ring[s], w_cols(w_in, 0, s * D_MODEL)).then_inc(w_loaded[s], 16)
            with sp.Fori(1, PAIRS) as c:
                for s in range(3):
                    sp.wait_ge(slot_done[s], c + BASE_PAIR[s])
                    sp.dma_start(ring[s], w_cols(w_in, 0, c * P + s * D_MODEL)).then_inc(w_loaded[s], 16)
            sp.wait_ge(dve_pair, PAIRS)
            sp.wait_ge(act_pair, PAIRS)
            sp.wait_ge(pe_pair, PAIRS)
            sp.wait_ge(bm_ready, PAIRS * 7)
            sp.wait_ge(acs_stored, 16)
            def load_group(g, first):
                for t in range(10):
                    s = t % 5
                    if not first or t >= 5 or s < 3:
                        sp.wait_ge(slot_done[s], g * 2 + BASE_GROUP[s] + t // 5)
                    col, step = GROUP_COLS[t]
                    sp.dma_start(ring[s], w_cols(w_in, 0, g * step + col)).then_inc(w_loaded[s], 16)
                    if t == 3:
                        if not first:
                            sp.wait_ge(m_exp, g * TILES)
                        sp.dma_start(acs_bc, acs_d[bass.ds(g * HEADS_PER_GROUP, HEADS_PER_GROUP), :].unsqueeze(0)
                                     .broadcast_to([P, HEADS_PER_GROUP, SEQ])).then_inc(acs_bc_in, 16)

            load_group(0, True)
            with sp.Fori(1, GROUPS) as g:
                load_group(g, False)
            def load_merge(j):
                for s, (name, kt0, col) in enumerate(MERGE_MATS):
                    sp.wait_ge(slot_done[s], j + BASE_MERGE[s])
                    sp.dma_start(ring[s], w_cols(a[name][0], kt0, j * P + col)).then_inc(w_loaded[s], 16)

            load_merge(0)
            sp.wait_ge(dve_group, GROUPS)
            sp.wait_ge(act_group, GROUPS)
            sp.wait_ge(yg_ready, GROUPS * TILES)
            sp.wait_ge(gn_mm, GROUPS)
            with sp.Fori(1, KT) as j:
                load_merge(j)
            for h in range(2):
                sp.dma_start(w_out_sb[:, :, h * 512:(h + 1) * 512],
                             a["w_out"][0][:, h * 512:(h + 1) * 512].rearrange("(k p) m -> p k m", p=P)
                             ).then_inc(w_out_in, 16)
            W1_IN, W3_IN, W2_IN = [w1_in0, w1_in1], [w3_in0, w3_in1], [w2_in0, w2_in1]

            def load_w13(e, u):
                sp.dma_start(w1_sb[u], E_W1[bass.ds(e, 1)].rearrange("o (p k) n -> p (o k) n", k=KT)).then_inc(W1_IN[u], 16)
                sp.dma_start(w3_sb[u], E_W3[bass.ds(e, 1)].rearrange("o (p k) n -> p (o k) n", k=KT)).then_inc(W3_IN[u], 16)

            def load_w2(e, u):
                sp.dma_start(w2_sb[u], E_W2[bass.ds(e, 1)].rearrange("o (p k) n -> p (o k) n", k=FT)).then_inc(W2_IN[u], 16)

            load_w13(0, 0)
            for s in range(5):
                wait_merge(sp, s, KT - 1)
            for t in range(TILES):
                sp.dma_start(x1_tok[:, t, :], a["x"][0, t * P:(t + 1) * P, :]).then_inc(x_in, 16)
            sp.dma_start(g2_bc, a["norm2_g"].broadcast_to([P, D_MODEL])).then_inc(router_in, 16)
            sp.dma_start(gf_bc, a["final_g"].unsqueeze(0).broadcast_to([P, D_MODEL])).then_inc(router_in, 16)
            sp.dma_start(wr_sb[:, :, 0:4], a["w_rg"][0].rearrange("(k p) m -> p k m", p=P)).then_inc(router_in, 16)
            sp.dma_start(wr_sb[:, :, 4:36], a["w_re"][0].rearrange("(k p) m -> p k m", p=P)).then_inc(router_in, 16)
            sp.dma_start(br_bc[:, 0:4], a["b_rg"].broadcast_to([P, 4])).then_inc(router_in, 16)
            sp.dma_start(br_bc[:, 4:36], a["b_re"].broadcast_to([P, 32])).then_inc(router_in, 16)

            sp.wait_ge(merged_ready, KT)
            load_w2(0, 0)
            sp.wait_ge(out_mm, 8)
            load_w13(1, 1)
            load_w2(1, 1)
            sp.wait_ge(items_out, 1)
            last_pair = sp.value_load(item_i[0:1, MAX_BLOCKS:MAX_BLOCKS + 1], min_val=N_EXPERTS // 2 - 1, max_val=MAX_BLOCKS // 2 - 1)
            with sp.Fori(1, last_pair + 1) as i:
                for u in range(2):
                    w = i * 2 + u
                    e = sp.value_load(item_i[0:1, bass.ds(w, 1)], min_val=0, max_val=N_EXPERTS - 1)
                    sp.wait_ge(h13_mm, w - 1)
                    load_w13(e, u)
                    sp.wait_ge(y2_mm, w - 1)
                    load_w2(e, u)
            for t in range(TILES):
                sp.wait_ge(final_ready, t + 1)
                sp.dma_start(out[0, t * P:(t + 1) * P, :], x1_tok[:, t, :]).then_inc(out_stored, 16)
            sp.wait_ge(out_stored, 16 * TILES)

        @block.gpsimd
        def _(pool):
            link = chain(pool, pool_step, 0)
            nc.gpsimd.memset(zero_tile, 0.0).then_inc(zeros_ready, 1)
            nc.gpsimd.iota(idx_i[:, 0:P], pattern=[[1, P]], base=0, channel_multiplier=0).then_inc(idx_ready, 1)
            nc.gpsimd.iota(idx_i[:, P:P + 1], pattern=[[0, 1]], base=0, channel_multiplier=1).then_inc(idx_ready, 1)
            pool.wait_ge(idx_ready, 2)
            nc.gpsimd.memset(st[0], 0.0).then_inc(s_zero, 1)
            nc.gpsimd.memset(st[1], 0.0).then_inc(s_zero, 1)
            pool.wait_ge(s_zero, 2)
            link(nc.gpsimd.memset(lw_w[DECAY_LORA:P], 0.0))
            link(nc.gpsimd.memset(lw_a[0:DECAY_LORA], 0.0))

            def pair(c):
                pool.wait_ge(xs_zeroed, 16 * (XS_ROWS // P))
                pool.wait_ge(dt_tok_ready, 1)
                pool.wait_ge(acs_stored, 16)
                pool.wait_ge(lora_in, 48)
                pool.wait_ge(pool_step, 2)
                for i, lw in enumerate([lw_w, lw_a, lw_g]):
                    nc.gpsimd.tensor_copy(lora_c[i], lw[:, bass.ds(c * P, P)]).then_inc(lorac_ready, 1)
                pool.wait_ge(lora_read, c * 3 + 2)
                pool.wait_ge(terms, c * 6 + 2)
                nc.gpsimd.tensor_tensor(kb, kkr, iclr, ALU.mult).then_inc(kb_rk, 1)
                pool.wait_ge(terms, c * 6 + 1)
                nc.gpsimd.tensor_tensor(rk, rkv[0], k2, ALU.mult).then_inc(kb_rk, 1)
                pool.wait_ge(terms, c * 6 + 4)
                for f, src in enumerate([a_t, r_t]):
                    for h in range(2):
                        own = head_ones[:, h * RWKV_HEAD:h * RWKV_HEAD + 1]
                        nc.gpsimd.tensor_tensor(ar[:, :, 2 * f + h, :], src.rearrange("p (j t) -> p j t", j=TILES),
                                                own.unsqueeze(2).broadcast_to([P, TILES, P]), ALU.mult).then_inc(ar_ready, 1)
                pool.wait_ge(gram_ready, c * 8 + 8)
                m4 = gb[:, :, 0:2, :]
                done(pool, nc.gpsimd.tensor_tensor(bm[0], m4, lev8[0], ALU.mult), bm_ready, c * 7 + 1)
                done(pool, nc.gpsimd.tensor_tensor(gi4, bm[0], ident8, ALU.add), ginit_ready, c + 1)
                for lv in range(1, LEVELS + 1):
                    if lv >= 3:
                        pool.wait_ge(xt_mm, c * 12 + 2 * (lv - 2))
                    nc.gpsimd.tensor_tensor(bm[lv % 2], m4, lev8[lv], ALU.mult).then_inc(bm_ready, 1)

            with pool.Fori(0, PAIRS) as c:
                pair(c)
                pool.wait_ge(dve_pair, c + 1)
                pool.wait_ge(act_pair, c + 1)
                pool.wait_ge(pe_pair, c + 1)

            def group(g):
                for j in range(TILES):
                    if j > 0:
                        if j == 1:
                            pool.wait_ge(e_bc_ready, g + 1)
                            pool.wait_ge(xbc_ready, g * 6 + 6)
                        if j == 3:
                            pool.wait_ge(ym_mm, g * 4 + 2)
                        nc.gpsimd.tensor_tensor(
                            c_sb[j % 2], e_bc[:, :, j * P:(j + 1) * P],
                            xbcT[:, 5, j * P:(j + 1) * P].unsqueeze(1).broadcast_to([P, 8, P]), ALU.mult
                        ).then_inc(c_ready, 1)
                for j in range(TILES):
                    if j == 0:
                        pool.wait_ge(z_ready, g * 4 + 4)
                    pool.wait_ge(yskip_ready, g * 4 + j + 1)
                    nc.gpsimd.tensor_tensor(y_g[:, :, j * P:(j + 1) * P],
                                            y_m4[j % 2], zs[:, :, j * P:(j + 1) * P], ALU.mult
                                            ).then_inc(yg_ready, 1)

            y_m4 = [y_m.rearrange("p (m t) -> p m t", m=4), y_m_b.rearrange("p (m t) -> p m t", m=4)]
            with pool.Fori(0, GROUPS) as g:
                group(g)

            pool.wait_ge(xs_zeroed, 16 * (XS_ROWS // P))
            pool.wait_ge(rows_out, 2)
            pool.wait_ge(h2_ready, TILES)
            for k in range(2):
                for t in range(TILES):
                    nc.gpsimd.indirect_dma_start(
                        out=xs_d, out_offset=bass.IndirectOffsetOnAxis(ap=r_i[:, k * TILES + t:k * TILES + t + 1], axis=0),
                        in_=h2_tok[:, t, :], in_offset=None).then_inc(scattered, 16)
            pool.wait_ge(scattered, 16 * 2 * TILES)
            pool.wait_ge(items_out, 1)
            pool.wait_ge(h2T_ready, 2 * TILES)
            pool.wait_ge(logit_mm, TILES)
            last_pair = pool.value_load(item_i[0:1, MAX_BLOCKS:MAX_BLOCKS + 1], min_val=N_EXPERTS // 2 - 1, max_val=MAX_BLOCKS // 2 - 1)
            XB_IN, YST = [xb_in0, xb_in1], [yst0, yst1]
            pool.dma_start(xs_sb[0], xs_d[0:BLOCK, :]).then_inc(XB_IN[0], 16)
            pool.dma_start(xs_sb[1], xs_d[BLOCK:2 * BLOCK, :]).then_inc(XB_IN[1], 16)
            pool.wait_ge(xg_tr, 1)
            pool.dma_start(xs_sb[0], xs_d[2 * BLOCK:3 * BLOCK, :]).then_inc(XB_IN[0], 16)

            def expert_pair(i, final):
                for u in range(2):
                    w = i * 2 + u
                    if not (final and u == 1):
                        pool.wait_ge(xg_tr, w + 2)
                        pool.dma_start(xs_sb[1 - u], xs_d[bass.ds((w + 3) * BLOCK, BLOCK), :]).then_inc(XB_IN[1 - u], 16)
                    pool.wait_ge(ycopy_a, w + 1)
                    pool.wait_ge(ycopy_b, w + 1)
                    pool.dma_start(xs_d[bass.ds(w * BLOCK, BLOCK), :], y_out[u]).then_inc(YST[u], 16)

            with pool.Fori(0, last_pair) as i:
                expert_pair(i, False)
            expert_pair(last_pair, True)
            pool.wait_ge(experts_done, 1)
            YG = [yg_in0, yg_in1]
            for t in range(TILES):
                for k in range(2):
                    if t > 0:
                        pool.wait_ge(ysum, 2 * (t - 1) + k + 1)
                    nc.gpsimd.indirect_dma_start(
                        out=y_rows[k], out_offset=None, in_=xs_d,
                        in_offset=bass.IndirectOffsetOnAxis(ap=r_i[:, k * TILES + t:k * TILES + t + 1], axis=0)
                    ).then_inc(YG[k], 16)
            for k in range(2):
                pool.wait_ge(YG[k], 16 * TILES)

        @block.scalar
        def _(act):
            for t in range(TILES):
                act.wait_ge(x_in, 16 * TILES)
                if t > 0:
                    act.wait_ge(sumsq_ready, t)
                nc.scalar.activation(sq_scr, x_tok[:, t, :], ACT.Square, accum_out=s_small[:, t:t + 1]).then_inc(sumsq_ready, 1)
            act.wait_ge(ms_ready, 1)
            nc.scalar.activation(s_small[:, 4:8], s_small[:, 4:8], ACT.Sqrt).then_inc(rms_ready, 1)
            act.wait_ge(rstd_ready, 1)
            for t in range(TILES):
                nc.scalar.activation(xn_tok[:, t, :], x_tok[:, t, :], ACT.Copy, scale=s_small[:, 8 + t:9 + t]).then_inc(xn_ready, 1)

            act.wait_ge(zeros_ready, 1)
            for n in range(XS_ROWS // P):
                act.dma_start(xs_d[n * P:(n + 1) * P, :], zero_tile).then_inc(xs_zeroed, 16)

            act.wait_ge(prm_ready, 1)
            for i, dst in enumerate([lo_wa, lo_g]):
                act.wait_ge(slot_done[i], 1)
                nc.scalar.activation(dst, bk[i], ACT.Copy, scale=lora_mu[:, 2 + i:3 + i]).then_inc(lo_scaled, 1)
            act.wait_ge(lo_shifted, 1)
            nc.scalar.activation(lo_wa[0:DECAY_LORA], lo_wa[0:DECAY_LORA], ACT.Tanh).then_inc(lo_ready, 1)
            act.wait_ge(lo_shifted, 2)
            nc.scalar.activation(lo_g, lo_g, ACT.Sigmoid).then_inc(lo_ready, 1)

            act.wait_ge(dt_dve, 1)
            done(act, nc.scalar.activation(dtw[1], dtw[0], ACT.Abs), dt_act, 1)
            done(act, nc.scalar.activation(dtw[2], dtw[1], ACT.Exp, scale=-1.0), dt_act, 2)
            act.wait_ge(rows_in, 16 * 16)
            nc.scalar.activation(dtp[0:MAMBA_HEADS, 2:3], dtp[0:MAMBA_HEADS, 1:2], ACT.Exp).then_inc(dt_act, 1)
            act.wait_ge(dt_dve, 2)
            nc.scalar.activation(dtw[4], dtw[3], ACT.Ln).then_inc(dt_act, 1)

            act.wait_ge(dt_dve, 3)
            act.dma_start(acs_d, dtw[1]).then_inc(acs_stored, 16)

            def pair(c):
                act.wait_ge(pair_prm_ready, c * 2 + 1)
                act.wait_ge(lo_ready, 2)
                act.wait_ge(dt_tok_ready, 1)
                act.wait_ge(acs_stored, 16)
                for i in range(3):
                    wait_pair(act, i, c)
                    nc.scalar.activation(rkv[i], bk[i], ACT.Copy, scale=prm[:, 10 + i:11 + i]).then_inc(rkv_scaled, 1)
                for i, (dst, func, col) in enumerate([(sigw, ACT.Sigmoid, 3), (iclr, ACT.Sigmoid, 4), (gate, ACT.Copy, None)]):
                    act.wait_ge(lora_mm, c * 3 + i + 1)
                    bias = prm[:, col:col + 1] if col else 0.0
                    nc.scalar.activation(dst, bk[3 + i], func, bias=bias).then_inc(lora_read, 1)
                act.wait_ge(shifted, c * 3 + 2)
                nc.scalar.activation(ksq, rkv[1], ACT.Square, scale=prm[:, 5:6]).then_inc(ksq_ready, 1)
                nc.scalar.activation(kkr, rkv[1], ACT.Copy, scale=prm[:, 5:6]).then_inc(ksq_ready, 1)
                act.wait_ge(lora_read, c * 3 + 2)
                nc.scalar.activation(kscale, iclr, ACT.Identity, scale=prm[:, 6:7], bias=prm[:, 13:14]).then_inc(kscale_ready, 1)
                act.wait_ge(norm_mm, c + 1)
                nc.scalar.activation(rnorm, bk[3], ACT.Sqrt).then_inc(nrm_ready, 1)
                act.wait_ge(centered, c + 1)
                nc.scalar.activation(e_a, cp, ACT.Exp, scale=-KAPPA).then_inc(exps_ready, 1)
                nc.scalar.activation(e_b, cc, ACT.Exp, scale=KAPPA).then_inc(exps_ready, 1)
                nc.scalar.activation(e_r, cc, ACT.Exp, scale=-KAPPA).then_inc(exps_ready, 1)
                nc.scalar.activation(s_small[:, 16:20], ccum[:, RWKV_HEAD - 1::P], ACT.Exp, scale=-KAPPA).then_inc(exps_ready, 1)
                for i, (dst, b) in enumerate([(v_tok, 4), (b_tok, 5), (k_tok, 3)]):
                    act.wait_ge(tok_tr, c * 3 + i + 1)
                    nc.scalar.activation(dst, bk[b], ACT.Copy).then_inc(tok_ready, 1)
                for q in range(2):
                    act.wait_ge(h_tr, c * 12 + q + 1)
                    nc.scalar.activation(hi[:, q * 512:(q + 1) * 512], bk[3 + q], ACT.Copy).then_inc(h_ready, 1)
                for lv in range(1, LEVELS + 1):
                    for q in range(2):
                        act.wait_ge(xt_mm, c * 12 + 2 * (lv - 1) + q + 1)
                        nc.scalar.activation(xt[:, q * 512:(q + 1) * 512], bk[3 + q], ACT.Copy).then_inc(xt_ready, 1)
                    if lv < LEVELS:
                        for q in range(2):
                            act.wait_ge(h_tr, c * 12 + 2 * lv + q + 1)
                            nc.scalar.activation(hi[:, q * 512:(q + 1) * 512], bk[3 + q], ACT.Copy).then_inc(h_ready, 1)
                act.wait_ge(f_ready, c + 1)
                for j in range(1, TILES - 1):
                    act.wait_ge(s_ready, c * 6 + 2 * j)
                    nc.scalar.activation(fs, st[j % 2], ACT.Copy, scale=s_small[:, 20 + j:21 + j]).then_inc(fs_ready, 1)
                act.wait_ge(head_norm, c * 3 + 1)
                nc.scalar.activation(y_sq, y_c, ACT.Square).then_inc(head_act, 1)
                act.wait_ge(head_norm, c * 3 + 2)
                nc.scalar.activation(s_small[:, 40:48], s_small[:, 40:48], ACT.Sqrt).then_inc(head_act, 1)
                act.wait_ge(pe_pair, c + 1)
                nc.scalar.activation(y_3, bk[7], ACT.Identity, scale=prm[:, 8:9], bias=prm[:, 9:10]).then_inc(act_pair, 1)

            with act.Fori(0, PAIRS) as c:
                pair(c)
                act.wait_ge(dve_pair, c + 1)
                act.wait_ge(bm_ready, c * 7 + 7)
                act.wait_ge(pe_pair, c + 1)

            def group(g):
                act.wait_ge(cprm_ready, g + 1)
                for t in range(6):
                    wait_group(act, t, g)
                    nc.scalar.activation(xbcT[:, t, :], bk[t % 4], ACT.Identity, scale=cprm[:, 5 * t + 3:5 * t + 4],
                                         bias=cprm[:, 5 * t + 4:5 * t + 5]).then_inc(taps_act, 1)
                    if t > 0:
                        act.wait_ge(taps_done, g * 6 + t)
                        nc.scalar.activation(xbcT[:, t - 1, :], xbcT[:, t - 1, :], ACT.Silu).then_inc(xbc_ready, 1)
                act.wait_ge(taps_done, g * 6 + 6)
                nc.scalar.activation(xbcT[:, 5, :], xbcT[:, 5, :], ACT.Silu).then_inc(xbc_ready, 1)
                act.wait_ge(acs_bc_in, g * 16 + 16)
                nc.scalar.activation(e_bc, acs_bc, ACT.Exp).then_inc(e_bc_ready, 1)
                for m in range(4):
                    if m == 2:
                        act.wait_ge(bt_tr, g + 1)
                        nc.scalar.activation(b_tk, bk[6], ACT.Copy).then_inc(bt_tok_ready, 1)
                    wait_group(act, 6 + m, g)
                    nc.scalar.activation(zs[:, m, :], bk[(6 + m) % 4], ACT.Silu).then_inc(z_ready, 1)
                for j in range(TILES):
                    act.wait_ge(te_in, g * 4 + j + 1)
                    nc.scalar.activation(te[j % 2], te[j % 2], ACT.Exp).then_inc(te_ready, 1)
                    act.wait_ge(d_ready, g * 4 + j + 1)
                    nc.scalar.activation(m_sb[j % 2], m_sb[j % 2], ACT.Exp).then_inc(m_exp, 1)
                act.wait_ge(yg_ready, g * 4 + 4)
                act.wait_ge(dve_done_e, g + 1)
                nc.scalar.activation(ysq2, y_g.rearrange("p m t -> p (m t)"), ACT.Square).then_inc(ysq_ready, 1)
                act.wait_ge(gn_ready, g + 1)
                nc.scalar.activation(rstd2, rstd2, ACT.Sqrt).then_inc(act_group, 1)

            with act.Fori(0, GROUPS) as g:
                group(g)

            act.wait_ge(dve_group, GROUPS)

            def gates(jj, first):
                for u in range(2):
                    if not first:
                        act.wait_ge(merged_ready, jj * 2 + u - 1)
                    for i, dst in enumerate([sg_a[u], sg_b[u]]):
                        wait_merge(act, 1 + i, jj * 2 + u)
                        nc.scalar.activation(dst, bk[4 * u + 1 + i], ACT.Sigmoid).then_inc(sig_ready, 1)

            gates(0, True)
            with act.Fori(1, KT // 2) as jj:
                gates(jj, False)

            for t in range(TILES):
                act.wait_ge(x1_done, 2 * t + 2)
                if t > 0:
                    act.wait_ge(sumsq_ready, TILES + t)
                nc.scalar.activation(sq_row, x1_tok[:, t, :], ACT.Square, accum_out=sm[0][:, t:t + 1]).then_inc(sumsq_ready, 1)
            act.wait_ge(ms_ready, 2)
            nc.scalar.activation(sm[1], sm[1], ACT.Sqrt).then_inc(rms_ready, 1)
            for t in range(TILES):
                for h in range(2):
                    act.wait_ge(norm_tr, 2 * TILES + 2 * t + h + 1)
                    nc.scalar.activation(h2T[:, 4 * h:4 * h + 4, t * P:(t + 1) * P],
                                         bk[h].rearrange("p (k t) -> p k t", k=4), ACT.Copy).then_inc(h2T_ready, 1)
            act.wait_ge(r_exp_in, 1)
            nc.scalar.activation(gs[1], gs[1], ACT.Exp).then_inc(r_exp, 1)
            act.wait_ge(r_exp_in, 2)
            nc.scalar.activation(sm[5], sm[5], ACT.Exp).then_inc(r_exp, 1)

            act.wait_ge(items_out, 1)
            act.wait_ge(scattered, 16 * 2 * TILES)
            last_pair = act.value_load(item_i[0:1, MAX_BLOCKS:MAX_BLOCKS + 1], min_val=N_EXPERTS // 2 - 1, max_val=MAX_BLOCKS // 2 - 1)
            YST = [yst0, yst1]

            def copy_rows(w):
                act.wait_ge(xg_tr, w + 1)
                nc.scalar.activation(xgT, bk[6].rearrange("p (k s) -> p k s", k=KT), ACT.Copy).then_inc(xg_ready, 1)

            def expert_pair(i, first, final):
                for u in range(2):
                    w = i * 2 + u
                    act.wait_ge(h13_mm, w + 1)
                    nc.scalar.activation(silu_hi, bk[2 * u][0:BLOCK, :], ACT.Silu).then_inc(silu_ready, 1)
                    if not (final and u == 1):
                        copy_rows(w + 1)
                    act.wait_ge(hid_tr, w + 1)
                    nc.scalar.activation(hidT, bk[7][:, 0:FT * BLOCK].rearrange("p (k s) -> p k s", k=FT), ACT.Copy).then_inc(hidT_ready, 1)
                    if not first:
                        act.wait_ge(YST[u], i * 16)
                    act.wait_ge(y2_mm, w + 1)
                    nc.scalar.activation(y_out[u][:, 0:512], bk[4][0:BLOCK, :], ACT.Copy).then_inc(ycopy_a, 1)

            copy_rows(0)
            expert_pair(0, True, False)
            with act.Fori(1, last_pair) as i:
                expert_pair(i, False, False)
            expert_pair(last_pair, False, True)
            for t in range(TILES):
                act.wait_ge(ysum, 2 * t + 2)
                done(act, nc.scalar.activation(sq_row, x1_tok[:, t, :], ACT.Square, accum_out=sm[0][:, t:t + 1]), sumsq_ready, 2 * TILES + t + 1)
                act.wait_ge(ms_ready, t + 3)
                nc.scalar.activation(sm[1][:, t:t + 1], sm[1][:, t:t + 1], ACT.Sqrt).then_inc(rms_ready, 1)

        @block.vector
        def _(dve):
            V = nc.vector
            link = chain(dve, dve_step, 0)
            link(V.memset(not_start, 1.0))
            link(V.memset(not_start[:, 0::P], 0.0))
            dve.wait_ge(idx_ready, 2)
            link(V.tensor_copy(col_f, idx_i[:, P:P + 1]))
            link(V.tensor_copy(row_f, idx_i[:, 0:P]))
            link(V.tensor_scalar(tri2[:, 0:P], row_f, col_f, None, ALU.is_gt))
            link(V.tensor_scalar(tri2[:, P:2 * P], row_f, col_f, None, ALU.is_ge))
            link(V.tensor_scalar(neg_tri, tri2[:, P:2 * P], -1.0, BIG, ALU.add, ALU.mult))
            sh = idx_i[:, P + 1:2 * (P + 1)]
            for n in range(LEVELS + 2):
                link(V.tensor_scalar(sh, idx_i[:, 0:P + 1], n, None, ALU.logical_shift_right))
                link(V.tensor_copy(row_sh, sh[:, 0:P]))
                link(V.tensor_copy(col_sh, sh[:, P:P + 1]))
                link(V.tensor_scalar(eq_blocks[n], row_sh, col_sh, None, ALU.is_equal))
            link(V.tensor_copy(ident, eq_blocks[0]))
            link(V.tensor_copy(head_ones, eq_blocks[6]))
            link(V.tensor_copy(ones, eq_blocks[7]))
            for n in range(LEVELS + 1):
                link(V.tensor_tensor(eq_tmp, eq_blocks[n + 1], eq_blocks[n], ALU.subtract))
                link(V.tensor_tensor(level_mask[n], eq_tmp, tri2[:, 0:P], ALU.mult))
            dve.wait_ge(rows_in, 16 * 16)
            link(V.tensor_copy(rows[3][0:16].rearrange("p (b r) -> p b r", b=2),
                               dskip_in[0:16].unsqueeze(2).broadcast_to([16, 2, RWKV_HEAD])))
            V.memset(s_small[:, 62:63], 0.0).then_inc(masks_ready, 1)
            dve.wait_ge(sumsq_ready, TILES)
            V.tensor_scalar(s_small[:, 4:8], s_small[:, 0:4], 1.0 / D_MODEL, 1e-6, ALU.mult, ALU.add).then_inc(ms_ready, 1)
            dve.wait_ge(rms_ready, 1)
            V.reciprocal(s_small[:, 8:12], s_small[:, 4:8]).then_inc(rstd_ready, 1)
            dve.wait_ge(rows_tr, 4)
            for i in range(10):
                link(V.tensor_copy(pp3[:, :, i], bk[7][:, 8 * i:8 * i + 8]))
            link(V.tensor_copy(norm1_c, bk[7][:, 80:88]))
            link(V.tensor_copy(lora_mu[:, 0:2], bk[7][:, 88:90]))
            link(V.tensor_scalar(lora_mu[:, 2:4], lora_mu[:, 0:2], -1.0, 1.0, ALU.mult, ALU.add))
            link(V.tensor_scalar(pp3[:, :, 10:13], pp3[:, :, 0:3], -1.0, 1.0, ALU.mult, ALU.add))
            link(V.tensor_scalar(pp3[:, :, 13:14], pp3[:, :, 6:7], -1.0, 1.0, ALU.mult, ALU.add))
            for tap in range(5):
                o = P + tap * 24
                link(V.tensor_copy(cp4[:, :, 0:4, tap], bk[7][:, o:o + 16].rearrange("p (g s) -> p g s", g=GROUPS)))
                link(V.tensor_copy(cp4[:, :, 4, tap], bk[7][:, o + 16:o + 20]))
                link(V.tensor_copy(cp4[:, :, 5, tap], bk[7][:, o + 20:o + 24]))
            for n in range(2):
                link(V.tensor_copy(op3[:, :, 4 * n:4 * n + 4],
                                   bk[7][:, 2 * P + 16 * n:2 * P + 16 * n + 16].rearrange("p (g s) -> p g s", g=GROUPS)))
            V.memset(s_small[:, 63:64], 0.0).then_inc(prm_ready, 1)
            for t in range(TILES):
                for h in range(2):
                    n = 2 * t + h
                    dve.wait_ge(norm_tr, n + 1)
                    V.tensor_tensor(hT[:, 4 * h:4 * h + 4, t * P:(t + 1) * P],
                                    bk[n % 4].rearrange("p (k t) -> p k t", k=4),
                                    norm1_c[:, 4 * h:4 * h + 4].unsqueeze(2).broadcast_to([P, 4, P]), ALU.mult
                                    ).then_inc(hT_ready, 1)
            for i, dst in enumerate([lo_wa, lo_g]):
                dve.wait_ge(lo_scaled, i + 1)
                V.scalar_tensor_tensor(dst[:, 1:SEQ], bk[i][:, 0:SEQ - 1], lora_mu[:, i:i + 1], dst[:, 1:SEQ],
                                       ALU.mult, ALU.add).then_inc(lo_shifted, 1)
            dve.wait_ge(dt_proj, 1)
            dve.wait_ge(rows_in, 16 * 16)
            V.tensor_scalar(dtw[0], bk[2][0:MAMBA_HEADS, :], dtp[0:MAMBA_HEADS, 0:1], None, ALU.add).then_inc(dt_dve, 1)
            dve.wait_ge(dt_act, 2)
            V.tensor_scalar(dtw[3], dtw[2], 1.0, None, ALU.add).then_inc(dt_dve, 1)
            dve.wait_ge(dt_dve, 2)
            link(V.tensor_scalar(dtw[5], dtw[3], -1.0, None, ALU.add))
            link(V.tensor_scalar(dtw[6], dtw[5], 0.0, None, ALU.is_equal))
            link(V.tensor_tensor(dtw[5], dtw[5], dtw[6], ALU.add))
            link(V.reciprocal(dtw[5], dtw[5]))
            dve.wait_ge(dt_act, 4)
            link(V.tensor_tensor(dtw[4], dtw[4], dtw[6], ALU.add))
            link(V.tensor_tensor(dtw[4], dtw[4], dtw[5], ALU.mult))
            link(V.tensor_tensor(dtw[4], dtw[4], dtw[2], ALU.mult))
            link(V.scalar_tensor_tensor(dtw[4], dtw[0], 0.0, dtw[4], ALU.max, ALU.add))
            link(V.tensor_scalar(dtp[0:MAMBA_HEADS, 3:4], dtp[0:MAMBA_HEADS, 2:3], -1.0, None, ALU.mult))
            link(V.tensor_scalar(dtw[7], dtw[4], dtp[0:MAMBA_HEADS, 3:4], None, ALU.mult))
            V.tensor_tensor_scan(dtw[1], not_start[0:MAMBA_HEADS], dtw[7], 0.0, ALU.mult, ALU.add).then_inc(dt_dve, 1)
            dve.wait_ge(dt_tr, 1)
            link(V.tensor_copy(dt_tok, bk[3][:, 0:P]))
            V.tensor_copy(acs_tok, bk[3][:, P:2 * P]).then_inc(dt_tok_ready, 1)
            dve.wait_ge(dt_tok_ready, 1)
            steps = link.count[0]

            PAIR_STEPS, GROUP_STEPS, MERGE_STEPS = 9, 20, 4

            def pair(c):
                link = chain(dve, dve_step, c * PAIR_STEPS + steps)
                dve.wait_ge(acs_stored, 16)
                done(dve, V.tensor_copy(prm, pair_prm[:, bass.ds(c * 14, 14)]), pair_prm_ready, c * 2 + 1)
                V.tensor_scalar(r_ones, head_ones, prm[:, 7:8], None, ALU.mult).then_inc(pair_prm_ready, 1)
                for i in range(3):
                    dve.wait_ge(rkv_scaled, c * 3 + i + 1)
                    V.scalar_tensor_tensor(rkv[i][:, 1:SEQ], bk[i][:, 0:SEQ - 1], prm[:, i:i + 1], rkv[i][:, 1:SEQ],
                                           ALU.mult, ALU.add).then_inc(shifted, 1)
                dve.wait_ge(lora_read, c * 3 + 1)
                link(V.tensor_tensor_scan(ccum, not_start, sigw, 0.0, ALU.mult, ALU.add))
                link(V.tensor_tensor(cc.rearrange("p (j t) -> p j t", j=TILES), ccum.rearrange("p (j t) -> p j t", j=TILES),
                                     ccum[:, RWKV_HEAD - 1::P].unsqueeze(2).broadcast_to([P, TILES, P]), ALU.subtract))
                V.tensor_tensor(cp, cc, sigw, ALU.subtract).then_inc(centered, 1)
                dve.wait_ge(kscale_ready, c + 1)
                dve.wait_ge(shifted, c * 3 + 3)
                V.tensor_tensor(k2, rkv[1], kscale, ALU.mult).then_inc(terms, 1)
                dve.wait_ge(nrm_ready, c + 1)
                link(V.tensor_scalar(rnorm, rnorm, 1e-12, None, ALU.max))
                link(V.reciprocal(rnorm, rnorm))
                done(dve, V.tensor_tensor(kkr, kkr, rnorm, ALU.mult), terms, c * 6 + 2)
                dve.wait_ge(exps_ready, c * 4 + 1)
                V.scalar_tensor_tensor(a_t, kkr, -1.0, e_a, ALU.mult, ALU.mult).then_inc(terms, 1)
                dve.wait_ge(exps_ready, c * 4 + 3)
                V.tensor_tensor(r_t, rkv[0], e_r, ALU.mult).then_inc(terms, 1)
                dve.wait_ge(kb_rk, c * 2 + 1)
                V.tensor_tensor(b_t, kb, e_b, ALU.mult).then_inc(terms, 1)
                dve.wait_ge(terms, c * 6 + 1)
                V.tensor_tensor(k_t, k2, e_b, ALU.mult).then_inc(terms, 1)
                dve.wait_ge(exps_ready, c * 4 + 4)
                V.tensor_tensor(s_small[:, 20:23], e_r[:, P - 1:3 * P:P], s_small[:, 17:20], ALU.mult).then_inc(f_ready, 1)
                dve.wait_ge(bonus_mm, c + 1)
                V.tensor_tensor(bonus, bk[6], rkv[2], ALU.mult).then_inc(bonus_ready, 1)
                t4 = tri2.rearrange("p (k t) -> p k t", k=2).unsqueeze(2).broadcast_to([P, 2, 2, P])
                for n in range(8):
                    j, of_k = n // 2, n % 2
                    dst = (gk if of_k else gb)[:, j].rearrange("p (k h) t -> p k h t", k=2)
                    dve.wait_ge(gram_mm, c * 8 + n + 1)
                    V.tensor_tensor(dst, bk[GRAM_BANKS[n % 4]].rearrange("p (k h t) -> p k h t", k=2, h=2), t4, ALU.mult
                                    ).then_inc(gram_ready, 1)
                dve.wait_ge(ginit_ready, c + 1)
                for lv in range(1, LEVELS + 1):
                    for q in range(2):
                        dve.wait_ge(g_mm, c * 12 + 2 * (lv - 1) + q + 1)
                        V.tensor_tensor(gi[:, q * 512:(q + 1) * 512], gi[:, q * 512:(q + 1) * 512], bk[5 + q], ALU.add
                                        ).then_inc(g_ready, 1)
                dve.wait_ge(f_ready, c + 1)
                dve.wait_ge(s_zero, 2)
                for j in range(TILES):
                    dve.wait_ge(x1_mm, c * 4 + j + 1)
                    V.tensor_copy(x1, bk[3][:, 0:P]).then_inc(x1_ready, 1)
                    dve.wait_ge(u_mm, c * 4 + j + 1)
                    V.tensor_copy(u_sb, bk[4][:, 0:P]).then_inc(u_ready, 1)
                    if j == TILES - 1:
                        break
                    dve.wait_ge(d_mm, c * 3 + j + 1)
                    if j > 0:
                        dve.wait_ge(fs_ready, c * 2 + j)
                        dve.wait_ge(y_mm, c * 4 + j)
                    for h in range(2):
                        q = slice(h * RWKV_HEAD, (h + 1) * RWKV_HEAD)
                        f = s_small[q, 20 + j:21 + j]
                        dst = st[(j + 1) % 2][q, q]
                        if j == 0:
                            ins = V.tensor_scalar(dst, bk[5][q, q], f, None, ALU.mult)
                        else:
                            ins = V.scalar_tensor_tensor(dst, bk[5][q, q], f, fs[q, q], ALU.mult, ALU.add)
                        ins.then_inc(s_ready, 1)
                y8 = bk[6].rearrange("p (n v) -> p n v", v=RWKV_HEAD)
                y8s = y_c.rearrange("p (n v) -> p n v", v=RWKV_HEAD)
                mean, var = s_small[:, 32:40], s_small[:, 40:48]
                dve.wait_ge(y_mm, c * 4 + 4)
                link(V.tensor_reduce(mean, y8, AX.X, ALU.add))
                link(V.tensor_scalar(mean, mean, 1.0 / RWKV_HEAD, None, ALU.mult))
                V.tensor_tensor(y8s, y8, mean.unsqueeze(2).broadcast_to([P, 8, RWKV_HEAD]), ALU.subtract).then_inc(head_norm, 1)
                dve.wait_ge(head_act, c * 2 + 1)
                link(V.tensor_reduce(var, y_sq.rearrange("p (n v) -> p n v", v=RWKV_HEAD), AX.X, ALU.add))
                V.tensor_scalar(var, var, 1.0 / RWKV_HEAD, 64e-5, ALU.mult, ALU.add).then_inc(head_norm, 1)
                dve.wait_ge(head_act, c * 2 + 2)
                link(V.reciprocal(var, var))
                done(dve, V.tensor_tensor(y8s, y8s, var.unsqueeze(2).broadcast_to([P, 8, RWKV_HEAD]), ALU.mult), head_norm, c * 3 + 3)
                dve.wait_ge(act_pair, c + 1)
                dve.wait_ge(bonus_ready, c + 1)
                link(V.tensor_tensor(y_3, y_3, bonus, ALU.add))
                V.tensor_tensor(ygT_t[:, bass.ds(c * SEQ, SEQ)], y_3, gate, ALU.mult).then_inc(dve_pair, 1)
                assert link.count[0] == PAIR_STEPS

            with dve.Fori(0, PAIRS) as c:
                pair(c)
                dve.wait_ge(dve_pair, c + 1)
                dve.wait_ge(act_pair, c + 1)
                dve.wait_ge(bm_ready, c * 7 + 7)
                dve.wait_ge(pe_pair, c + 1)

            def group(g):
                link = chain(dve, dve_step, g * GROUP_STEPS + steps + PAIRS * PAIR_STEPS)
                link(V.tensor_copy(oprm, out_prm[:, bass.ds(g * 8, 8)]))
                V.tensor_copy(cprm, conv_prm[:, bass.ds(g * 30, 30)]).then_inc(cprm_ready, 1)
                for t in range(6):
                    dve.wait_ge(taps_act, g * 6 + t + 1)
                    if t == 0:
                        dve.wait_ge(cprm_ready, g + 1)
                    for k in range(1, TAPS):
                        x = xbcT[:, t, k:SEQ]
                        ins = V.scalar_tensor_tensor(x, bk[t % 4][:, 0:SEQ - k], cprm[:, 5 * t + 3 - k:5 * t + 4 - k], x,
                                                     ALU.mult, ALU.add)
                        if k < TAPS - 1:
                            link(ins)
                        else:
                            ins.then_inc(taps_done, 1)
                for j in range(TILES):
                    dve.wait_ge(xt_tr, g * 4 + j + 1)
                    V.tensor_tensor(xdt[:, j, :].rearrange("p (h n) -> p h n", h=8), bk[4 + j % 2].rearrange("p (h n) -> p h n", h=8),
                                    dt_tok[:, bass.ds(g * 8 + j * MAMBA_HEADS, 8)].unsqueeze(2).broadcast_to([P, 8, RWKV_HEAD]),
                                    ALU.mult).then_inc(xdt_ready, 1)
                dve.wait_ge(acs_bc_in, g * 16 + 16)

                def decays(j):
                    tj = slice(j * P, (j + 1) * P)
                    at = acs_tok[:, bass.ds(g * 8 + j * MAMBA_HEADS, 8)]
                    if j >= 2:
                        dve.wait_ge(ym_mm, g * 4 + j - 1)
                    V.tensor_tensor(te[j % 2], acs_bc[:, :, j * P + P - 1], at, ALU.subtract).then_inc(te_in, 1)
                    link(V.tensor_tensor(m_sb[j % 2], acs_bc[:, :, tj], at.unsqueeze(2).broadcast_to([P, 8, P]), ALU.subtract))
                    V.tensor_tensor(m_sb[j % 2], m_sb[j % 2], neg_tri.unsqueeze(1).broadcast_to([P, 8, P]), ALU.add
                                    ).then_inc(d_ready, 1)
                    if j < TILES - 1:
                        dve.wait_ge(te_ready, g * 4 + j + 1)
                        dve.wait_ge(xdt_ready, g * 4 + j + 1)
                        if j == 2:
                            dve.wait_ge(st_mm, g * 3 + 1)
                        V.tensor_tensor(xe[j % 2].rearrange("p (h n) -> p h n", h=8), xdt[:, j, :].rearrange("p (h n) -> p h n", h=8),
                                        te[j % 2].unsqueeze(2).broadcast_to([P, 8, RWKV_HEAD]), ALU.mult).then_inc(xe_ready, 1)
                    dve.wait_ge(m_exp, g * 4 + j + 1)
                    dve.wait_ge(cb_mm, g * 4 + j + 1)
                    V.tensor_tensor(m_sb[j % 2], m_sb[j % 2], bk[6][:, 0:P].unsqueeze(1).broadcast_to([P, 8, P]), ALU.mult
                                    ).then_inc(m_ready, 1)

                def next_state(j):
                    dve.wait_ge(st_mm, g * 3 + j + 1)
                    if j == 0:
                        V.tensor_copy(state[1], bk[7]).then_inc(st_ready, 1)
                        return
                    if j == 1:
                        dve.wait_ge(e_bc_ready, g + 1)
                    dve.wait_ge(st_ready, g * 3 + j)
                    link(V.tensor_tensor(s_dec.rearrange("p (h n) -> p h n", h=8),
                                         state[j % 2].rearrange("p (h n) -> p h n", h=8),
                                         e_bc[:, :, j * P + P - 1].unsqueeze(2).broadcast_to([P, 8, RWKV_HEAD]), ALU.mult))
                    if j == 2:
                        dve.wait_ge(ym_mm, g * 4 + 2)
                    V.tensor_tensor(state[(j + 1) % 2], s_dec, bk[7], ALU.add).then_inc(st_ready, 1)

                def skip(j):
                    dve.wait_ge(ym_mm, g * 4 + j + 1)
                    if j == 0:
                        dve.wait_ge(xbc_ready, g * 6 + 4)
                    if j >= 2:
                        dve.wait_ge(yg_ready, g * 4 + j - 1)
                    ym = [y_m, y_m_b][j % 2]
                    for m in range(4):
                        ins = V.scalar_tensor_tensor(ym[:, m * P:(m + 1) * P], xbcT[:, m, j * P:(j + 1) * P], oprm[:, 4 + m:5 + m],
                                                     bk[4 + j % 2][:, m * P:(m + 1) * P], ALU.mult, ALU.add)
                    ins.then_inc(yskip_ready, 1)

                decays(0)
                next_state(0)
                for j in range(TILES - 1):
                    decays(j + 1)
                    if j < TILES - 2:
                        next_state(j + 1)
                    skip(j)
                skip(TILES - 1)
                V.memset(s_small[:, 59:60], 0.0).then_inc(dve_done_e, 1)
                dve.wait_ge(gn_mm, g + 1)
                V.tensor_scalar(rstd2, bk[6], 1.0 / 512, 1e-5, ALU.mult, ALU.add).then_inc(gn_ready, 1)
                dve.wait_ge(act_group, g + 1)
                link(V.reciprocal(rstd2, rstd2))
                for m in range(4):
                    ins = V.scalar_tensor_tensor(ymT_t[:, bass.ds(g * 4 * SEQ + m * SEQ, SEQ)], y_g[:, m, :], oprm[:, m:m + 1], rstd2,
                                                 ALU.mult, ALU.mult)
                ins.then_inc(dve_group, 1)
                assert link.count[0] == GROUP_STEPS

            with dve.Fori(0, GROUPS) as g:
                group(g)
                dve.wait_ge(dve_group, g + 1)

            with dve.Fori(0, KT // 2) as jj:
                link = chain(dve, dve_step, jj * MERGE_STEPS + steps + PAIRS * PAIR_STEPS + GROUPS * GROUP_STEPS)
                for u in range(2):
                    n = jj * 2 + u
                    dve.wait_ge(sig_ready, n * 2 + 2)
                    wait_merge(dve, 0, n)
                    wait_merge(dve, 4, n)
                    link(V.tensor_tensor(t_a[u], sg_a[u], bk[4 * u], ALU.mult))
                    link(V.tensor_tensor(t_b[u], sg_b[u], bk[4 * u + 3], ALU.mult))
                    V.tensor_tensor(arena[:, bass.ds(SLOT + 8192 + n * SEQ, SEQ)], t_a[u], t_b[u], ALU.add).then_inc(merged_ready, 1)
            for n in range(8):
                t, h = n // 2, n % 2
                dve.wait_ge(x_in, 2 * 16 * TILES)
                dve.wait_ge(out_mm, n + 1)
                x = x1_tok[:, t, h * 512:(h + 1) * 512]
                V.tensor_tensor(x, x, bk[n % 4], ALU.add).then_inc(x1_done, 1)
            dve.wait_ge(sumsq_ready, 2 * TILES)
            V.tensor_scalar(sm[1], sm[0], 1.0 / D_MODEL, 1e-6, ALU.mult, ALU.add).then_inc(ms_ready, 1)
            dve.wait_ge(rms_ready, 2)
            lk = chain(dve, dve_step, steps + PAIRS * PAIR_STEPS + GROUPS * GROUP_STEPS + KT // 2 * MERGE_STEPS)
            lk(V.reciprocal(sm[1], sm[1]))
            dve.wait_ge(router_in, 16 * 6)
            for t in range(TILES):
                V.scalar_tensor_tensor(h2_tok[:, t, :], x1_tok[:, t, :], sm[1][:, t:t + 1], g2_bc, ALU.mult, ALU.mult
                                       ).then_inc(h2_ready, 1)
            lk(V.tensor_copy(pri, idx_i[:, 0:32]))
            lk(V.tensor_scalar(pri, pri, -1.0, 32.0, ALU.mult, ALU.add))
            lk(V.memset(ones32, 1.0))
            for b in range(8):
                lk(V.memset(thr[:, :, b], float((b + 1) * BLOCK)))
            lk(V.tensor_copy(item_w, idx_i[:, 0:MAX_EXTRA]))
            lk(V.tensor_copy(item_f[0:1, 0:N_EXPERTS], idx_i[0:1, 0:N_EXPERTS]))
            lk(V.tensor_scalar(home, idx_i[:, 0:32], float(BLOCK), None, ALU.mult))
            bc = lambda x, n: x.unsqueeze(2).broadcast_to([P, TILES, n])
            row = lambda x, n: x.unsqueeze(1).broadcast_to([P, TILES, n])
            dve.wait_ge(logit_mm, TILES)
            for t in range(TILES):
                lk(V.tensor_tensor(lg[:, t, :], bk[4][:, t * 36:(t + 1) * 36], br_bc, ALU.add))
            lk(V.tensor_reduce(sm[2], g_l, AX.X, ALU.max))
            lk(V.tensor_tensor(gs[0], g_l, bc(sm[2], 4), ALU.is_equal))
            V.tensor_tensor(gs[1], g_l, bc(sm[2], 4), ALU.subtract).then_inc(r_exp_in, 1)
            lk(V.tensor_tensor(gs[0], gs[0], row(pri[:, 0:4], 4), ALU.mult))
            lk(V.tensor_reduce(sm[3], gs[0], AX.X, ALU.max))
            lk(V.tensor_tensor(gs[0], gs[0], bc(sm[3], 4), ALU.is_equal))
            lk(V.tensor_scalar(gs[2], gs[0], -1.0, BIG, ALU.add, ALU.mult))
            for gg in range(N_GROUPS):
                lk(V.tensor_tensor(rt[0][:, :, gg * 8:gg * 8 + 8], e_l[:, :, gg * 8:gg * 8 + 8],
                                   gs[2][:, :, gg:gg + 1].broadcast_to([P, TILES, 8]), ALU.add))
            for k in range(2):
                top, oh = sm[6 + k], rt[1 + k]
                lk(V.tensor_reduce(top, rt[0], AX.X, ALU.max))
                lk(V.tensor_tensor(oh, rt[0], bc(top, 32), ALU.is_equal))
                lk(V.tensor_tensor(oh, oh, row(pri, 32), ALU.mult))
                lk(V.tensor_reduce(sm[8], oh, AX.X, ALU.max))
                lk(V.tensor_tensor(oh, oh, bc(sm[8], 32), ALU.is_equal))
                if k == 0:
                    lk(V.tensor_scalar(rt[3], oh, -3.0 * BIG, None, ALU.mult))
                    lk(V.tensor_tensor(rt[0], rt[0], rt[3], ALU.add))
            V.tensor_tensor(rt[3], rt[1], rt[2], ALU.add).then_inc(sel_ready, 1)
            V.tensor_tensor(sm[5], sm[7], sm[6], ALU.subtract).then_inc(r_exp_in, 1)
            dve.wait_ge(pos_mm, 1)
            lk(V.tensor_copy(rt[4].rearrange("p t n -> p (t n)"), bk[5][:, 0:P]))
            lk(V.tensor_tensor(over, bk[6][:, 0:32].unsqueeze(2).broadcast_to([P, 32, 8]), thr, ALU.is_gt))
            lk(V.tensor_reduce(extra, over, AX.X, ALU.add))
            lk(V.tensor_tensor_scan(incl, ones32, extra, 0.0, ALU.mult, ALU.add))
            lk(V.tensor_tensor(away, incl, extra, ALU.subtract))
            lk(V.tensor_scalar(away, away, float(BLOCK), float((N_EXPERTS - 1) * BLOCK), ALU.mult, ALU.add))
            lk(V.tensor_tensor(away, away, home, ALU.subtract))
            lk(V.tensor_scalar(rt[6], rt[4], float(BLOCK), None, ALU.is_ge))
            lk(V.tensor_tensor(rt[6], rt[6], row(away, 32), ALU.mult))
            lk(V.tensor_tensor(rt[4], rt[4], row(home, 32), ALU.add))
            lk(V.tensor_tensor(rt[4], rt[4], rt[6], ALU.add))
            for k in range(2):
                lk(V.tensor_tensor(rt[5], rt[4], rt[1 + k], ALU.mult))
                lk(V.tensor_reduce(r_f[k], rt[5], AX.X, ALU.add))
                ins = V.tensor_copy(r_i[:, k * TILES:(k + 1) * TILES], r_f[k])
                ins.then_inc(rows_out, 1)
            lk(V.tensor_tensor(item_c[0:1], incl[0:1].unsqueeze(1).broadcast_to([1, MAX_EXTRA, 32]),
                               item_w[0:1].unsqueeze(2).broadcast_to([1, MAX_EXTRA, 32]), ALU.is_le))
            lk(V.tensor_reduce(item_f[0:1, N_EXPERTS:MAX_BLOCKS], item_c[0:1], AX.X, ALU.add))
            lk(V.tensor_scalar(item_f[0:1, N_EXPERTS:MAX_BLOCKS], item_f[0:1, N_EXPERTS:MAX_BLOCKS],
                               float(N_EXPERTS - 1), None, ALU.min))
            lk(V.tensor_scalar(item_w[0:1], item_w[0:1], incl[0:1, 31:32], None, ALU.is_lt))
            lk(V.tensor_reduce(s_small[0:1, 56:57], item_w[0:1, 0::2], AX.X, ALU.add))
            lk(V.tensor_scalar(item_f[0:1, MAX_BLOCKS:MAX_BLOCKS + 1], s_small[0:1, 56:57], float(N_EXPERTS // 2 - 1), None, ALU.add))
            V.tensor_copy(item_i[0:1, 0:MAX_BLOCKS + 1], item_f[0:1, 0:MAX_BLOCKS + 1]).then_inc(items_out, 1)
            dve.wait_ge(r_exp, 2)
            lk(V.tensor_reduce(sm[4], gs[1], AX.X, ALU.add))
            lk(V.tensor_scalar(sm[9], sm[5], 1.0, None, ALU.add))
            lk(V.tensor_tensor(sm[9], sm[9], sm[4], ALU.mult))
            lk(V.reciprocal(sm[10], sm[9]))
            lk(V.tensor_tensor(sm[11], sm[10], sm[5], ALU.mult))

            dve.wait_ge(items_out, 1)
            dve.wait_ge(scattered, 16 * 2 * TILES)
            last_pair = dve.value_load(item_i[0:1, MAX_BLOCKS:MAX_BLOCKS + 1], min_val=N_EXPERTS // 2 - 1, max_val=MAX_BLOCKS // 2 - 1)
            YST = [yst0, yst1]
            def expert_pair(i, first):
                for u in range(2):
                    w = i * 2 + u
                    dve.wait_ge(silu_ready, w + 1)
                    V.tensor_tensor(hid, silu_hi, bk[2 * u + 1][BLOCK:P, :], ALU.mult).then_inc(hid_ready, 1)
                    if not first:
                        dve.wait_ge(YST[u], i * 16)
                    dve.wait_ge(y2_mm, w + 1)
                    V.tensor_copy(y_out[u][:, 512:1024], bk[5][BLOCK:P, :]).then_inc(ycopy_b, 1)

            expert_pair(0, True)
            with dve.Fori(1, last_pair + 1) as i:
                expert_pair(i, False)
            for u in range(2):
                dve.wait_ge(YST[u], last_pair * 16 + 16)
                dve.wait_ge([xb_in0, xb_in1][u], last_pair * 16 + 32)
            V.memset(s_small[:, 57:58], 0.0).then_inc(experts_done, 1)
            YG = [yg_in0, yg_in1]
            for t in range(TILES):
                for k in range(2):
                    dve.wait_ge(YG[k], 16 * (t + 1))
                    done(dve, V.scalar_tensor_tensor(x1_tok[:, t, :], y_rows[k], sm[10 + k][:, t:t + 1], x1_tok[:, t, :],
                                                     ALU.mult, ALU.add), ysum, 2 * t + k + 1)
                dve.wait_ge(sumsq_ready, 2 * TILES + t + 1)
                V.tensor_scalar(sm[1][:, t:t + 1], sm[0][:, t:t + 1], 1.0 / D_MODEL, 1e-6, ALU.mult, ALU.add).then_inc(ms_ready, 1)
                dve.wait_ge(rms_ready, t + 3)
                lk(V.reciprocal(sm[1][:, t:t + 1], sm[1][:, t:t + 1]))
                V.scalar_tensor_tensor(x1_tok[:, t, :], x1_tok[:, t, :], sm[1][:, t:t + 1], gf_bc, ALU.mult, ALU.mult
                                       ).then_inc(final_ready, 1)

        @block.tensor
        def _(pe):
            T = nc.tensor

            def mm(dst, lhsT, rhs, start, stop):
                return T.matmul(dst, lhsT, rhs, start=start, stop=stop, skip_group_check=True)

            def project(dst, slot, src, uses, m=P):
                pe.wait_ge(w_loaded[slot], uses)
                for k in range(KT):
                    last = mm(dst, ring[slot][:, k, 0:m], src[:, k, :], k == 0, k == KT - 1)
                last.then_inc(slot_done[slot], 1)

            pe.wait_ge(masks_ready, 1)
            pe.wait_ge(rows_in, 16 * 16)
            for i, (n, o) in enumerate([(90, 0), (120, P), (16, 2 * P), (16, 2 * P + 16)]):
                T.transpose(bk[7][:, o:o + n], rows[i][0:n, :], ident[0:n, 0:n]).then_inc(rows_tr, 1)
            for t in range(TILES):
                pe.wait_ge(xn_ready, t + 1)
                for h in range(2):
                    n = 2 * t + h
                    if n >= 4:
                        pe.wait_ge(hT_ready, n - 3)
                    for k in range(4):
                        last = T.transpose(bk[n % 4][:, k * P:(k + 1) * P], xn_tok[:, t, (4 * h + k) * P:(4 * h + k + 1) * P], ident)
                    last.then_inc(norm_tr, 1)
            pe.wait_ge(hT_ready, 2 * TILES)
            project(bk[0], 0, hT, 16)
            project(bk[1], 1, hT, 16)
            pe.wait_ge(dtw_in, 16)
            for k in range(KT):
                last = mm(bk[2][0:MAMBA_HEADS, :], dt_w[:, k, :], hT[:, k, :], k == 0, k == KT - 1)
            last.then_inc(dt_proj, 1)
            pe.wait_ge(dt_dve, 3)
            for i, src in enumerate([dtw[4], dtw[1]]):
                for j in range(TILES):
                    o = i * P + j * MAMBA_HEADS
                    last = T.transpose(bk[3][:, o:o + MAMBA_HEADS], src[:, j * P:(j + 1) * P], ident[0:MAMBA_HEADS, 0:MAMBA_HEADS])
            last.then_inc(dt_tr, 1)

            def pair(c, more):
                pe.wait_ge(lorac_ready, c * 3 + 3)
                pe.wait_ge(lo_ready, 2)
                for i, src in enumerate([lo_wa, lo_wa, lo_g]):
                    mm(bk[3 + i], lora_c[i], src, True, True).then_inc(lora_mm, 1)
                if more:
                    pe.wait_ge(shifted, c * 3 + 1)
                    project(bk[0], 0, hT, (c + 2 + BASE_PAIR[0]) * 16)
                pe.wait_ge(ksq_ready, c * 2 + 1)
                pe.wait_ge(lora_read, c * 3 + 1)
                mm(bk[3], head_ones, ksq, True, True).then_inc(norm_mm, 1)
                if more:
                    for i in (1, 2):
                        pe.wait_ge(shifted, c * 3 + 1 + i)
                        project(bk[i], i, hT, (c + 2 + BASE_PAIR[i]) * 16)
                pe.wait_ge(kb_rk, c * 2 + 2)
                pe.wait_ge(pair_prm_ready, c * 2 + 2)
                mm(bk[6], r_ones, rk, True, True).then_inc(bonus_mm, 1)
                for i, (src, b) in enumerate([(rkv[2], 4), (b_t, 5), (k_t, 3)]):
                    if i == 0:
                        pe.wait_ge(shifted, c * 3 + 3)
                        pe.wait_ge(lora_read, c * 3 + 3)
                    elif i == 1:
                        pe.wait_ge(terms, c * 6 + 5)
                    else:
                        pe.wait_ge(terms, c * 6 + 6)
                        pe.wait_ge(nrm_ready, c + 1)
                    for j in range(TILES):
                        last = T.transpose(bk[b][:, j * P:(j + 1) * P], src[:, j * P:(j + 1) * P], ident)
                    last.then_inc(tok_tr, 1)
                pe.wait_ge(ar_ready, c * 4 + 4)
                for n in range(8):
                    j, of_k = n // 2, n % 2
                    if n == 1:
                        pe.wait_ge(tok_ready, c * 3 + 3)
                    if n >= 4:
                        pe.wait_ge(gram_ready, c * 8 + n - 3)
                    mm(bk[GRAM_BANKS[n % 4]], (k_t if of_k else b_t)[:, j * P:(j + 1) * P],
                       ar[:, j].rearrange("p f t -> p (f t)"), True, True).then_inc(gram_mm, 1)
                pe.wait_ge(gram_ready, c * 8 + 8)
                pe.wait_ge(ginit_ready, c + 1)

                def transpose_g(q):
                    for k in range(4):
                        o = q * 512 + k * P
                        last = T.transpose(bk[3 + q][:, k * P:(k + 1) * P], gi[:, o:o + P], ident)
                    last.then_inc(h_tr, 1)

                for q in range(2):
                    transpose_g(q)
                pe.wait_ge(bonus_ready, c + 1)
                for lv in range(1, LEVELS + 1):
                    pe.wait_ge(bm_ready, c * 7 + lv + 1)
                    for q in range(2):
                        pe.wait_ge(h_ready, c * 12 + 2 * (lv - 1) + q + 1)
                        for k in range(4):
                            b_blk = bm[lv % 2][:, 2 * q + k // 2, k % 2, :]
                            last = mm(bk[3 + q][:, k * P:(k + 1) * P], b_blk, hi[:, q * 512 + k * P:q * 512 + (k + 1) * P], k == 0, k == 3)
                        last.then_inc(xt_mm, 1)
                    for q in range(2):
                        pe.wait_ge(xt_ready, c * 12 + 2 * (lv - 1) + q + 1)
                        for k in range(4):
                            o = q * 512 + k * P
                            last = mm(bk[5 + q][:, k * P:(k + 1) * P], xt[:, o:o + P], gi[:, o:o + P], k == 0, k == 3)
                        last.then_inc(g_mm, 1)
                    if lv < LEVELS:
                        for q in range(2):
                            pe.wait_ge(g_ready, c * 12 + 2 * (lv - 1) + q + 1)
                            transpose_g(q)
                pe.wait_ge(g_ready, c * 12 + 12)
                for j in range(TILES):
                    tj = slice(j * P, (j + 1) * P)
                    for h in range(2):
                        vh = slice(j * P + h * RWKV_HEAD, j * P + (h + 1) * RWKV_HEAD)
                        last = mm(bk[3][:, h * RWKV_HEAD:(h + 1) * RWKV_HEAD], gk[:, j, h, :], v_tok[:, vh], h == 0, h == 1 and j == 0)
                    if j > 0:
                        pe.wait_ge(s_ready, c * 6 + 2 * j)
                        last = mm(bk[3][:, 0:P], a_t[:, tj], st[j % 2], False, True)
                    last.then_inc(x1_mm, 1)
                    if j < TILES - 1:
                        mm(bk[5][:, 0:P], k_tok[:, tj], v_tok[:, tj], True, False)
                    if j > 0:
                        mm(bk[6][:, tj], r_t[:, tj], st[j % 2], True, False)
                    for h in range(2):
                        vh = slice(j * P + h * RWKV_HEAD, j * P + (h + 1) * RWKV_HEAD)
                        mm(bk[6][:, vh], gk[:, j, 2 + h, :], v_tok[:, vh], j == 0 and h == 0, False)
                    pe.wait_ge(x1_ready, c * 4 + j + 1)
                    for h in range(2):
                        o = slice(h * RWKV_HEAD, (h + 1) * RWKV_HEAD)
                        last = mm(bk[4][:, o], gi4[:, j, h, :], x1[:, o], h == 0, h == 1)
                    last.then_inc(u_mm, 1)
                    pe.wait_ge(u_ready, c * 4 + j + 1)
                    if j < TILES - 1:
                        mm(bk[5][:, 0:P], b_tok[:, tj], u_sb, False, True).then_inc(d_mm, 1)
                    for h in range(2):
                        o = slice(h * RWKV_HEAD, (h + 1) * RWKV_HEAD)
                        last = mm(bk[6][:, j * P + h * RWKV_HEAD:j * P + (h + 1) * RWKV_HEAD], gb[:, j, 2 + h, :], u_sb[:, o], False, True)
                    last.then_inc(y_mm, 1)
                pe.wait_ge(head_norm, c * 3 + 3)
                for j in range(TILES):
                    last = T.transpose(bk[7][:, j * P:(j + 1) * P], y_c[:, j * P:(j + 1) * P], ident)
                last.then_inc(pe_pair, 1)

            pe.wait_ge(lo_shifted, 2)
            pe.wait_ge(dt_dve, 1)
            pe.wait_ge(dt_tok_ready, 1)
            for i in range(3):
                project(bk[i], i, hT, (1 + BASE_PAIR[i]) * 16)
            with pe.Fori(0, PAIRS - 1) as c:
                pair(c, True)
                pe.wait_ge(dve_pair, c + 1)
                pe.wait_ge(act_pair, c + 1)
                pe.wait_ge(bm_ready, c * 7 + 7)
            pair(PAIRS - 1, False)

            def group_tile(g, t):
                project(bk[t % 4], t % 5, hT, (g * 2 + BASE_GROUP[t % 5] + t // 5 + 1) * 16)

            def group(g, more):
                for t in range(4, 8):
                    pe.wait_ge(taps_done, g * 6 + t - 3)
                    group_tile(g, t)
                pe.wait_ge(xbc_ready, g * 6 + 5)
                for j in range(TILES):
                    tj = slice(j * P, (j + 1) * P)
                    last = T.transpose(bk[6][:, tj], xbcT[:, 4, tj], ident)
                last.then_inc(bt_tr, 1)
                for j in range(TILES):
                    tj = slice(j * P, (j + 1) * P)
                    if j >= 2:
                        pe.wait_ge(xdt_ready, g * 4 + j - 1)
                    for m in range(4):
                        last = T.transpose(bk[4 + j % 2][:, m * P:(m + 1) * P], xbcT[:, m, tj], ident)
                    last.then_inc(xt_tr, 1)
                for t in (8, 9):
                    pe.wait_ge(taps_done, g * 6 + t - 3)
                    group_tile(g, t)

                def scores(j):
                    if j > 0:
                        pe.wait_ge(m_ready, g * 4 + j)
                    tj = slice(j * P, (j + 1) * P)
                    mm(bk[6][:, 0:P], xbcT[:, 4, tj], xbcT[:, 5, tj], True, True).then_inc(cb_mm, 1)

                def state_part(j):
                    pe.wait_ge(xe_ready, g * 3 + j + 1)
                    if j > 0:
                        pe.wait_ge(st_ready, g * 3 + j)
                    mm(bk[7], b_tk[:, j * P:(j + 1) * P], xe[j % 2], True, True).then_inc(st_mm, 1)

                def outputs(j):
                    pe.wait_ge(m_ready, g * 4 + j + 1)
                    if j > 0:
                        pe.wait_ge(c_ready, g * 3 + j)
                        pe.wait_ge(st_ready, g * 3 + j)
                    if j >= 2:
                        pe.wait_ge(yskip_ready, g * 4 + j - 1)
                    for h in range(8):
                        half, m = h % 2, h // 2
                        dst = bk[4 + j % 2][half * 64:half * 64 + 64, m * P:(m + 1) * P]
                        hs = slice(h * RWKV_HEAD, (h + 1) * RWKV_HEAD)
                        last = mm(dst, xdt[:, j, hs], m_sb[j % 2][:, h, :], m == 0, j == 0)
                        if j > 0:
                            last = mm(dst, state[j % 2][:, hs], c_sb[j % 2][:, h, :], False, True)
                    last.then_inc(ym_mm, 1)

                def next_tile(t):
                    if more:
                        pe.wait_ge(z_ready, g * 4 + [3, 4, 1, 2][t])
                        group_tile(g + 1, t)

                pe.wait_ge(bt_tok_ready, g + 1)
                pe.wait_ge(xbc_ready, g * 6 + 6)
                pe.wait_ge(xdt_ready, g * 4 + 4)
                scores(0)
                next_tile(0)
                state_part(0)
                for j in range(TILES - 1):
                    scores(j + 1)
                    outputs(j)
                    if j < TILES - 2:
                        next_tile(j + 1)
                        state_part(j + 1)
                outputs(TILES - 1)
                next_tile(3)
                pe.wait_ge(ysq_ready, g + 1)
                for m in range(4):
                    last = mm(bk[6], ones, ysq2[:, m * SEQ:(m + 1) * SEQ], m == 0, m == 3)
                last.then_inc(gn_mm, 1)

            pe.wait_ge(dve_pair, PAIRS)
            pe.wait_ge(act_pair, PAIRS)
            pe.wait_ge(bm_ready, PAIRS * 7)
            for t in range(4):
                group_tile(0, t)
            with pe.Fori(0, GROUPS - 1) as g:
                group(g, True)
            group(GROUPS - 1, False)

            def merge_products(jj, first):
                for u in range(2):
                    if not first:
                        pe.wait_ge(merged_ready, jj * 2 + u - 1)
                    for s in range(5):
                        uses = (jj * 2 + u + BASE_MERGE[s] + 1) * 16
                        src = [ygT, hT, hT, ymT[:, 0:KT], ymT[:, KT:2 * KT]][s]
                        pe.wait_ge(w_loaded[s], uses)
                        if first and u == 0 and s == 3:
                            pe.wait_ge(dve_group, GROUPS)
                        for k in range(KT):
                            last = mm(bk[4 * u + min(s, 3)], ring[s][:, k, :], src[:, k, :], k == 0 and s < 4, k == KT - 1 and s != 3)
                        last.then_inc(slot_done[s], 1)

            merge_products(0, True)
            with pe.Fori(1, KT // 2) as jj:
                merge_products(jj, False)
            pe.wait_ge(merged_ready, KT)
            for n in range(8):
                t, h = n // 2, n % 2
                pe.wait_ge(w_out_in, 32)
                if n >= 4:
                    pe.wait_ge(x1_done, n - 3)
                for k in range(KT):
                    last = mm(bk[n % 4], merged[:, k, t * P:(t + 1) * P], w_out_sb[:, k, h * 512:(h + 1) * 512], k == 0, k == KT - 1)
                last.then_inc(out_mm, 1)
            for t in range(TILES):
                pe.wait_ge(h2_ready, t + 1)
                for h in range(2):
                    if t > 0:
                        pe.wait_ge(h2T_ready, 2 * t + h - 1)
                    for k in range(4):
                        last = T.transpose(bk[h][:, k * P:(k + 1) * P], h2_tok[:, t, (4 * h + k) * P:(4 * h + k + 1) * P], ident)
                    last.then_inc(norm_tr, 1)
            pe.wait_ge(router_in, 16 * 6)
            for t in range(TILES):
                pe.wait_ge(h2T_ready, 2 * t + 2)
                for k in range(KT):
                    last = mm(bk[4][:, t * 36:(t + 1) * 36], h2T[:, k, t * P:(t + 1) * P], wr_sb[:, k, :], k == 0, k == KT - 1)
                last.then_inc(logit_mm, 1)
            pe.wait_ge(sel_ready, 1)
            for t in range(TILES):
                o = bk[5][:, t * 32:(t + 1) * 32]
                mm(o, tri2[:, 0:P], rt[3][:, t, :], True, t == 0)
                for t2 in range(t):
                    mm(o, ones, rt[3][:, t2, :], False, t2 == t - 1)
            for t in range(TILES):
                last = mm(bk[6][:, 0:32], ones, rt[3][:, t, :], t == 0, t == TILES - 1)
            last.then_inc(pos_mm, 1)

            pe.wait_ge(items_out, 1)
            last_pair = pe.value_load(item_i[0:1, MAX_BLOCKS:MAX_BLOCKS + 1], min_val=N_EXPERTS // 2 - 1, max_val=MAX_BLOCKS // 2 - 1)
            W1_IN, W3_IN, W2_IN, XB_IN = [w1_in0, w1_in1], [w3_in0, w3_in1], [w2_in0, w2_in1], [xb_in0, xb_in1]

            def rows_in_block(w, u, seen):
                pe.wait_ge(XB_IN[u], seen)
                for k in range(KT):
                    last = mm(bk[6][:, k * BLOCK:(k + 1) * BLOCK], xs_sb[u][:, k::KT], ident[0:BLOCK, 0:BLOCK], True, True)
                last.then_inc(xg_tr, 1)

            def first_products(w, u, seen):
                pe.wait_ge(xg_ready, w + 1)
                pe.wait_ge(W1_IN[u], seen)
                pe.wait_ge(W3_IN[u], seen)
                for k in range(KT):
                    mm(bk[2 * u][0:BLOCK, :], xgT[:, k, :], w1_sb[u][:, k, :], k == 0, k == KT - 1)
                    last = mm(bk[2 * u + 1][BLOCK:P, :], xgT[:, k, :], w3_sb[u][:, k, :], k == 0, k == KT - 1)
                last.then_inc(h13_mm, 1)

            def expert_pair(i, first, final):
                for u in range(2):
                    w = i * 2 + u
                    more = not (final and u == 1)
                    next_seen = (i + 1 + u) * 16
                    if more:
                        rows_in_block(w + 1, 1 - u, next_seen)
                    pe.wait_ge(hid_ready, w + 1)
                    for k in range(FT):
                        last = mm(bk[7][:, k * BLOCK:(k + 1) * BLOCK], hid[:, k::FT], ident[0:BLOCK, 0:BLOCK], True, True)
                    last.then_inc(hid_tr, 1)
                    if more:
                        first_products(w + 1, 1 - u, next_seen)
                    pe.wait_ge(hidT_ready, w + 1)
                    pe.wait_ge(W2_IN[u], (i + 1) * 16)
                    if not first or u > 0:
                        pe.wait_ge(ycopy_a, w)
                        pe.wait_ge(ycopy_b, w)
                    for k in range(FT):
                        mm(bk[4][0:BLOCK, :], hidT[:, k, :], w2_sb[u][:, k, 0:512], k == 0, k == FT - 1)
                        last = mm(bk[5][BLOCK:P, :], hidT[:, k, :], w2_sb[u][:, k, 512:1024], k == 0, k == FT - 1)
                    last.then_inc(y2_mm, 1)

            rows_in_block(0, 0, 16)
            first_products(0, 0, 16)
            expert_pair(0, True, False)
            with pe.Fori(1, last_pair) as i:
                expert_pair(i, False, False)
            expert_pair(last_pair, False, True)


_INS = ['x', 'norm1_g', 'w_in', 'mu_rwkv', 'w0', 'w_decay2', 'a0', 'w_iclr2', 'w_gate2', 'k_k', 'k_a', 'r_k', 'lnx_g',
        'lnx_b', 'w_rwkv_o', 'conv_w', 'conv_b', 'dt_bias', 'a_log', 'd_skip', 'mnorm_g', 'w_mamba_o', 'w_out', 'norm2_g',
        'w_rg', 'b_rg', 'w_re', 'b_re', 'w_e1', 'w_e3', 'w_e2', 'final_g']


def kernel(**inputs):
    import numpy as np
    import concourse.bacc as bacc
    from concourse.bass_utils import run_bass_kernel_spmd

    nc = bacc.Bacc("TRN2", target_bir_lowering=False, num_devices=1)
    arrays, aps = {}, {}
    for name in _INS:
        arrays[f"in_{name}"] = np.ascontiguousarray(inputs[name])
        aps[name] = nc.dram_tensor(f"in_{name}", arrays[f"in_{name}"].shape, F32, kind="ExternalInput").ap()
    out = nc.dram_tensor("out_0", (1, SEQ, D_MODEL), F32, kind="ExternalOutput").ap()
    hybrid_block_kernel(nc, aps, out)
    r = run_bass_kernel_spmd(nc, [arrays], core_ids=[0])
    return r.results[0]["out_0"]
```

```python
import concourse.bass as bass
from concourse import mybir
from contextlib import ExitStack

F32 = mybir.dt.float32
I32 = mybir.dt.int32
ALU = mybir.AluOpType
ACT = mybir.ActivationFunctionType
AX = mybir.AxisListType

P = 128
D_MODEL = 1024
SEQ = 512
TILES = SEQ // P
KT = D_MODEL // P
RWKV_HEAD = 64
PAIRS = D_MODEL // P
DECAY_LORA = 64
RWKV_COLS = 3 * D_MODEL + 256
MAMBA_INNER = 2048
GROUPS = 4
HEADS_PER_GROUP = 8
MAMBA_HEADS = GROUPS * HEADS_PER_GROUP
XBC_TILES = (MAMBA_INNER + 2 * GROUPS * P) // P
TAPS = 4
Z_COL = RWKV_COLS
XS_COL = Z_COL + MAMBA_INNER
B_COL = XS_COL + MAMBA_INNER
C_COL = B_COL + GROUPS * P
DT_COL = C_COL + GROUPS * P
GATE_COL = DT_COL + MAMBA_HEADS
N_GROUPS = 4
N_EXPERTS = 32
EXPERT_FF = 512
FT = EXPERT_FF // P
BLOCK = 64
MAX_EXTRA = 2 * SEQ // BLOCK
MAX_BLOCKS = N_EXPERTS + MAX_EXTRA
XS_ROWS = (MAX_BLOCKS + 2) * BLOCK
ZERO_PAIRS = 5
ZERO_TILES = XS_ROWS // P // ZERO_PAIRS
KAPPA = 0.6065306597126334
BIG = 1.0e30
LEVELS = 6


def hybrid_block_kernel(nc, a, out):
    ctx = ExitStack()
    with ctx:
        def sem(name):
            return ctx.enter_context(nc.semaphore(name))

        def sb(name, cols):
            return ctx.enter_context(nc.sbuf_tensor(name, [P, cols], F32))

        hT_t = sb("hT", KT * SEQ)
        ygT_t = sb("ygT", PAIRS * SEQ)
        ymT_t = sb("ymT", 16 * SEQ)
        ring_t = sb("ring", 5 * KT * P)
        arena = sb("arena", 26240)
        const = sb("const", 3600)
        hT = hT_t[:, :].rearrange("p (k t) -> p k t", k=KT)
        ygT = ygT_t[:, :].rearrange("p (k t) -> p k t", k=PAIRS)
        ymT = ymT_t[:, :].rearrange("p (k t) -> p k t", k=16)
        ring = [ring_t[:, s * KT * P:(s + 1) * KT * P].rearrange("p (k m) -> p k m", k=KT) for s in range(5)]

        def taker(t):
            at = [0]

            def take(n):
                at[0] += n
                assert at[0] <= t[:, :].shape[1], (at[0], t[:, :].shape)
                return t[:, at[0] - n:at[0]]
            return take

        kc = taker(const)
        ident, head_ones, ones = kc(P), kc(P), kc(P)
        tri2 = kc(2 * P)
        neg_tri = kc(P)
        level_mask = [kc(P) for _ in range(LEVELS + 1)]
        not_start = kc(SEQ)
        pair_prm = kc(PAIRS * 14)
        norm1_c = kc(KT)
        lora_mu = kc(4)
        conv_prm = kc(GROUPS * 6 * 5)
        out_prm = kc(GROUPS * 8)
        prm = kc(14)
        cprm = kc(30)
        oprm = kc(8)
        dt_tok = kc(TILES * MAMBA_HEADS)
        acs_tok = kc(TILES * MAMBA_HEADS)
        s_small = kc(64)
        dtp = kc(4)
        pp3 = pair_prm.rearrange("p (c n) -> p c n", c=PAIRS)
        cp4 = conv_prm.rearrange("p (g s n) -> p g s n", g=GROUPS, s=6)
        op3 = out_prm.rearrange("p (g n) -> p g n", g=GROUPS)

        bank = [ctx.enter_context(nc.psum_tensor(f"bank{i}", [P, 512], F32)) for i in range(8)]
        bk = [b[:, :] for b in bank]

        acs_d = nc.dram_tensor("acs_d", [MAMBA_HEADS, SEQ], F32, kind="Internal").ap()
        xs_d = nc.dram_tensor("xs_d", [XS_ROWS, D_MODEL], F32, kind="Internal").ap()

        w_in = a["w_in"][0]

        def w_cols(mat, kt0, col):
            return mat[kt0 * P:(kt0 + KT) * P, bass.ds(col, P)].rearrange("(k p) m -> p k m", p=P)

        ks = taker(arena)
        ks(3 * D_MODEL + 2 * SEQ)
        x_tok = ks(TILES * D_MODEL).rearrange("p (t d) -> p t d", t=TILES)
        xn_tok = ks(TILES * D_MODEL).rearrange("p (t d) -> p t d", t=TILES)
        rows = [ks(P), ks(P), ks(P), ks(P)]
        dskip_in = ks(2)
        row_f, row_sh, eq_tmp = ks(P), ks(P), ks(P)
        col_f, col_sh = ks(1), ks(1)
        eq_blocks = [ks(P) for _ in range(LEVELS + 2)]
        idx_i = ctx.enter_context(nc.sbuf_tensor("idx_i", [P, 2 * (P + 1)], I32))
        sq_scr = ks(D_MODEL)
        dtw = [ks(SEQ)[0:MAMBA_HEADS] for _ in range(8)]
        dt_w = ks(KT * MAMBA_HEADS).rearrange("p (k m) -> p k m", k=KT)

        kr = taker(arena)
        lw_w = kr(D_MODEL)
        lw_a = kr(D_MODEL)
        lw_g = kr(D_MODEL)
        lo_wa, lo_g = kr(SEQ), kr(SEQ)
        rkv = [kr(SEQ) for _ in range(3)]
        sigw, iclr, gate = kr(SEQ), kr(SEQ), kr(SEQ)
        ccum, cc, cp = kr(SEQ), kr(SEQ), kr(SEQ)
        e_a, e_r, e_b = kr(SEQ), kr(SEQ), kr(SEQ)
        kkr, ksq, rnorm, kscale, k2, rk = kr(SEQ), kr(SEQ), kr(SEQ), kr(SEQ), kr(SEQ), kr(SEQ)
        kb, bonus = kr(SEQ), kr(SEQ)
        a_t, r_t, b_t, k_t = kr(SEQ), kr(SEQ), kr(SEQ), kr(SEQ)
        ar = kr(TILES * 4 * P).rearrange("p (j f t) -> p j f t", j=TILES, f=4)
        v_tok, b_tok, k_tok = kr(SEQ), kr(SEQ), kr(SEQ)
        x1, u_sb, fs = kr(P), kr(P), kr(P)
        st = [kr(P), kr(P)]
        r_ones = kr(P)
        lora_c = [kr(P) for _ in range(3)]
        y_c, y_sq, y_3 = kr(SEQ), kr(SEQ), kr(SEQ)
        km = taker(ymT_t)
        gb = km(TILES * 512).rearrange("p (j f t) -> p j f t", j=TILES, f=4)
        gk = km(TILES * 512).rearrange("p (j f t) -> p j f t", j=TILES, f=4)
        bm = [km(8 * P).rearrange("p (j f t) -> p j f t", j=TILES, f=2) for _ in range(2)]
        xt, gi, hi = km(8 * P), km(8 * P), kr(8 * P)
        lev8 = [m.unsqueeze(1).unsqueeze(1).broadcast_to([P, TILES, 2, P]) for m in level_mask]
        ident8 = ident.unsqueeze(1).unsqueeze(1).broadcast_to([P, TILES, 2, P])
        gi4 = gi.rearrange("p (j f t) -> p j f t", j=TILES, f=2)
        zero_tile = ygT_t[:, 6 * SEQ:8 * SEQ]

        kb2 = taker(arena)
        zs = kb2(4 * SEQ).rearrange("p (m t) -> p m t", m=4)
        xbcT = kb2(6 * SEQ).rearrange("p (m t) -> p m t", m=6)
        b_tk = kb2(SEQ)
        xdt = kb2(TILES * 512).rearrange("p (j n) -> p j n", j=TILES)
        xe = [kb2(512) for _ in range(2)]
        m_sb = [kb2(1024).rearrange("p (h t) -> p h t", h=8) for _ in range(2)]
        c_sb = [kb2(1024).rearrange("p (h t) -> p h t", h=8) for _ in range(2)]
        acs_bc = kb2(8 * SEQ).rearrange("p (h t) -> p h t", h=8)
        e_bc = kb2(8 * SEQ).rearrange("p (h t) -> p h t", h=8)
        state = [kb2(512) for _ in range(2)]
        s_dec = kb2(512)
        y_m, y_m_b = kb2(512), kb2(512)
        y_g = kb2(4 * SEQ).rearrange("p (m t) -> p m t", m=4)
        ysq2 = e_bc.rearrange("p h t -> p (h t)")[:, 0:4 * SEQ]
        rstd2 = kb2(SEQ)
        te = [kb2(8) for _ in range(2)]


        SLOT = 12288
        w1_sb = [arena[:, s_ * SLOT:s_ * SLOT + 4096].rearrange("p (k n) -> p k n", k=KT) for s_ in range(2)]
        w3_sb = [arena[:, s_ * SLOT + 4096:s_ * SLOT + 8192].rearrange("p (k n) -> p k n", k=KT) for s_ in range(2)]
        w2_sb = [arena[:, s_ * SLOT + 8192:s_ * SLOT + 12288].rearrange("p (k n) -> p k n", k=FT) for s_ in range(2)]
        merged = arena[:, SLOT + 8192:SLOT + 12288].rearrange("p (k t) -> p k t", k=KT)
        w_out_sb = arena[:, SLOT:SLOT + 8192].rearrange("p (k n) -> p k n", k=KT)
        mg = taker(arena)
        mg(8192)
        sg_a = [mg(SEQ), mg(SEQ)]
        sg_b = [mg(SEQ), mg(SEQ)]
        t_a = [mg(SEQ), mg(SEQ)]
        t_b = [mg(SEQ), mg(SEQ)]
        x1_tok = ygT_t[:, :].rearrange("p (t d) -> p t d", t=TILES)
        k5 = taker(ymT_t)
        h2T = k5(KT * SEQ).rearrange("p (k t) -> p k t", k=KT)
        h2_tok = k5(TILES * D_MODEL).rearrange("p (t d) -> p t d", t=TILES)
        k6 = taker(hT_t)
        g2_bc, gf_bc = k6(D_MODEL), k6(D_MODEL)
        wr_sb = k6(KT * 36).rearrange("p (k n) -> p k n", k=KT)
        br_bc = k6(36)
        sq_row = k6(D_MODEL)
        k8 = taker(ring_t)
        lg = k8(TILES * 36).rearrange("p (t n) -> p t n", t=TILES)
        g_l = lg[:, :, 0:4]
        e_l = lg[:, :, 4:36]
        rt = [k8(TILES * 32).rearrange("p (t n) -> p t n", t=TILES) for _ in range(7)]
        gs = [k8(TILES * 4).rearrange("p (t n) -> p t n", t=TILES) for _ in range(3)]
        sm = [k8(TILES) for _ in range(12)]
        thr = k8(32 * 8).rearrange("p (n b) -> p n b", n=32)
        over = k8(32 * 8).rearrange("p (n b) -> p n b", n=32)
        pri = k8(32)
        extra, incl, away, home = k8(32), k8(32), k8(32), k8(32)
        ones32 = k8(32)
        r_f = [k8(TILES), k8(TILES)]
        item_w = k8(MAX_EXTRA)
        item_f = k8(MAX_BLOCKS + 2)
        item_c = k8(MAX_EXTRA * 32).rearrange("p (w n) -> p w n", w=MAX_EXTRA)
        r_i = ctx.enter_context(nc.sbuf_tensor("r_i", [P, 2 * TILES], I32))
        item_i = ctx.enter_context(nc.sbuf_tensor("item_i", [P, MAX_BLOCKS + 2], I32))
        expert_buf = taker(ymT_t)
        xs_sb = [expert_buf(D_MODEL)[0:BLOCK] for _ in range(2)]
        xgT = expert_buf(KT * BLOCK).rearrange("p (k s) -> p k s", k=KT)
        silu_hi = expert_buf(EXPERT_FF)[BLOCK:2 * BLOCK]
        hid = expert_buf(EXPERT_FF)[0:BLOCK]
        hidT = expert_buf(FT * BLOCK).rearrange("p (k s) -> p k s", k=FT)
        y_out = [expert_buf(D_MODEL)[0:BLOCK] for _ in range(2)]
        y_rows = [arena[:, n * D_MODEL:(n + 1) * D_MODEL] for n in range(2 * TILES)]

        (head_norm, head_act, terms, kb_rk, lorac_ready, dve_done_e, ginit_ready, x_in) = (
            sem(n) for n in "head_norm head_act terms kb_rk lorac_ready dve_done_e ginit_ready x_in".split())
        (rows_in, dtw_in, zeros_ready, xs_zeroed, idx_ready, masks_ready, sumsq_ready, ms_ready) = (
            sem(n) for n in "rows_in dtw_in zeros_ready xs_zeroed idx_ready masks_ready sumsq_ready ms_ready".split())
        (rms_ready, rstd_ready, xn_ready, norm_tr, hT_ready, rows_tr, prm_ready, lora_in) = (
            sem(n) for n in "rms_ready rstd_ready xn_ready norm_tr hT_ready rows_tr prm_ready lora_in".split())
        (lo_scaled, lo_shifted, lo_ready, dt_proj, dt_act, dt_dve, dt_tr, dt_tok_ready) = (
            sem(n) for n in "lo_scaled lo_shifted lo_ready dt_proj dt_act dt_dve dt_tr dt_tok_ready".split())
        (acs_stored, rkv_scaled, shifted, pair_prm_ready, lora_mm, lora_read, ksq_ready, norm_mm) = (
            sem(n) for n in "acs_stored rkv_scaled shifted pair_prm_ready lora_mm lora_read ksq_ready norm_mm".split())
        (nrm_ready, kscale_ready, centered, exps_ready, ar_ready, bonus_mm, bonus_ready, tok_tr) = (
            sem(n) for n in "nrm_ready kscale_ready centered exps_ready ar_ready bonus_mm bonus_ready tok_tr".split())
        (tok_ready, gram_mm, gram_ready, bm_ready, g_ready, h_ready, h_tr, xt_mm) = (
            sem(n) for n in "tok_ready gram_mm gram_ready bm_ready g_ready h_ready h_tr xt_mm".split())
        (xt_ready, g_mm, x1_mm, x1_ready, u_mm, u_ready, d_mm, s_ready) = (
            sem(n) for n in "xt_ready g_mm x1_mm x1_ready u_mm u_ready d_mm s_ready".split())
        (fs_ready, f_ready, s_zero, y_mm, pe_pair, act_pair, dve_pair, dve_step) = (
            sem(n) for n in "fs_ready f_ready s_zero y_mm pe_pair act_pair dve_pair dve_step".split())
        (pool_step, z_ready, taps_act, taps_done, xbc_ready, acs_bc_in, e_bc_ready, bt_tr) = (
            sem(n) for n in "pool_step z_ready taps_act taps_done xbc_ready acs_bc_in e_bc_ready bt_tr".split())
        (bt_tok_ready, xt_tr, xdt_ready, cprm_ready, d_ready, m_exp, m_ready, cb_mm) = (
            sem(n) for n in "bt_tok_ready xt_tr xdt_ready cprm_ready d_ready m_exp m_ready cb_mm".split())
        (c_ready, ym_mm, st_mm, te_in, te_ready, xe_ready, st_ready, yskip_ready) = (
            sem(n) for n in "c_ready ym_mm st_mm te_in te_ready xe_ready st_ready yskip_ready".split())
        (yg_ready, ysq_ready, ysq_summed, gn_mm, gn_ready, act_group, dve_group, sig_ready, merged_ready) = (
            sem(n) for n in "yg_ready ysq_ready ysq_summed gn_mm gn_ready act_group dve_group sig_ready merged_ready".split())
        (w_out_in, router_in, out_mm, x1_done, h2_ready, h2T_ready, logit_mm, r_exp_in) = (
            sem(n) for n in "w_out_in router_in out_mm x1_done h2_ready h2T_ready logit_mm r_exp_in".split())
        (r_exp, sel_ready, pos_mm, scattered, rows_out, items_out, w1_in0, w1_in1, w3_in0) = (
            sem(n) for n in "r_exp sel_ready pos_mm scattered rows_out items_out w1_in0 w1_in1 w3_in0".split())
        (w3_in1, w2_in0, w2_in1, xb_in0, xb_in1, xg_tr, xg_ready, h13_mm) = (
            sem(n) for n in "w3_in1 w2_in0 w2_in1 xb_in0 xb_in1 xg_tr xg_ready h13_mm".split())
        (silu_ready, hid_ready, hid_tr, hidT_ready, y2_mm, ycopy_a, ycopy_b, yst0) = (
            sem(n) for n in "silu_ready hid_ready hid_tr hidT_ready y2_mm ycopy_a ycopy_b yst0".split())
        (yst1, yg_in0, yg_in1, yg_in2, yg_in3, experts_done, ysum, final_ready, out_stored) = (
            sem(n) for n in "yst1 yg_in0 yg_in1 yg_in2 yg_in3 experts_done ysum final_ready out_stored".split())
        w_loaded = [sem(f"w_loaded{i}") for i in range(5)]
        slot_done = [sem(f"slot_done{i}") for i in range(5)]

        def chain(eng, step, base):
            count = [0]

            def link(ins):
                ins.then_inc(step, 1)
                count[0] += 1
                eng.wait_ge(step, base + count[0])
            link.count = count
            return link

        def done(eng, ins, what, value):
            ins.then_inc(what, 1)
            eng.wait_ge(what, value)

        BASE_PAIR = [1, 1, 0, 0, 0]
        BASE_GROUP = [BASE_PAIR[i] + (PAIRS if i < 3 else 0) for i in range(5)]
        BASE_MERGE = [BASE_GROUP[i] + 2 * GROUPS for i in range(5)]
        MERGE_MATS = [("w_rwkv_o", 0, 0), ("w_in", 0, GATE_COL), ("w_in", 0, GATE_COL + D_MODEL),
                      ("w_mamba_o", 0, 0), ("w_mamba_o", KT, 0)]
        GROUP_COLS = [(XS_COL + m * P, 4 * P) for m in range(4)] + [(B_COL, P), (C_COL, P)] \
            + [(Z_COL + m * P, 4 * P) for m in range(4)]

        def wait_pair(eng, i, c):
            eng.wait_ge(slot_done[i], c + BASE_PAIR[i] + 1)

        def wait_group(eng, t, g):
            eng.wait_ge(slot_done[t % 5], g * 2 + BASE_GROUP[t % 5] + t // 5 + 1)

        def wait_merge(eng, s, j):
            eng.wait_ge(slot_done[s], j + BASE_MERGE[s] + 1)

        def low_rank_count(n, i):
            return i + 1 if isinstance(n, int) else n * 3 + i

        GRAM_BANKS = [7, 4, 5, 3]
        E_W1, E_W3, E_W2 = a["w_e1"][0], a["w_e3"][0], a["w_e2"][0]

        block = ctx.enter_context(nc.Block())

        @block.sync
        def _(sp):
            for t in range(TILES):
                sp.dma_start(x_tok[:, t, :], a["x"][0, t * P:(t + 1) * P, :]).then_inc(x_in, 16)

            def row(dst, src, n):
                sp.dma_start(dst[0:n, :], src.rearrange("(n m) -> n m", m=P)).then_inc(rows_in, 16)

            row(rows[0][0:24], a["mu_rwkv"][0, 0:3 * D_MODEL], 24)
            for i, name in enumerate(["w0", "a0", "k_k", "k_a"]):
                row(rows[0][24 + 8 * i:32 + 8 * i], a[name][0], 8)
            row(rows[0][56:64], a["r_k"][0].rearrange("h n -> (h n)"), 8)
            row(rows[0][64:72], a["lnx_g"][0], 8)
            row(rows[0][72:80], a["lnx_b"][0], 8)
            row(rows[0][80:88], a["norm1_g"][0], 8)
            row(rows[0][88:90], a["mu_rwkv"][0, 3 * D_MODEL:RWKV_COLS], 2)
            row(rows[1][0:96], a["conv_w"][0].rearrange("a b -> (a b)"), 96)
            row(rows[1][96:120], a["conv_b"][0], 24)
            row(rows[2][0:16], a["mnorm_g"][0], 16)
            sp.dma_start(dskip_in[0:16], a["d_skip"][0].rearrange("(a b) -> a b", b=2)).then_inc(rows_in, 16)
            sp.dma_start(dtp[0:MAMBA_HEADS, 0:1], a["dt_bias"].rearrange("a b -> b a")).then_inc(rows_in, 16)
            sp.dma_start(dtp[0:MAMBA_HEADS, 1:2], a["a_log"].rearrange("a b -> b a")).then_inc(rows_in, 16)
            sp.dma_start(ring[0], w_cols(w_in, 0, 3 * D_MODEL)).then_inc(w_loaded[0], 16)
            sp.dma_start(ring[1], w_cols(w_in, 0, 3 * D_MODEL + P)).then_inc(w_loaded[1], 16)
            sp.dma_start(dt_w, w_in[:, DT_COL:DT_COL + MAMBA_HEADS].rearrange("(k p) m -> p k m", p=P)
                         ).then_inc(dtw_in, 16)
            sp.dma_start(lw_g, a["w_gate2"][0]).then_inc(lora_in, 16)
            sp.dma_start(lw_w[0:DECAY_LORA], a["w_decay2"][0]).then_inc(lora_in, 16)
            sp.dma_start(lw_a[DECAY_LORA:P], a["w_iclr2"][0]).then_inc(lora_in, 16)
            for s in range(3):
                if s < 2:
                    sp.wait_ge(slot_done[s], BASE_PAIR[s])
                sp.dma_start(ring[s], w_cols(w_in, 0, s * D_MODEL)).then_inc(w_loaded[s], 16)
            def load_pair(c):
                for s in range(3):
                    sp.wait_ge(slot_done[s], c + BASE_PAIR[s])
                    sp.dma_start(ring[s], w_cols(w_in, 0, c * P + s * D_MODEL)).then_inc(w_loaded[s], 16)

            sp.wait_ge(zeros_ready, 1)
            with sp.Fori(1, 1 + ZERO_PAIRS) as c:
                load_pair(c)
                for n in range(ZERO_TILES):
                    row0 = (c - 1) * ZERO_TILES * P + n * P
                    sp.dma_start(xs_d[bass.ds(row0, P), :], zero_tile).then_inc(xs_zeroed, 16)
            with sp.Fori(1 + ZERO_PAIRS, PAIRS) as c:
                load_pair(c)

            def load_group(g, first):
                for t in range(10):
                    s = t % 5
                    if not first or t >= 5 or s < 3:
                        sp.wait_ge(slot_done[s], g * 2 + BASE_GROUP[s] + t // 5)
                    col, step = GROUP_COLS[t]
                    sp.dma_start(ring[s], w_cols(w_in, 0, g * step + col)).then_inc(w_loaded[s], 16)
                    if t == 3:
                        if first:
                            sp.wait_ge(acs_stored, 16)
                            sp.wait_ge(dve_pair, PAIRS)
                        else:
                            sp.wait_ge(m_exp, g * TILES)
                        sp.dma_start(acs_bc, acs_d[bass.ds(g * HEADS_PER_GROUP, HEADS_PER_GROUP), :].unsqueeze(0)
                                     .broadcast_to([P, HEADS_PER_GROUP, SEQ])).then_inc(acs_bc_in, 16)

            load_group(0, True)
            with sp.Fori(1, GROUPS) as g:
                load_group(g, False)
            def load_merge(j):
                for s, (name, kt0, col) in enumerate(MERGE_MATS):
                    sp.wait_ge(slot_done[s], j + BASE_MERGE[s])
                    sp.dma_start(ring[s], w_cols(a[name][0], kt0, j * P + col)).then_inc(w_loaded[s], 16)

            load_merge(0)
            sp.wait_ge(dve_group, GROUPS)
            sp.wait_ge(act_group, GROUPS)
            sp.wait_ge(yg_ready, GROUPS * TILES)
            sp.wait_ge(gn_mm, GROUPS)
            with sp.Fori(1, KT) as j:
                load_merge(j)
            for h in range(2):
                sp.dma_start(w_out_sb[:, :, h * 512:(h + 1) * 512],
                             a["w_out"][0][:, h * 512:(h + 1) * 512].rearrange("(k p) m -> p k m", p=P)
                             ).then_inc(w_out_in, 16)
            W1_IN, W3_IN, W2_IN = [w1_in0, w1_in1], [w3_in0, w3_in1], [w2_in0, w2_in1]

            def load_w13(e, u):
                sp.dma_start(w1_sb[u], E_W1[bass.ds(e, 1)].rearrange("o (p k) n -> p (o k) n", k=KT)).then_inc(W1_IN[u], 16)
                sp.dma_start(w3_sb[u], E_W3[bass.ds(e, 1)].rearrange("o (p k) n -> p (o k) n", k=KT)).then_inc(W3_IN[u], 16)

            def load_w2(e, u):
                sp.dma_start(w2_sb[u], E_W2[bass.ds(e, 1)].rearrange("o (p k) n -> p (o k) n", k=FT)).then_inc(W2_IN[u], 16)

            load_w13(0, 0)
            for s in range(5):
                wait_merge(sp, s, KT - 1)
            for t in range(TILES):
                sp.dma_start(x1_tok[:, t, :], a["x"][0, t * P:(t + 1) * P, :]).then_inc(x_in, 16)
            sp.dma_start(g2_bc, a["norm2_g"].broadcast_to([P, D_MODEL])).then_inc(router_in, 16)
            sp.dma_start(gf_bc, a["final_g"].unsqueeze(0).broadcast_to([P, D_MODEL])).then_inc(router_in, 16)
            sp.dma_start(wr_sb[:, :, 0:4], a["w_rg"][0].rearrange("(k p) m -> p k m", p=P)).then_inc(router_in, 16)
            sp.dma_start(wr_sb[:, :, 4:36], a["w_re"][0].rearrange("(k p) m -> p k m", p=P)).then_inc(router_in, 16)
            sp.dma_start(br_bc[:, 0:4], a["b_rg"].broadcast_to([P, 4])).then_inc(router_in, 16)
            sp.dma_start(br_bc[:, 4:36], a["b_re"].broadcast_to([P, 32])).then_inc(router_in, 16)

            sp.wait_ge(merged_ready, KT)
            load_w2(0, 0)
            sp.wait_ge(out_mm, 8)
            load_w13(1, 1)
            load_w2(1, 1)
            sp.wait_ge(items_out, 1)
            last_pair = sp.value_load(item_i[0:1, MAX_BLOCKS:MAX_BLOCKS + 1], min_val=N_EXPERTS // 2 - 1, max_val=MAX_BLOCKS // 2 - 1)
            with sp.Fori(1, last_pair + 1) as i:
                for u in range(2):
                    w = i * 2 + u
                    e = sp.value_load(item_i[0:1, bass.ds(w, 1)], min_val=0, max_val=N_EXPERTS - 1)
                    sp.wait_ge(h13_mm, w - 1)
                    load_w13(e, u)
                    sp.wait_ge(y2_mm, w - 1)
                    load_w2(e, u)
            for t in range(TILES):
                sp.wait_ge(final_ready, t + 1)
                sp.dma_start(out[0, t * P:(t + 1) * P, :], x1_tok[:, t, :]).then_inc(out_stored, 16)
            sp.wait_ge(out_stored, 16 * TILES)

        @block.gpsimd
        def _(pool):
            link = chain(pool, pool_step, 0)
            nc.gpsimd.memset(zero_tile, 0.0).then_inc(zeros_ready, 1)
            nc.gpsimd.iota(idx_i[:, 0:P], pattern=[[1, P]], base=0, channel_multiplier=0).then_inc(idx_ready, 1)
            nc.gpsimd.iota(idx_i[:, P:P + 1], pattern=[[0, 1]], base=0, channel_multiplier=1).then_inc(idx_ready, 1)
            pool.wait_ge(idx_ready, 2)
            nc.gpsimd.memset(st[0], 0.0).then_inc(s_zero, 1)
            nc.gpsimd.memset(st[1], 0.0).then_inc(s_zero, 1)
            pool.wait_ge(s_zero, 2)
            link(nc.gpsimd.memset(lw_w[DECAY_LORA:P], 0.0))
            link(nc.gpsimd.memset(lw_a[0:DECAY_LORA], 0.0))

            def low_rank_columns(i, n):
                nc.gpsimd.tensor_copy(lora_c[i], [lw_w, lw_a, lw_g][i][:, bass.ds(n * P, P)]).then_inc(lorac_ready, 1)

            def products(n):
                pool.wait_ge(terms, n * 6 + 1)
                nc.gpsimd.tensor_tensor(rk, rkv[0], k2, ALU.mult).then_inc(kb_rk, 1)
                pool.wait_ge(terms, n * 6 + 2)
                nc.gpsimd.tensor_tensor(kb, kkr, iclr, ALU.mult).then_inc(kb_rk, 1)

            def pair(c, more):
                pool.wait_ge(terms, c * 6 + 4)
                for f, src in enumerate([a_t, r_t]):
                    for h in range(2):
                        own = head_ones[:, h * RWKV_HEAD:h * RWKV_HEAD + 1]
                        nc.gpsimd.tensor_tensor(ar[:, :, 2 * f + h, :], src.rearrange("p (j t) -> p j t", j=TILES),
                                                own.unsqueeze(2).broadcast_to([P, TILES, P]), ALU.mult).then_inc(ar_ready, 1)
                if more:
                    low_rank_columns(0, c + 1)
                    low_rank_columns(1, c + 1)
                pool.wait_ge(ginit_ready, c + 1)
                m4 = gb[:, :, 0:2, :]
                for lv in range(1, LEVELS + 1):
                    if lv >= 3:
                        pool.wait_ge(xt_mm, c * 12 + 2 * (lv - 2))
                    nc.gpsimd.tensor_tensor(bm[lv % 2], m4, lev8[lv], ALU.mult).then_inc(bm_ready, 1)
                    if lv == 2:
                        low_rank_columns(2, c)
                if more:
                    products(c + 1)

            pool.wait_ge(dt_tok_ready, 1)
            pool.wait_ge(acs_stored, 16)
            pool.wait_ge(lora_in, 48)
            pool.wait_ge(pool_step, 2)
            low_rank_columns(0, 0)
            low_rank_columns(1, 0)
            products(0)
            with pool.Fori(0, PAIRS - 1) as c:
                pair(c, True)
            pair(PAIRS - 1, False)

            def group(g):
                for j in range(TILES):
                    if j > 0:
                        if j == 1:
                            pool.wait_ge(e_bc_ready, g + 1)
                            pool.wait_ge(xbc_ready, g * 6 + 6)
                        if j == 3:
                            pool.wait_ge(ym_mm, g * 4 + 2)
                        nc.gpsimd.tensor_tensor(
                            c_sb[j % 2], e_bc[:, :, j * P:(j + 1) * P],
                            xbcT[:, 5, j * P:(j + 1) * P].unsqueeze(1).broadcast_to([P, 8, P]), ALU.mult
                        ).then_inc(c_ready, 1)
                for j in range(TILES):
                    if j == 0:
                        pool.wait_ge(z_ready, g * 4 + 4)
                    pool.wait_ge(yskip_ready, g * 4 + j + 1)
                    nc.gpsimd.tensor_tensor(y_g[:, :, j * P:(j + 1) * P],
                                            y_m4[j % 2], zs[:, :, j * P:(j + 1) * P], ALU.mult
                                            ).then_inc(yg_ready, 1)

            y_m4 = [y_m.rearrange("p (m t) -> p m t", m=4), y_m_b.rearrange("p (m t) -> p m t", m=4)]
            with pool.Fori(0, GROUPS) as g:
                group(g)

            pool.wait_ge(xs_zeroed, 16 * (XS_ROWS // P))
            pool.wait_ge(rows_out, 2)
            pool.wait_ge(h2_ready, TILES)
            for k in range(2):
                for t in range(TILES):
                    nc.gpsimd.indirect_dma_start(
                        out=xs_d, out_offset=bass.IndirectOffsetOnAxis(ap=r_i[:, k * TILES + t:k * TILES + t + 1], axis=0),
                        in_=h2_tok[:, t, :], in_offset=None).then_inc(scattered, 16)
            pool.wait_ge(scattered, 16 * 2 * TILES)
            pool.wait_ge(items_out, 1)
            pool.wait_ge(h2T_ready, 2 * TILES)
            pool.wait_ge(logit_mm, TILES)
            last_pair = pool.value_load(item_i[0:1, MAX_BLOCKS:MAX_BLOCKS + 1], min_val=N_EXPERTS // 2 - 1, max_val=MAX_BLOCKS // 2 - 1)
            XB_IN, YST = [xb_in0, xb_in1], [yst0, yst1]
            pool.dma_start(xs_sb[0], xs_d[0:BLOCK, :]).then_inc(XB_IN[0], 16)
            pool.dma_start(xs_sb[1], xs_d[BLOCK:2 * BLOCK, :]).then_inc(XB_IN[1], 16)
            pool.wait_ge(xg_tr, 1)
            pool.dma_start(xs_sb[0], xs_d[2 * BLOCK:3 * BLOCK, :]).then_inc(XB_IN[0], 16)

            def expert_pair(i, final):
                for u in range(2):
                    w = i * 2 + u
                    if not (final and u == 1):
                        pool.wait_ge(xg_tr, w + 2)
                        pool.dma_start(xs_sb[1 - u], xs_d[bass.ds((w + 3) * BLOCK, BLOCK), :]).then_inc(XB_IN[1 - u], 16)
                    pool.wait_ge(ycopy_a, w + 1)
                    pool.wait_ge(ycopy_b, w + 1)
                    pool.dma_start(xs_d[bass.ds(w * BLOCK, BLOCK), :], y_out[u]).then_inc(YST[u], 16)

            with pool.Fori(0, last_pair) as i:
                expert_pair(i, False)
            expert_pair(last_pair, True)
            pool.wait_ge(experts_done, 1)
            YG = [yg_in0, yg_in1, yg_in2, yg_in3]
            for t in range(TILES):
                for k in range(2):
                    if t >= 2:
                        pool.wait_ge(ysum, 2 * (t - 2) + k + 1)
                    nc.gpsimd.indirect_dma_start(
                        out=y_rows[2 * t + k], out_offset=None, in_=xs_d,
                        in_offset=bass.IndirectOffsetOnAxis(ap=r_i[:, k * TILES + t:k * TILES + t + 1], axis=0)
                    ).then_inc(YG[t % 2 * 2 + k], 16)
            for n in range(4):
                pool.wait_ge(YG[n], 16 * TILES // 2)

        @block.scalar
        def _(act):
            for t in range(TILES):
                act.wait_ge(x_in, 16 * TILES)
                if t > 0:
                    act.wait_ge(sumsq_ready, t)
                nc.scalar.activation(sq_scr, x_tok[:, t, :], ACT.Square, accum_out=s_small[:, t:t + 1]).then_inc(sumsq_ready, 1)
            act.wait_ge(ms_ready, 1)
            nc.scalar.activation(s_small[:, 4:8], s_small[:, 4:8], ACT.Sqrt).then_inc(rms_ready, 1)
            act.wait_ge(rstd_ready, 1)
            for t in range(TILES):
                nc.scalar.activation(xn_tok[:, t, :], x_tok[:, t, :], ACT.Copy, scale=s_small[:, 8 + t:9 + t]).then_inc(xn_ready, 1)

            act.wait_ge(prm_ready, 1)
            for i, dst in enumerate([lo_wa, lo_g]):
                act.wait_ge(slot_done[i], 1)
                nc.scalar.activation(dst, bk[i], ACT.Copy, scale=lora_mu[:, 2 + i:3 + i]).then_inc(lo_scaled, 1)
            act.wait_ge(lo_shifted, 1)
            nc.scalar.activation(lo_wa[0:DECAY_LORA], lo_wa[0:DECAY_LORA], ACT.Tanh).then_inc(lo_ready, 1)
            act.wait_ge(lo_shifted, 2)
            nc.scalar.activation(lo_g, lo_g, ACT.Sigmoid).then_inc(lo_ready, 1)

            act.wait_ge(dt_dve, 1)
            done(act, nc.scalar.activation(dtw[1], dtw[0], ACT.Abs), dt_act, 1)
            done(act, nc.scalar.activation(dtw[2], dtw[1], ACT.Exp, scale=-1.0), dt_act, 2)
            act.wait_ge(rows_in, 16 * 16)
            nc.scalar.activation(dtp[0:MAMBA_HEADS, 2:3], dtp[0:MAMBA_HEADS, 1:2], ACT.Exp).then_inc(dt_act, 1)
            act.wait_ge(dt_dve, 2)
            nc.scalar.activation(dtw[4], dtw[3], ACT.Ln).then_inc(dt_act, 1)

            act.wait_ge(dt_dve, 3)
            act.dma_start(acs_d, dtw[1]).then_inc(acs_stored, 16)

            def scale(i, n):
                wait_pair(act, i, n)
                nc.scalar.activation(rkv[i], bk[i], ACT.Copy, scale=prm[:, 10 + i:11 + i]).then_inc(rkv_scaled, 1)

            def scale_rk(n):
                act.wait_ge(pair_prm_ready, n * 2 + 1)
                scale(0, n)
                scale(1, n)

            def decay_gate(n):
                act.wait_ge(lora_mm, low_rank_count(n, 0))
                nc.scalar.activation(sigw, bk[7], ACT.Sigmoid, bias=prm[:, 3:4]).then_inc(lora_read, 1)

            def rate_and_squares(n):
                act.wait_ge(lora_mm, low_rank_count(n, 1))
                nc.scalar.activation(iclr, bk[0], ACT.Sigmoid, bias=prm[:, 4:5]).then_inc(lora_read, 1)
                act.wait_ge(shifted, n * 3 + 2)
                nc.scalar.activation(ksq, rkv[1], ACT.Square, scale=prm[:, 5:6]).then_inc(ksq_ready, 1)
                nc.scalar.activation(kkr, rkv[1], ACT.Copy, scale=prm[:, 5:6]).then_inc(ksq_ready, 1)
                act.wait_ge(lora_read, low_rank_count(n, 1))
                nc.scalar.activation(kscale, iclr, ACT.Identity, scale=prm[:, 6:7], bias=prm[:, 13:14]).then_inc(kscale_ready, 1)

            def norms(n):
                act.wait_ge(norm_mm, n + 1)
                nc.scalar.activation(rnorm, bk[7], ACT.Sqrt).then_inc(nrm_ready, 1)

            def decays(n):
                act.wait_ge(centered, n + 1)
                nc.scalar.activation(e_a, cp, ACT.Exp, scale=-KAPPA).then_inc(exps_ready, 1)
                nc.scalar.activation(e_b, cc, ACT.Exp, scale=KAPPA).then_inc(exps_ready, 1)
                nc.scalar.activation(e_r, cc, ACT.Exp, scale=-KAPPA).then_inc(exps_ready, 1)
                nc.scalar.activation(s_small[:, 16:20], ccum[:, RWKV_HEAD - 1::P], ACT.Exp, scale=-KAPPA).then_inc(exps_ready, 1)

            def pair(c, more):
                scale(2, c)
                for i, (dst, b) in enumerate([(b_tok, 5), (k_tok, 3), (v_tok, 4)]):
                    act.wait_ge(tok_tr, c * 3 + i + 1)
                    nc.scalar.activation(dst, bk[b], ACT.Copy).then_inc(tok_ready, 1)
                if more:
                    scale_rk(c + 1)
                for lv in range(1, LEVELS + 1):
                    for q in range(2):
                        act.wait_ge(xt_mm, c * 12 + 2 * (lv - 1) + q + 1)
                        nc.scalar.activation(xt[:, q * 512:(q + 1) * 512], bk[3 + q], ACT.Copy).then_inc(xt_ready, 1)
                    if more and lv <= 4:
                        [decay_gate, rate_and_squares, norms, decays][lv - 1](c + 1)
                act.wait_ge(f_ready, c + 1)
                for j in range(1, TILES - 1):
                    act.wait_ge(s_ready, c * 6 + 2 * j)
                    nc.scalar.activation(fs, st[j % 2], ACT.Copy, scale=s_small[:, 20 + j:21 + j]).then_inc(fs_ready, 1)
                act.wait_ge(head_norm, c * 3 + 1)
                nc.scalar.activation(y_sq, y_c, ACT.Square).then_inc(head_act, 1)
                act.wait_ge(head_norm, c * 3 + 2)
                nc.scalar.activation(s_small[:, 40:48], s_small[:, 40:48], ACT.Sqrt).then_inc(head_act, 1)
                act.wait_ge(lora_mm, c * 3 + (5 if more else 3))
                nc.scalar.activation(gate, bk[3], ACT.Copy).then_inc(lora_read, 1)
                act.wait_ge(pe_pair, c + 1)
                nc.scalar.activation(y_3, bk[7], ACT.Identity, scale=s_small[:, 50:51], bias=s_small[:, 51:52]).then_inc(act_pair, 1)

            act.wait_ge(lo_ready, 2)
            act.wait_ge(dt_tok_ready, 1)
            act.wait_ge(acs_stored, 16)
            for step in [scale_rk, decay_gate, rate_and_squares, norms, decays]:
                step(0)
            with act.Fori(0, PAIRS - 1) as c:
                pair(c, True)
            pair(PAIRS - 1, False)
            act.wait_ge(dve_pair, PAIRS)

            def group(g):
                act.wait_ge(cprm_ready, g + 1)
                for t in range(6):
                    wait_group(act, t, g)
                    nc.scalar.activation(xbcT[:, t, :], bk[t % 4], ACT.Identity, scale=cprm[:, 5 * t + 3:5 * t + 4],
                                         bias=cprm[:, 5 * t + 4:5 * t + 5]).then_inc(taps_act, 1)
                    if t > 0:
                        act.wait_ge(taps_done, g * 6 + t)
                        nc.scalar.activation(xbcT[:, t - 1, :], xbcT[:, t - 1, :], ACT.Silu).then_inc(xbc_ready, 1)
                act.wait_ge(taps_done, g * 6 + 6)
                nc.scalar.activation(xbcT[:, 5, :], xbcT[:, 5, :], ACT.Silu).then_inc(xbc_ready, 1)
                act.wait_ge(acs_bc_in, g * 16 + 16)
                nc.scalar.activation(e_bc, acs_bc, ACT.Exp).then_inc(e_bc_ready, 1)
                def z_gate(m):
                    wait_group(act, 6 + m, g)
                    nc.scalar.activation(zs[:, m, :], bk[(6 + m) % 4], ACT.Silu).then_inc(z_ready, 1)

                for m in range(3):
                    if m == 2:
                        act.wait_ge(bt_tr, g + 1)
                        nc.scalar.activation(b_tk, bk[6], ACT.Copy).then_inc(bt_tok_ready, 1)
                    z_gate(m)
                for j in range(TILES):
                    act.wait_ge(te_in, g * 4 + j + 1)
                    nc.scalar.activation(te[j % 2], te[j % 2], ACT.Exp).then_inc(te_ready, 1)
                    act.wait_ge(d_ready, g * 4 + j + 1)
                    nc.scalar.activation(m_sb[j % 2], m_sb[j % 2], ACT.Exp).then_inc(m_exp, 1)
                    if j == 1:
                        z_gate(3)
                act.wait_ge(yg_ready, g * 4 + 4)
                act.wait_ge(dve_done_e, g + 1)
                nc.scalar.activation(ysq2, y_g.rearrange("p m t -> p (m t)"), ACT.Square).then_inc(ysq_ready, 1)
                act.wait_ge(gn_ready, g + 1)
                nc.scalar.activation(rstd2, rstd2, ACT.Sqrt).then_inc(act_group, 1)

            with act.Fori(0, GROUPS) as g:
                group(g)

            act.wait_ge(dve_group, GROUPS)

            def gates(jj, first):
                for u in range(2):
                    if not first:
                        act.wait_ge(merged_ready, jj * 2 + u - 1)
                    for i, dst in enumerate([sg_a[u], sg_b[u]]):
                        wait_merge(act, 1 + i, jj * 2 + u)
                        nc.scalar.activation(dst, bk[4 * u + 1 + i], ACT.Sigmoid).then_inc(sig_ready, 1)

            gates(0, True)
            with act.Fori(1, KT // 2) as jj:
                gates(jj, False)

            def copy_h2T(t):
                for h in range(2):
                    act.wait_ge(norm_tr, 2 * TILES + 2 * t + h + 1)
                    nc.scalar.activation(h2T[:, 4 * h:4 * h + 4, t * P:(t + 1) * P],
                                         bk[6 + h].rearrange("p (k t) -> p k t", k=4), ACT.Copy).then_inc(h2T_ready, 1)

            for t in range(TILES):
                act.wait_ge(x1_done, 2 * t + 2)
                if t > 0:
                    act.wait_ge(sumsq_ready, TILES + t)
                nc.scalar.activation(sq_row, x1_tok[:, t, :], ACT.Square, accum_out=sm[0][:, t:t + 1]).then_inc(sumsq_ready, 1)
                act.wait_ge(ms_ready, t + 2)
                nc.scalar.activation(sm[1][:, t:t + 1], sm[1][:, t:t + 1], ACT.Sqrt).then_inc(rms_ready, 1)
                if t > 0:
                    copy_h2T(t - 1)
            copy_h2T(TILES - 1)
            act.wait_ge(r_exp_in, 1)
            nc.scalar.activation(gs[1], gs[1], ACT.Exp).then_inc(r_exp, 1)
            act.wait_ge(r_exp_in, 2)
            nc.scalar.activation(sm[5], sm[5], ACT.Exp).then_inc(r_exp, 1)

            act.wait_ge(items_out, 1)
            act.wait_ge(scattered, 16 * 2 * TILES)
            last_pair = act.value_load(item_i[0:1, MAX_BLOCKS:MAX_BLOCKS + 1], min_val=N_EXPERTS // 2 - 1, max_val=MAX_BLOCKS // 2 - 1)
            YST = [yst0, yst1]

            def copy_rows(w):
                act.wait_ge(xg_tr, w + 1)
                nc.scalar.activation(xgT, bk[6].rearrange("p (k s) -> p k s", k=KT), ACT.Copy).then_inc(xg_ready, 1)

            def expert_pair(i, first, final):
                for u in range(2):
                    w = i * 2 + u
                    act.wait_ge(h13_mm, w + 1)
                    nc.scalar.activation(silu_hi, bk[2 * u][0:BLOCK, :], ACT.Silu).then_inc(silu_ready, 1)
                    if not (final and u == 1):
                        copy_rows(w + 1)
                    act.wait_ge(hid_tr, w + 1)
                    nc.scalar.activation(hidT, bk[7][:, 0:FT * BLOCK].rearrange("p (k s) -> p k s", k=FT), ACT.Copy).then_inc(hidT_ready, 1)
                    if not first:
                        act.wait_ge(YST[u], i * 16)
                    act.wait_ge(y2_mm, w + 1)
                    nc.scalar.activation(y_out[u][:, 0:512], bk[4][0:BLOCK, :], ACT.Copy).then_inc(ycopy_a, 1)

            copy_rows(0)
            expert_pair(0, True, False)
            with act.Fori(1, last_pair) as i:
                expert_pair(i, False, False)
            expert_pair(last_pair, False, True)
            for t in range(TILES):
                act.wait_ge(ysum, 2 * t + 2)
                done(act, nc.scalar.activation(sq_row, x1_tok[:, t, :], ACT.Square, accum_out=sm[0][:, t:t + 1]), sumsq_ready, 2 * TILES + t + 1)
                act.wait_ge(ms_ready, TILES + t + 2)
                nc.scalar.activation(sm[1][:, t:t + 1], sm[1][:, t:t + 1], ACT.Sqrt).then_inc(rms_ready, 1)

        @block.vector
        def _(dve):
            V = nc.vector
            link = chain(dve, dve_step, 0)
            link(V.memset(not_start, 1.0))
            link(V.memset(not_start[:, 0::P], 0.0))
            dve.wait_ge(idx_ready, 2)
            link(V.tensor_copy(col_f, idx_i[:, P:P + 1]))
            link(V.tensor_copy(row_f, idx_i[:, 0:P]))
            link(V.tensor_scalar(eq_blocks[0], row_f, col_f, None, ALU.is_equal))
            link(V.tensor_copy(ident, eq_blocks[0]))
            dve.wait_ge(rows_in, 16 * 16)
            link(V.tensor_copy(rows[3][0:16].rearrange("p (b r) -> p b r", b=2),
                               dskip_in[0:16].unsqueeze(2).broadcast_to([16, 2, RWKV_HEAD])))
            V.memset(s_small[:, 62:63], 0.0).then_inc(masks_ready, 1)
            dve.wait_ge(sumsq_ready, TILES)
            V.tensor_scalar(s_small[:, 4:8], s_small[:, 0:4], 1.0 / D_MODEL, 1e-6, ALU.mult, ALU.add).then_inc(ms_ready, 1)
            dve.wait_ge(rms_ready, 1)
            V.reciprocal(s_small[:, 8:12], s_small[:, 4:8]).then_inc(rstd_ready, 1)
            dve.wait_ge(rows_tr, 4)
            link(V.tensor_copy(norm1_c, bk[7][:, 80:88]))
            for t in range(TILES):
                for h in range(2):
                    n = 2 * t + h
                    dve.wait_ge(norm_tr, n + 1)
                    V.tensor_tensor(hT[:, 4 * h:4 * h + 4, t * P:(t + 1) * P],
                                    bk[n % 4].rearrange("p (k t) -> p k t", k=4),
                                    norm1_c[:, 4 * h:4 * h + 4].unsqueeze(2).broadcast_to([P, 4, P]), ALU.mult
                                    ).then_inc(hT_ready, 1)
            for i in range(10):
                link(V.tensor_copy(pp3[:, :, i], bk[7][:, 8 * i:8 * i + 8]))
            link(V.tensor_copy(lora_mu[:, 0:2], bk[7][:, 88:90]))
            link(V.tensor_scalar(lora_mu[:, 2:4], lora_mu[:, 0:2], -1.0, 1.0, ALU.mult, ALU.add))
            link(V.tensor_scalar(pp3[:, :, 10:13], pp3[:, :, 0:3], -1.0, 1.0, ALU.mult, ALU.add))
            link(V.tensor_scalar(pp3[:, :, 13:14], pp3[:, :, 6:7], -1.0, 1.0, ALU.mult, ALU.add))
            for tap in range(5):
                o = P + tap * 24
                link(V.tensor_copy(cp4[:, :, 0:4, tap], bk[7][:, o:o + 16].rearrange("p (g s) -> p g s", g=GROUPS)))
                link(V.tensor_copy(cp4[:, :, 4, tap], bk[7][:, o + 16:o + 20]))
                link(V.tensor_copy(cp4[:, :, 5, tap], bk[7][:, o + 20:o + 24]))
            for n in range(2):
                link(V.tensor_copy(op3[:, :, 4 * n:4 * n + 4],
                                   bk[7][:, 2 * P + 16 * n:2 * P + 16 * n + 16].rearrange("p (g s) -> p g s", g=GROUPS)))
            V.memset(s_small[:, 63:64], 0.0).then_inc(prm_ready, 1)
            link(V.tensor_scalar(tri2[:, 0:P], row_f, col_f, None, ALU.is_gt))
            link(V.tensor_scalar(tri2[:, P:2 * P], row_f, col_f, None, ALU.is_ge))
            link(V.tensor_scalar(neg_tri, tri2[:, P:2 * P], -1.0, BIG, ALU.add, ALU.mult))
            sh = idx_i[:, P + 1:2 * (P + 1)]
            for n in range(1, LEVELS + 2):
                link(V.tensor_scalar(sh, idx_i[:, 0:P + 1], n, None, ALU.logical_shift_right))
                link(V.tensor_copy(row_sh, sh[:, 0:P]))
                link(V.tensor_copy(col_sh, sh[:, P:P + 1]))
                link(V.tensor_scalar(eq_blocks[n], row_sh, col_sh, None, ALU.is_equal))
            link(V.tensor_copy(head_ones, eq_blocks[6]))
            link(V.tensor_copy(ones, eq_blocks[7]))
            for n in range(LEVELS + 1):
                link(V.tensor_tensor(eq_tmp, eq_blocks[n + 1], eq_blocks[n], ALU.subtract))
                link(V.tensor_tensor(level_mask[n], eq_tmp, tri2[:, 0:P], ALU.mult))
            for i, dst in enumerate([lo_wa, lo_g]):
                dve.wait_ge(lo_scaled, i + 1)
                V.scalar_tensor_tensor(dst[:, 1:SEQ], bk[i][:, 0:SEQ - 1], lora_mu[:, i:i + 1], dst[:, 1:SEQ],
                                       ALU.mult, ALU.add).then_inc(lo_shifted, 1)
            dve.wait_ge(dt_proj, 1)
            dve.wait_ge(rows_in, 16 * 16)
            V.tensor_scalar(dtw[0], bk[2][0:MAMBA_HEADS, :], dtp[0:MAMBA_HEADS, 0:1], None, ALU.add).then_inc(dt_dve, 1)
            dve.wait_ge(dt_act, 2)
            V.tensor_scalar(dtw[3], dtw[2], 1.0, None, ALU.add).then_inc(dt_dve, 1)
            dve.wait_ge(dt_dve, 2)
            link(V.tensor_scalar(dtw[5], dtw[3], -1.0, None, ALU.add))
            link(V.tensor_scalar(dtw[6], dtw[5], 0.0, None, ALU.is_equal))
            link(V.tensor_tensor(dtw[5], dtw[5], dtw[6], ALU.add))
            link(V.reciprocal(dtw[5], dtw[5]))
            dve.wait_ge(dt_act, 4)
            link(V.tensor_tensor(dtw[4], dtw[4], dtw[6], ALU.add))
            link(V.tensor_tensor(dtw[4], dtw[4], dtw[5], ALU.mult))
            link(V.tensor_tensor(dtw[4], dtw[4], dtw[2], ALU.mult))
            link(V.scalar_tensor_tensor(dtw[4], dtw[0], 0.0, dtw[4], ALU.max, ALU.add))
            link(V.tensor_scalar(dtp[0:MAMBA_HEADS, 3:4], dtp[0:MAMBA_HEADS, 2:3], -1.0, None, ALU.mult))
            link(V.tensor_scalar(dtw[7], dtw[4], dtp[0:MAMBA_HEADS, 3:4], None, ALU.mult))
            V.tensor_tensor_scan(dtw[1], not_start[0:MAMBA_HEADS], dtw[7], 0.0, ALU.mult, ALU.add).then_inc(dt_dve, 1)
            dve.wait_ge(dt_tr, 1)
            link(V.tensor_copy(dt_tok, bk[3][:, 0:P]))
            V.tensor_copy(acs_tok, bk[3][:, P:2 * P]).then_inc(dt_tok_ready, 1)
            dve.wait_ge(dt_tok_ready, 1)

            GROUP_STEPS, MERGE_STEPS = 21, 4

            def parameters(n, link):
                done(dve, V.tensor_copy(prm, pair_prm[:, bass.ds(n * 14, 14)]), pair_prm_ready, n * 2 + 1)
                V.tensor_scalar(r_ones, head_ones, prm[:, 7:8], None, ALU.mult).then_inc(pair_prm_ready, 1)

            def shift(i, n):
                dve.wait_ge(rkv_scaled, n * 3 + i + 1)
                V.scalar_tensor_tensor(rkv[i][:, 1:SEQ], bk[i][:, 0:SEQ - 1], prm[:, i:i + 1], rkv[i][:, 1:SEQ],
                                       ALU.mult, ALU.add).then_inc(shifted, 1)

            def shift_rk(n, link):
                shift(0, n)
                shift(1, n)

            def exponents(n, link):
                dve.wait_ge(lora_read, low_rank_count(n, 0))
                link(V.tensor_tensor_scan(ccum, not_start, sigw, 0.0, ALU.mult, ALU.add))
                link(V.tensor_tensor(cc.rearrange("p (j t) -> p j t", j=TILES), ccum.rearrange("p (j t) -> p j t", j=TILES),
                                     ccum[:, RWKV_HEAD - 1::P].unsqueeze(2).broadcast_to([P, TILES, P]), ALU.subtract))
                V.tensor_tensor(cp, cc, sigw, ALU.subtract).then_inc(centered, 1)

            def scaled_k(n, link):
                dve.wait_ge(kscale_ready, n + 1)
                V.tensor_tensor(k2, rkv[1], kscale, ALU.mult).then_inc(terms, 1)

            def inverse_norm(n, link):
                dve.wait_ge(nrm_ready, n + 1)
                link(V.tensor_scalar(rnorm, rnorm, 1e-12, None, ALU.max))
                V.reciprocal(rnorm[:, 0:SEQ // 2], rnorm[:, 0:SEQ // 2])

            def unit_kk(n, link):
                link(V.reciprocal(rnorm[:, SEQ // 2:SEQ], rnorm[:, SEQ // 2:SEQ]))
                done(dve, V.tensor_tensor(kkr, kkr, rnorm, ALU.mult), terms, n * 6 + 2)

            def decayed_ar(n):
                dve.wait_ge(exps_ready, n * 4 + 1)
                V.scalar_tensor_tensor(a_t, kkr, -1.0, e_a, ALU.mult, ALU.mult).then_inc(terms, 1)
                dve.wait_ge(exps_ready, n * 4 + 3)
                V.tensor_tensor(r_t, rkv[0], e_r, ALU.mult).then_inc(terms, 1)

            def decayed_bk(n):
                dve.wait_ge(kb_rk, n * 2 + 2)
                V.tensor_tensor(b_t, kb, e_b, ALU.mult).then_inc(terms, 1)
                V.tensor_tensor(k_t, k2, e_b, ALU.mult).then_inc(terms, 1)

            def pair(c, base, more):
                link = chain(dve, dve_step, base)
                shift(2, c)
                link(V.tensor_copy(s_small[:, 50:52], prm[:, 8:10]))
                dve.wait_ge(bonus_mm, c + 1)
                if more:
                    parameters(c + 1, link)
                dve.wait_ge(exps_ready, c * 4 + 4)
                V.tensor_tensor(s_small[:, 20:23], e_r[:, P - 1:3 * P:P], s_small[:, 17:20], ALU.mult).then_inc(f_ready, 1)
                dve.wait_ge(shifted, c * 3 + 3)
                V.tensor_tensor(bonus, bk[6], rkv[2], ALU.mult).then_inc(bonus_ready, 1)
                t4 = tri2.rearrange("p (k t) -> p k t", k=2).unsqueeze(2).broadcast_to([P, 2, 2, P])
                for n in range(8):
                    j, of_k = n // 2, n % 2
                    dst = (gk if of_k else gb)[:, j].rearrange("p (k h) t -> p k h t", k=2)
                    dve.wait_ge(gram_mm, c * 8 + n + 1)
                    V.tensor_tensor(dst, bk[GRAM_BANKS[n % 4]].rearrange("p (k h t) -> p k h t", k=2, h=2), t4, ALU.mult
                                    ).then_inc(gram_ready, 1)
                dve.wait_ge(gram_ready, c * 8 + 8)
                link(V.tensor_tensor(bm[0], gb[:, :, 0:2, :], lev8[0], ALU.mult))
                done(dve, V.tensor_tensor(gi4, bm[0], ident8, ALU.add), ginit_ready, c + 1)

                def copy_h(lv):
                    for q in range(2):
                        dve.wait_ge(h_tr, c * 12 + 2 * lv + q + 1)
                        V.tensor_copy(hi[:, q * 512:(q + 1) * 512], bk[3 + q]).then_inc(h_ready, 1)

                copy_h(0)
                if more:
                    shift_rk(c + 1, link)
                for lv in range(1, LEVELS + 1):
                    for q in range(2):
                        dve.wait_ge(g_mm, c * 12 + 2 * (lv - 1) + q + 1)
                        V.tensor_tensor(gi[:, q * 512:(q + 1) * 512], gi[:, q * 512:(q + 1) * 512], bk[5 + q], ALU.add
                                        ).then_inc(g_ready, 1)
                    if lv < LEVELS:
                        copy_h(lv)
                        if more and lv > 1:
                            [exponents, scaled_k, inverse_norm, unit_kk][lv - 2](c + 1, link)
                dve.wait_ge(f_ready, c + 1)
                dve.wait_ge(s_zero, 2)
                for j in range(TILES):
                    dve.wait_ge(x1_mm, c * 4 + j + 1)
                    V.tensor_copy(x1, bk[3][:, 0:P]).then_inc(x1_ready, 1)
                    dve.wait_ge(u_mm, c * 4 + j + 1)
                    V.tensor_copy(u_sb, bk[4][:, 0:P]).then_inc(u_ready, 1)
                    if j == TILES - 1:
                        break
                    dve.wait_ge(d_mm, c * 3 + j + 1)
                    if j > 0:
                        dve.wait_ge(fs_ready, c * 2 + j)
                        dve.wait_ge(y_mm, c * 4 + j)
                    for h in range(2):
                        q = slice(h * RWKV_HEAD, (h + 1) * RWKV_HEAD)
                        f = s_small[q, 20 + j:21 + j]
                        dst = st[(j + 1) % 2][q, q]
                        if j == 0:
                            ins = V.tensor_scalar(dst, bk[5][q, q], f, None, ALU.mult)
                        else:
                            ins = V.scalar_tensor_tensor(dst, bk[5][q, q], f, fs[q, q], ALU.mult, ALU.add)
                        ins.then_inc(s_ready, 1)
                y8 = bk[6].rearrange("p (n v) -> p n v", v=RWKV_HEAD)
                y8s = y_c.rearrange("p (n v) -> p n v", v=RWKV_HEAD)
                mean, var = s_small[:, 32:40], s_small[:, 40:48]
                dve.wait_ge(y_mm, c * 4 + 4)
                link(V.tensor_reduce(mean, y8, AX.X, ALU.add))
                link(V.tensor_scalar(mean, mean, 1.0 / RWKV_HEAD, None, ALU.mult))
                V.tensor_tensor(y8s, y8, mean.unsqueeze(2).broadcast_to([P, 8, RWKV_HEAD]), ALU.subtract).then_inc(head_norm, 1)
                if more:
                    decayed_ar(c + 1)
                dve.wait_ge(head_act, c * 2 + 1)
                link(V.tensor_reduce(var, y_sq.rearrange("p (n v) -> p n v", v=RWKV_HEAD), AX.X, ALU.add))
                V.tensor_scalar(var, var, 1.0 / RWKV_HEAD, 64e-5, ALU.mult, ALU.add).then_inc(head_norm, 1)
                if more:
                    decayed_bk(c + 1)
                dve.wait_ge(head_act, c * 2 + 2)
                link(V.reciprocal(var, var))
                done(dve, V.tensor_tensor(y8s, y8s, var.unsqueeze(2).broadcast_to([P, 8, RWKV_HEAD]), ALU.mult), head_norm, c * 3 + 3)
                dve.wait_ge(act_pair, c + 1)
                dve.wait_ge(bonus_ready, c + 1)
                link(V.tensor_tensor(y_3, y_3, bonus, ALU.add))
                V.tensor_tensor(ygT_t[:, bass.ds(c * SEQ, SEQ)], y_3, gate, ALU.mult).then_inc(dve_pair, 1)
                return link.count[0]

            dve.wait_ge(acs_stored, 16)
            for step in [parameters, shift_rk, exponents, scaled_k, inverse_norm, unit_kk]:
                step(0, link)
            decayed_ar(0)
            decayed_bk(0)
            steps = link.count[0]
            PAIR_STEPS = 11
            with dve.Fori(0, 1 + ZERO_PAIRS) as c:
                assert pair(c, c * PAIR_STEPS + steps, True) == PAIR_STEPS
            dve.wait_ge(xs_zeroed, 16 * (XS_ROWS // P))
            with dve.Fori(1 + ZERO_PAIRS, PAIRS - 1) as c:
                pair(c, c * PAIR_STEPS + steps, True)
            steps += (PAIRS - 1) * PAIR_STEPS
            steps += pair(PAIRS - 1, steps, False)

            def group(g, more):
                link = chain(dve, dve_step, g * GROUP_STEPS + steps)
                link(V.tensor_copy(oprm, out_prm[:, bass.ds(g * 8, 8)]))
                for t in range(6):
                    dve.wait_ge(taps_act, g * 6 + t + 1)
                    if t == 0:
                        dve.wait_ge(cprm_ready, g + 1)
                    for k in range(1, TAPS):
                        x = xbcT[:, t, k:SEQ]
                        ins = V.scalar_tensor_tensor(x, bk[t % 4][:, 0:SEQ - k], cprm[:, 5 * t + 3 - k:5 * t + 4 - k], x,
                                                     ALU.mult, ALU.add)
                        if k < TAPS - 1:
                            link(ins)
                        else:
                            ins.then_inc(taps_done, 1)
                for j in range(TILES):
                    dve.wait_ge(xt_tr, g * 4 + j + 1)
                    V.tensor_tensor(xdt[:, j, :].rearrange("p (h n) -> p h n", h=8), bk[4 + j % 2].rearrange("p (h n) -> p h n", h=8),
                                    dt_tok[:, bass.ds(g * 8 + j * MAMBA_HEADS, 8)].unsqueeze(2).broadcast_to([P, 8, RWKV_HEAD]),
                                    ALU.mult).then_inc(xdt_ready, 1)
                if more:
                    V.tensor_copy(cprm, conv_prm[:, bass.ds(g * 30 + 30, 30)]).then_inc(cprm_ready, 1)
                dve.wait_ge(acs_bc_in, g * 16 + 16)

                def decays(j):
                    tj = slice(j * P, (j + 1) * P)
                    at = acs_tok[:, bass.ds(g * 8 + j * MAMBA_HEADS, 8)]
                    if j >= 2:
                        dve.wait_ge(ym_mm, g * 4 + j - 1)
                    V.tensor_tensor(te[j % 2], acs_bc[:, :, j * P + P - 1], at, ALU.subtract).then_inc(te_in, 1)
                    link(V.tensor_tensor(m_sb[j % 2], acs_bc[:, :, tj], at.unsqueeze(2).broadcast_to([P, 8, P]), ALU.subtract))
                    V.tensor_tensor(m_sb[j % 2], m_sb[j % 2], neg_tri.unsqueeze(1).broadcast_to([P, 8, P]), ALU.add
                                    ).then_inc(d_ready, 1)
                    if j < TILES - 1:
                        dve.wait_ge(te_ready, g * 4 + j + 1)
                        dve.wait_ge(xdt_ready, g * 4 + j + 1)
                        if j == 2:
                            dve.wait_ge(st_mm, g * 3 + 1)
                        V.tensor_tensor(xe[j % 2].rearrange("p (h n) -> p h n", h=8), xdt[:, j, :].rearrange("p (h n) -> p h n", h=8),
                                        te[j % 2].unsqueeze(2).broadcast_to([P, 8, RWKV_HEAD]), ALU.mult).then_inc(xe_ready, 1)
                    dve.wait_ge(m_exp, g * 4 + j + 1)
                    dve.wait_ge(cb_mm, g * 4 + j + 1)
                    V.tensor_tensor(m_sb[j % 2], m_sb[j % 2], bk[6][:, 0:P].unsqueeze(1).broadcast_to([P, 8, P]), ALU.mult
                                    ).then_inc(m_ready, 1)

                def next_state(j):
                    dve.wait_ge(st_mm, g * 3 + j + 1)
                    if j == 0:
                        V.tensor_copy(state[1], bk[7]).then_inc(st_ready, 1)
                        return
                    if j == 1:
                        dve.wait_ge(e_bc_ready, g + 1)
                    dve.wait_ge(st_ready, g * 3 + j)
                    link(V.tensor_tensor(s_dec.rearrange("p (h n) -> p h n", h=8),
                                         state[j % 2].rearrange("p (h n) -> p h n", h=8),
                                         e_bc[:, :, j * P + P - 1].unsqueeze(2).broadcast_to([P, 8, RWKV_HEAD]), ALU.mult))
                    if j == 2:
                        dve.wait_ge(ym_mm, g * 4 + 2)
                    V.tensor_tensor(state[(j + 1) % 2], s_dec, bk[7], ALU.add).then_inc(st_ready, 1)

                def skip(j):
                    dve.wait_ge(ym_mm, g * 4 + j + 1)
                    if j == 0:
                        dve.wait_ge(xbc_ready, g * 6 + 4)
                    if j >= 2:
                        dve.wait_ge(yg_ready, g * 4 + j - 1)
                    ym = [y_m, y_m_b][j % 2]
                    for m in range(4):
                        ins = V.scalar_tensor_tensor(ym[:, m * P:(m + 1) * P], xbcT[:, m, j * P:(j + 1) * P], oprm[:, 4 + m:5 + m],
                                                     bk[4 + j % 2][:, m * P:(m + 1) * P], ALU.mult, ALU.add)
                    ins.then_inc(yskip_ready, 1)

                decays(0)
                next_state(0)
                for j in range(TILES - 1):
                    decays(j + 1)
                    if j < TILES - 2:
                        next_state(j + 1)
                    skip(j)
                skip(TILES - 1)
                V.memset(s_small[:, 59:60], 0.0).then_inc(dve_done_e, 1)
                dve.wait_ge(ysq_ready, g + 1)
                link(V.tensor_tensor(ysq2[:, 0:2 * SEQ], ysq2[:, 0:2 * SEQ], ysq2[:, 2 * SEQ:4 * SEQ], ALU.add))
                V.tensor_tensor(ysq2[:, 0:SEQ], ysq2[:, 0:SEQ], ysq2[:, SEQ:2 * SEQ], ALU.add).then_inc(ysq_summed, 1)
                dve.wait_ge(gn_mm, g + 1)
                V.tensor_scalar(rstd2, bk[6], 1.0 / 512, 1e-5, ALU.mult, ALU.add).then_inc(gn_ready, 1)
                dve.wait_ge(act_group, g + 1)
                link(V.reciprocal(rstd2, rstd2))
                for m in range(4):
                    ins = V.scalar_tensor_tensor(ymT_t[:, bass.ds(g * 4 * SEQ + m * SEQ, SEQ)], y_g[:, m, :], oprm[:, m:m + 1], rstd2,
                                                 ALU.mult, ALU.mult)
                ins.then_inc(dve_group, 1)
                assert link.count[0] == GROUP_STEPS

            V.tensor_copy(cprm, conv_prm[:, 0:30]).then_inc(cprm_ready, 1)
            with dve.Fori(0, GROUPS - 1) as g:
                group(g, True)
                dve.wait_ge(dve_group, g + 1)
            group(GROUPS - 1, False)

            with dve.Fori(0, KT // 2) as jj:
                link = chain(dve, dve_step, jj * MERGE_STEPS + steps + GROUPS * GROUP_STEPS)
                for u in range(2):
                    n = jj * 2 + u
                    dve.wait_ge(sig_ready, n * 2 + 2)
                    wait_merge(dve, 0, n)
                    wait_merge(dve, 4, n)
                    link(V.tensor_tensor(t_a[u], sg_a[u], bk[4 * u], ALU.mult))
                    link(V.tensor_tensor(t_b[u], sg_b[u], bk[4 * u + 3], ALU.mult))
                    V.tensor_tensor(arena[:, bass.ds(SLOT + 8192 + n * SEQ, SEQ)], t_a[u], t_b[u], ALU.add).then_inc(merged_ready, 1)
            lk = chain(dve, dve_step, steps + GROUPS * GROUP_STEPS + KT // 2 * MERGE_STEPS)
            dve.wait_ge(x_in, 2 * 16 * TILES)
            for t in range(TILES):
                for h in range(2):
                    n = 2 * t + h
                    dve.wait_ge(out_mm, n + 1)
                    x = x1_tok[:, t, h * 512:(h + 1) * 512]
                    V.tensor_tensor(x, x, bk[n % 4], ALU.add).then_inc(x1_done, 1)
                dve.wait_ge(sumsq_ready, TILES + t + 1)
                V.tensor_scalar(sm[1][:, t:t + 1], sm[0][:, t:t + 1], 1.0 / D_MODEL, 1e-6, ALU.mult, ALU.add).then_inc(ms_ready, 1)
                dve.wait_ge(rms_ready, t + 2)
                lk(V.reciprocal(sm[1][:, t:t + 1], sm[1][:, t:t + 1]))
                dve.wait_ge(router_in, 16 * 6)
                V.scalar_tensor_tensor(h2_tok[:, t, :], x1_tok[:, t, :], sm[1][:, t:t + 1], g2_bc, ALU.mult, ALU.mult
                                       ).then_inc(h2_ready, 1)
                if t == 0:
                    lk(V.tensor_copy(pri, idx_i[:, 0:32]))
                    lk(V.tensor_scalar(pri, pri, -1.0, 32.0, ALU.mult, ALU.add))
                    lk(V.memset(ones32, 1.0))
                    for b in range(8):
                        lk(V.memset(thr[:, :, b], float((b + 1) * BLOCK)))
                    lk(V.tensor_copy(item_w, idx_i[:, 0:MAX_EXTRA]))
                    lk(V.tensor_copy(item_f[0:1, 0:N_EXPERTS], idx_i[0:1, 0:N_EXPERTS]))
                    lk(V.tensor_scalar(home, idx_i[:, 0:32], float(BLOCK), None, ALU.mult))
            bc = lambda x, n: x.unsqueeze(2).broadcast_to([P, TILES, n])
            row = lambda x, n: x.unsqueeze(1).broadcast_to([P, TILES, n])
            dve.wait_ge(logit_mm, TILES)
            for t in range(TILES):
                lk(V.tensor_tensor(lg[:, t, :], bk[4][:, t * 36:(t + 1) * 36], br_bc, ALU.add))
            lk(V.tensor_reduce(sm[2], g_l, AX.X, ALU.max))
            lk(V.tensor_tensor(gs[0], g_l, bc(sm[2], 4), ALU.is_equal))
            V.tensor_tensor(gs[1], g_l, bc(sm[2], 4), ALU.subtract).then_inc(r_exp_in, 1)
            lk(V.tensor_tensor(gs[0], gs[0], row(pri[:, 0:4], 4), ALU.mult))
            lk(V.tensor_reduce(sm[3], gs[0], AX.X, ALU.max))
            lk(V.tensor_tensor(gs[0], gs[0], bc(sm[3], 4), ALU.is_equal))
            lk(V.tensor_scalar(gs[2], gs[0], -1.0, BIG, ALU.add, ALU.mult))
            for gg in range(N_GROUPS):
                lk(V.tensor_tensor(rt[0][:, :, gg * 8:gg * 8 + 8], e_l[:, :, gg * 8:gg * 8 + 8],
                                   gs[2][:, :, gg:gg + 1].broadcast_to([P, TILES, 8]), ALU.add))
            for k in range(2):
                top, oh = sm[6 + k], rt[1 + k]
                lk(V.tensor_reduce(top, rt[0], AX.X, ALU.max))
                lk(V.tensor_tensor(oh, rt[0], bc(top, 32), ALU.is_equal))
                lk(V.tensor_tensor(oh, oh, row(pri, 32), ALU.mult))
                lk(V.tensor_reduce(sm[8], oh, AX.X, ALU.max))
                lk(V.tensor_tensor(oh, oh, bc(sm[8], 32), ALU.is_equal))
                if k == 0:
                    lk(V.tensor_scalar(rt[3], oh, -3.0 * BIG, None, ALU.mult))
                    lk(V.tensor_tensor(rt[0], rt[0], rt[3], ALU.add))
            V.tensor_tensor(rt[3], rt[1], rt[2], ALU.add).then_inc(sel_ready, 1)
            V.tensor_tensor(sm[5], sm[7], sm[6], ALU.subtract).then_inc(r_exp_in, 1)
            dve.wait_ge(pos_mm, 1)
            lk(V.tensor_copy(rt[0][:, 0, :], bk[6][:, 0:32]))
            for t in range(1, TILES):
                lk(V.tensor_tensor(rt[0][:, t, :], rt[0][:, t - 1, :], bk[6][:, t * 32:(t + 1) * 32], ALU.add))
            lk(V.tensor_copy(rt[4][:, 0, :], bk[5][:, 0:32]))
            lk(V.tensor_tensor(rt[4][:, 1:TILES, :], rt[0][:, 0:TILES - 1, :],
                               bk[5][:, 32:P].rearrange("p (t n) -> p t n", n=32), ALU.add))
            lk(V.tensor_tensor(over, rt[0][:, TILES - 1, :].unsqueeze(2).broadcast_to([P, 32, 8]), thr, ALU.is_gt))
            lk(V.tensor_reduce(extra, over, AX.X, ALU.add))
            lk(V.tensor_tensor_scan(incl, ones32, extra, 0.0, ALU.mult, ALU.add))
            lk(V.tensor_tensor(away, incl, extra, ALU.subtract))
            lk(V.tensor_scalar(away, away, float(BLOCK), float((N_EXPERTS - 1) * BLOCK), ALU.mult, ALU.add))
            lk(V.tensor_tensor(away, away, home, ALU.subtract))
            lk(V.tensor_scalar(rt[6], rt[4], float(BLOCK), None, ALU.is_ge))
            lk(V.tensor_tensor(rt[6], rt[6], row(away, 32), ALU.mult))
            lk(V.tensor_tensor(rt[4], rt[4], row(home, 32), ALU.add))
            lk(V.tensor_tensor(rt[4], rt[4], rt[6], ALU.add))
            for k in range(2):
                lk(V.tensor_tensor(rt[5], rt[4], rt[1 + k], ALU.mult))
                lk(V.tensor_reduce(r_f[k], rt[5], AX.X, ALU.add))
                ins = V.tensor_copy(r_i[:, k * TILES:(k + 1) * TILES], r_f[k])
                ins.then_inc(rows_out, 1)
            lk(V.tensor_tensor(item_c[0:1], incl[0:1].unsqueeze(1).broadcast_to([1, MAX_EXTRA, 32]),
                               item_w[0:1].unsqueeze(2).broadcast_to([1, MAX_EXTRA, 32]), ALU.is_le))
            lk(V.tensor_reduce(item_f[0:1, N_EXPERTS:MAX_BLOCKS], item_c[0:1], AX.X, ALU.add))
            lk(V.tensor_scalar(item_f[0:1, N_EXPERTS:MAX_BLOCKS], item_f[0:1, N_EXPERTS:MAX_BLOCKS],
                               float(N_EXPERTS - 1), None, ALU.min))
            lk(V.tensor_scalar(item_w[0:1], item_w[0:1], incl[0:1, 31:32], None, ALU.is_lt))
            lk(V.tensor_reduce(s_small[0:1, 56:57], item_w[0:1, 0::2], AX.X, ALU.add))
            lk(V.tensor_scalar(item_f[0:1, MAX_BLOCKS:MAX_BLOCKS + 1], s_small[0:1, 56:57], float(N_EXPERTS // 2 - 1), None, ALU.add))
            V.tensor_copy(item_i[0:1, 0:MAX_BLOCKS + 1], item_f[0:1, 0:MAX_BLOCKS + 1]).then_inc(items_out, 1)
            dve.wait_ge(r_exp, 2)
            lk(V.tensor_reduce(sm[4], gs[1], AX.X, ALU.add))
            lk(V.tensor_scalar(sm[9], sm[5], 1.0, None, ALU.add))
            lk(V.tensor_tensor(sm[9], sm[9], sm[4], ALU.mult))
            lk(V.reciprocal(sm[10], sm[9]))
            lk(V.tensor_tensor(sm[11], sm[10], sm[5], ALU.mult))

            dve.wait_ge(items_out, 1)
            dve.wait_ge(scattered, 16 * 2 * TILES)
            last_pair = dve.value_load(item_i[0:1, MAX_BLOCKS:MAX_BLOCKS + 1], min_val=N_EXPERTS // 2 - 1, max_val=MAX_BLOCKS // 2 - 1)
            YST = [yst0, yst1]
            def expert_pair(i, first):
                for u in range(2):
                    w = i * 2 + u
                    dve.wait_ge(silu_ready, w + 1)
                    V.tensor_tensor(hid, silu_hi, bk[2 * u + 1][BLOCK:P, :], ALU.mult).then_inc(hid_ready, 1)
                    if not first:
                        dve.wait_ge(YST[u], i * 16)
                    dve.wait_ge(y2_mm, w + 1)
                    V.tensor_copy(y_out[u][:, 512:1024], bk[5][BLOCK:P, :]).then_inc(ycopy_b, 1)

            expert_pair(0, True)
            with dve.Fori(1, last_pair + 1) as i:
                expert_pair(i, False)
            for u in range(2):
                dve.wait_ge(YST[u], last_pair * 16 + 16)
                dve.wait_ge([xb_in0, xb_in1][u], last_pair * 16 + 32)
            V.memset(s_small[:, 57:58], 0.0).then_inc(experts_done, 1)
            YG = [yg_in0, yg_in1, yg_in2, yg_in3]

            def add_experts(t):
                for k in range(2):
                    dve.wait_ge(YG[t % 2 * 2 + k], 16 * (t // 2 + 1))
                    done(dve, V.scalar_tensor_tensor(x1_tok[:, t, :], y_rows[2 * t + k], sm[10 + k][:, t:t + 1], x1_tok[:, t, :],
                                                     ALU.mult, ALU.add), ysum, 2 * t + k + 1)

            def final_norm(t):
                dve.wait_ge(sumsq_ready, 2 * TILES + t + 1)
                V.tensor_scalar(sm[1][:, t:t + 1], sm[0][:, t:t + 1], 1.0 / D_MODEL, 1e-6, ALU.mult, ALU.add).then_inc(ms_ready, 1)
                dve.wait_ge(rms_ready, TILES + t + 2)
                lk(V.reciprocal(sm[1][:, t:t + 1], sm[1][:, t:t + 1]))
                V.scalar_tensor_tensor(x1_tok[:, t, :], x1_tok[:, t, :], sm[1][:, t:t + 1], gf_bc, ALU.mult, ALU.mult
                                       ).then_inc(final_ready, 1)

            add_experts(0)
            for t in range(TILES):
                if t + 1 < TILES:
                    add_experts(t + 1)
                final_norm(t)

        @block.tensor
        def _(pe):
            T = nc.tensor

            def mm(dst, lhsT, rhs, start, stop):
                return T.matmul(dst, lhsT, rhs, start=start, stop=stop, skip_group_check=True)

            def project(dst, slot, src, uses, m=P):
                pe.wait_ge(w_loaded[slot], uses)
                for k in range(KT):
                    last = mm(dst, ring[slot][:, k, 0:m], src[:, k, :], k == 0, k == KT - 1)
                last.then_inc(slot_done[slot], 1)

            pe.wait_ge(masks_ready, 1)
            pe.wait_ge(rows_in, 16 * 16)
            for i, (n, o) in enumerate([(90, 0), (120, P), (16, 2 * P), (16, 2 * P + 16)]):
                T.transpose(bk[7][:, o:o + n], rows[i][0:n, :], ident[0:n, 0:n]).then_inc(rows_tr, 1)
            for t in range(TILES):
                pe.wait_ge(xn_ready, t + 1)
                for h in range(2):
                    n = 2 * t + h
                    if n >= 4:
                        pe.wait_ge(hT_ready, n - 3)
                    for k in range(4):
                        last = T.transpose(bk[n % 4][:, k * P:(k + 1) * P], xn_tok[:, t, (4 * h + k) * P:(4 * h + k + 1) * P], ident)
                    last.then_inc(norm_tr, 1)
            pe.wait_ge(hT_ready, 2 * TILES)
            project(bk[0], 0, hT, 16)
            project(bk[1], 1, hT, 16)
            pe.wait_ge(dtw_in, 16)
            for k in range(KT):
                last = mm(bk[2][0:MAMBA_HEADS, :], dt_w[:, k, :], hT[:, k, :], k == 0, k == KT - 1)
            last.then_inc(dt_proj, 1)

            def group_tile(g, t):
                project(bk[t % 4], t % 5, hT, (g * 2 + BASE_GROUP[t % 5] + t // 5 + 1) * 16)

            def next_projection(c, i, more, steps=range(KT)):
                uses = (c + 2 + BASE_PAIR[i]) if more else BASE_GROUP[i] + 1
                if 0 in steps:
                    pe.wait_ge(w_loaded[i], uses * 16)
                for k in steps:
                    last = mm(bk[i], ring[i][:, k, :], hT[:, k, :], k == 0, k == KT - 1)
                if KT - 1 in steps:
                    last.then_inc(slot_done[i], 1)

            def decay_lora(n):
                mm(bk[7], lora_c[0], lo_wa, True, True).then_inc(lora_mm, 1)

            def rate_lora(n):
                pe.wait_ge(shifted, n * 3 + 1)
                mm(bk[0], lora_c[1], lo_wa, True, True).then_inc(lora_mm, 1)

            def kk_norm(n):
                pe.wait_ge(ksq_ready, n * 2 + 1)
                pe.wait_ge(lora_read, low_rank_count(n, 0))
                mm(bk[7], head_ones, ksq, True, True).then_inc(norm_mm, 1)

            def pair(c, more):
                def token_major(src, b):
                    for j in range(TILES):
                        last = T.transpose(bk[b][:, j * P:(j + 1) * P], src[:, j * P:(j + 1) * P], ident)
                    last.then_inc(tok_tr, 1)

                pe.wait_ge(lora_read, c * 3 + 2)
                pe.wait_ge(terms, c * 6 + 6)
                token_major(b_t, 5)
                token_major(k_t, 3)
                next_projection(c, 0, more)
                pe.wait_ge(shifted, c * 3 + 3)
                token_major(rkv[2], 4)
                pe.wait_ge(kb_rk, c * 2 + 1)
                pe.wait_ge(pair_prm_ready, c * 2 + 2)
                mm(bk[6], r_ones, rk, True, True).then_inc(bonus_mm, 1)
                pe.wait_ge(ar_ready, c * 4 + 4)
                pe.wait_ge(tok_ready, c * 3 + 3)
                for n in range(8):
                    j, of_k = n // 2, n % 2
                    if n >= 4:
                        pe.wait_ge(gram_ready, c * 8 + n - 3)
                    mm(bk[GRAM_BANKS[n % 4]], (k_t if of_k else b_t)[:, j * P:(j + 1) * P],
                       ar[:, j].rearrange("p f t -> p (f t)"), True, True).then_inc(gram_mm, 1)
                next_projection(c, 1, more)
                pe.wait_ge(gram_ready, c * 8 + 8)
                pe.wait_ge(ginit_ready, c + 1)

                def transpose_g(q):
                    for k in range(4):
                        o = q * 512 + k * P
                        last = T.transpose(bk[3 + q][:, k * P:(k + 1) * P], gi[:, o:o + P], ident)
                    last.then_inc(h_tr, 1)

                for q in range(2):
                    transpose_g(q)
                pe.wait_ge(bonus_ready, c + 1)
                for lv in range(1, LEVELS + 1):
                    pe.wait_ge(bm_ready, c * LEVELS + lv)
                    for q in range(2):
                        pe.wait_ge(h_ready, c * 12 + 2 * (lv - 1) + q + 1)
                        for k in range(4):
                            b_blk = bm[lv % 2][:, 2 * q + k // 2, k % 2, :]
                            last = mm(bk[3 + q][:, k * P:(k + 1) * P], b_blk, hi[:, q * 512 + k * P:q * 512 + (k + 1) * P], k == 0, k == 3)
                        last.then_inc(xt_mm, 1)
                    if more:
                        if lv == 1:
                            pe.wait_ge(lorac_ready, c * 3 + 4)
                            decay_lora(c + 1)
                        elif lv == 2:
                            rate_lora(c + 1)
                        elif lv == 3:
                            kk_norm(c + 1)
                    for q in range(2):
                        pe.wait_ge(xt_ready, c * 12 + 2 * (lv - 1) + q + 1)
                        for k in range(4):
                            o = q * 512 + k * P
                            last = mm(bk[5 + q][:, k * P:(k + 1) * P], xt[:, o:o + P], gi[:, o:o + P], k == 0, k == 3)
                        last.then_inc(g_mm, 1)
                    if lv < LEVELS:
                        for q in range(2):
                            pe.wait_ge(g_ready, c * 12 + 2 * (lv - 1) + q + 1)
                            transpose_g(q)
                pe.wait_ge(g_ready, c * 12 + 12)
                for j in range(TILES):
                    tj = slice(j * P, (j + 1) * P)
                    for h in range(2):
                        vh = slice(j * P + h * RWKV_HEAD, j * P + (h + 1) * RWKV_HEAD)
                        last = mm(bk[3][:, h * RWKV_HEAD:(h + 1) * RWKV_HEAD], gk[:, j, h, :], v_tok[:, vh], h == 0, h == 1 and j == 0)
                    if j > 0:
                        pe.wait_ge(s_ready, c * 6 + 2 * j)
                        last = mm(bk[3][:, 0:P], a_t[:, tj], st[j % 2], False, True)
                    last.then_inc(x1_mm, 1)
                    if j < TILES - 1:
                        mm(bk[5][:, 0:P], k_tok[:, tj], v_tok[:, tj], True, False)
                    if j > 0:
                        mm(bk[6][:, tj], r_t[:, tj], st[j % 2], True, False)
                    for h in range(2):
                        vh = slice(j * P + h * RWKV_HEAD, j * P + (h + 1) * RWKV_HEAD)
                        mm(bk[6][:, vh], gk[:, j, 2 + h, :], v_tok[:, vh], j == 0 and h == 0, False)
                    pe.wait_ge(x1_ready, c * 4 + j + 1)
                    for h in range(2):
                        o = slice(h * RWKV_HEAD, (h + 1) * RWKV_HEAD)
                        last = mm(bk[4][:, o], gi4[:, j, h, :], x1[:, o], h == 0, h == 1)
                    last.then_inc(u_mm, 1)
                    next_projection(c, 2, more, [j])
                    pe.wait_ge(u_ready, c * 4 + j + 1)
                    if j < TILES - 1:
                        mm(bk[5][:, 0:P], b_tok[:, tj], u_sb, False, True).then_inc(d_mm, 1)
                    for h in range(2):
                        o = slice(h * RWKV_HEAD, (h + 1) * RWKV_HEAD)
                        last = mm(bk[6][:, j * P + h * RWKV_HEAD:j * P + (h + 1) * RWKV_HEAD], gb[:, j, 2 + h, :], u_sb[:, o], False, True)
                    last.then_inc(y_mm, 1)
                pe.wait_ge(lorac_ready, c * 3 + (5 if more else 3))
                mm(bk[3], lora_c[2], lo_g, True, True).then_inc(lora_mm, 1)
                next_projection(c, 2, more, range(TILES, KT))
                if more:
                    pe.wait_ge(nrm_ready, c + 2)
                pe.wait_ge(head_norm, c * 3 + 3)
                for j in range(TILES):
                    last = T.transpose(bk[7][:, j * P:(j + 1) * P], y_c[:, j * P:(j + 1) * P], ident)
                last.then_inc(pe_pair, 1)

            pe.wait_ge(lo_shifted, 2)
            for i in range(2):
                project(bk[i], i, hT, (1 + BASE_PAIR[i]) * 16)
            pe.wait_ge(dt_dve, 3)
            for i, src in enumerate([dtw[4], dtw[1]]):
                for j in range(TILES):
                    o = i * P + j * MAMBA_HEADS
                    last = T.transpose(bk[3][:, o:o + MAMBA_HEADS], src[:, j * P:(j + 1) * P], ident[0:MAMBA_HEADS, 0:MAMBA_HEADS])
            last.then_inc(dt_tr, 1)
            pe.wait_ge(dt_dve, 1)

            def first_v(steps):
                for k in steps:
                    last = mm(bk[2], ring[2][:, k, :], hT[:, k, :], k == 0, k == KT - 1)
                if KT - 1 in steps:
                    last.then_inc(slot_done[2], 1)

            pe.wait_ge(w_loaded[2], (1 + BASE_PAIR[2]) * 16)
            first_v(range(0, 4))
            pe.wait_ge(lorac_ready, 2)
            pe.wait_ge(lo_ready, 2)
            decay_lora(0)
            rate_lora(0)
            first_v(range(4, 6))
            kk_norm(0)
            first_v(range(6, KT))
            with pe.Fori(0, PAIRS - 1) as c:
                pair(c, True)
            pair(PAIRS - 1, False)

            def group(g, more):
                for t in range(4, 8):
                    pe.wait_ge(taps_done, g * 6 + t - 3)
                    group_tile(g, t)
                pe.wait_ge(xbc_ready, g * 6 + 5)
                for j in range(TILES):
                    tj = slice(j * P, (j + 1) * P)
                    last = T.transpose(bk[6][:, tj], xbcT[:, 4, tj], ident)
                last.then_inc(bt_tr, 1)
                for j in range(TILES):
                    tj = slice(j * P, (j + 1) * P)
                    if j >= 2:
                        pe.wait_ge(xdt_ready, g * 4 + j - 1)
                    for m in range(4):
                        last = T.transpose(bk[4 + j % 2][:, m * P:(m + 1) * P], xbcT[:, m, tj], ident)
                    last.then_inc(xt_tr, 1)
                pe.wait_ge(taps_done, g * 6 + 5)
                group_tile(g, 8)

                def scores(j):
                    if j > 0:
                        pe.wait_ge(m_ready, g * 4 + j)
                    tj = slice(j * P, (j + 1) * P)
                    mm(bk[6][:, 0:P], xbcT[:, 4, tj], xbcT[:, 5, tj], True, True).then_inc(cb_mm, 1)

                def state_part(j):
                    pe.wait_ge(xe_ready, g * 3 + j + 1)
                    if j > 0:
                        pe.wait_ge(st_ready, g * 3 + j)
                    mm(bk[7], b_tk[:, j * P:(j + 1) * P], xe[j % 2], True, True).then_inc(st_mm, 1)

                def outputs(j):
                    pe.wait_ge(m_ready, g * 4 + j + 1)
                    if j > 0:
                        pe.wait_ge(c_ready, g * 3 + j)
                        pe.wait_ge(st_ready, g * 3 + j)
                    if j >= 2:
                        pe.wait_ge(yskip_ready, g * 4 + j - 1)
                    for h in range(8):
                        half, m = h % 2, h // 2
                        dst = bk[4 + j % 2][half * 64:half * 64 + 64, m * P:(m + 1) * P]
                        hs = slice(h * RWKV_HEAD, (h + 1) * RWKV_HEAD)
                        last = mm(dst, xdt[:, j, hs], m_sb[j % 2][:, h, :], m == 0, j == 0)
                        if j > 0:
                            last = mm(dst, state[j % 2][:, hs], c_sb[j % 2][:, h, :], False, True)
                    last.then_inc(ym_mm, 1)

                filler = [(9, k) for k in range(KT)] + [(t, k) for t in range(4) for k in range(KT) if more]

                def fill(first, end):
                    for t, k in filler[first:end]:
                        s = t % 5
                        if k == 0:
                            if t == 9:
                                pe.wait_ge(taps_done, g * 6 + 6)
                            else:
                                pe.wait_ge(z_ready, g * 4 + [3, 4, 1, 2][t])
                            pe.wait_ge(w_loaded[s], (g * 2 + BASE_GROUP[s] + (2 if t == 9 else 3)) * 16)
                        last = mm(bk[t % 4], ring[s][:, k, :], hT[:, k, :], k == 0, k == KT - 1)
                        if k == KT - 1:
                            last.then_inc(slot_done[s], 1)

                pe.wait_ge(bt_tok_ready, g + 1)
                pe.wait_ge(xbc_ready, g * 6 + 6)
                pe.wait_ge(xdt_ready, g * 4 + 4)
                scores(0)
                fill(0, 4)
                state_part(0)
                for j in range(TILES - 1):
                    scores(j + 1)
                    outputs(j)
                    if j < TILES - 2:
                        fill(4 + 5 * j, 9 + 5 * j)
                        state_part(j + 1)
                fill(14, 20)
                outputs(TILES - 1)
                fill(20, 28)
                pe.wait_ge(ysq_summed, g + 1)
                mm(bk[6], ones, ysq2[:, 0:SEQ], True, True).then_inc(gn_mm, 1)
                fill(28, 40)

            pe.wait_ge(lora_read, PAIRS * 3)
            group_tile(0, 3)
            with pe.Fori(0, GROUPS - 1) as g:
                group(g, True)
            group(GROUPS - 1, False)

            def merge_products(jj, first):
                for u in range(2):
                    if not first:
                        pe.wait_ge(merged_ready, jj * 2 + u - 1)
                    for s in range(5):
                        uses = (jj * 2 + u + BASE_MERGE[s] + 1) * 16
                        src = [ygT, hT, hT, ymT[:, 0:KT], ymT[:, KT:2 * KT]][s]
                        pe.wait_ge(w_loaded[s], uses)
                        if first and u == 0 and s == 3:
                            pe.wait_ge(dve_group, GROUPS)
                        for k in range(KT):
                            last = mm(bk[4 * u + min(s, 3)], ring[s][:, k, :], src[:, k, :], k == 0 and s < 4, k == KT - 1 and s != 3)
                        last.then_inc(slot_done[s], 1)

            merge_products(0, True)
            with pe.Fori(1, KT // 2) as jj:
                merge_products(jj, False)
            def transpose_h2(t):
                pe.wait_ge(h2_ready, t + 1)
                for h in range(2):
                    if t > 0:
                        pe.wait_ge(h2T_ready, 2 * t + h - 1)
                    for k in range(4):
                        last = T.transpose(bk[6 + h][:, k * P:(k + 1) * P], h2_tok[:, t, (4 * h + k) * P:(4 * h + k + 1) * P], ident)
                    last.then_inc(norm_tr, 1)

            def logits(t):
                pe.wait_ge(router_in, 16 * 6)
                pe.wait_ge(h2T_ready, 2 * t + 2)
                for k in range(KT):
                    last = mm(bk[4][:, t * 36:(t + 1) * 36], h2T[:, k, t * P:(t + 1) * P], wr_sb[:, k, :], k == 0, k == KT - 1)
                last.then_inc(logit_mm, 1)

            pe.wait_ge(merged_ready, KT)
            pe.wait_ge(w_out_in, 32)
            for t in range(TILES):
                for h in range(2):
                    n = 2 * t + h
                    if n >= 4:
                        pe.wait_ge(x1_done, n - 3)
                    for k in range(KT):
                        last = mm(bk[n % 4], merged[:, k, t * P:(t + 1) * P], w_out_sb[:, k, h * 512:(h + 1) * 512], k == 0, k == KT - 1)
                    last.then_inc(out_mm, 1)
                if t >= 1:
                    transpose_h2(t - 1)
                if t >= 2:
                    logits(t - 2)
            logits(TILES - 2)
            transpose_h2(TILES - 1)
            logits(TILES - 1)
            pe.wait_ge(sel_ready, 1)
            picks = rt[3].rearrange("p t n -> p (t n)")
            mm(bk[5][:, 0:P], tri2[:, 0:P], picks, True, True)
            mm(bk[6][:, 0:P], ones, picks, True, True).then_inc(pos_mm, 1)

            pe.wait_ge(items_out, 1)
            last_pair = pe.value_load(item_i[0:1, MAX_BLOCKS:MAX_BLOCKS + 1], min_val=N_EXPERTS // 2 - 1, max_val=MAX_BLOCKS // 2 - 1)
            W1_IN, W3_IN, W2_IN, XB_IN = [w1_in0, w1_in1], [w3_in0, w3_in1], [w2_in0, w2_in1], [xb_in0, xb_in1]

            def rows_in_block(w, u, seen):
                pe.wait_ge(XB_IN[u], seen)
                for k in range(KT):
                    last = mm(bk[6][:, k * BLOCK:(k + 1) * BLOCK], xs_sb[u][:, k::KT], ident[0:BLOCK, 0:BLOCK], True, True)
                last.then_inc(xg_tr, 1)

            def first_products(w, u, seen):
                pe.wait_ge(xg_ready, w + 1)
                pe.wait_ge(W1_IN[u], seen)
                pe.wait_ge(W3_IN[u], seen)
                for k in range(KT):
                    mm(bk[2 * u][0:BLOCK, :], xgT[:, k, :], w1_sb[u][:, k, :], k == 0, k == KT - 1)
                    last = mm(bk[2 * u + 1][BLOCK:P, :], xgT[:, k, :], w3_sb[u][:, k, :], k == 0, k == KT - 1)
                last.then_inc(h13_mm, 1)

            def expert_pair(i, first, final):
                for u in range(2):
                    w = i * 2 + u
                    more = not (final and u == 1)
                    next_seen = (i + 1 + u) * 16
                    if more:
                        rows_in_block(w + 1, 1 - u, next_seen)
                    pe.wait_ge(hid_ready, w + 1)
                    for k in range(FT):
                        last = mm(bk[7][:, k * BLOCK:(k + 1) * BLOCK], hid[:, k::FT], ident[0:BLOCK, 0:BLOCK], True, True)
                    last.then_inc(hid_tr, 1)
                    if more:
                        first_products(w + 1, 1 - u, next_seen)
                    pe.wait_ge(hidT_ready, w + 1)
                    pe.wait_ge(W2_IN[u], (i + 1) * 16)
                    if not first or u > 0:
                        pe.wait_ge(ycopy_a, w)
                        pe.wait_ge(ycopy_b, w)
                    for k in range(FT):
                        mm(bk[4][0:BLOCK, :], hidT[:, k, :], w2_sb[u][:, k, 0:512], k == 0, k == FT - 1)
                        last = mm(bk[5][BLOCK:P, :], hidT[:, k, :], w2_sb[u][:, k, 512:1024], k == 0, k == FT - 1)
                    last.then_inc(y2_mm, 1)

            rows_in_block(0, 0, 16)
            first_products(0, 0, 16)
            expert_pair(0, True, False)
            with pe.Fori(1, last_pair) as i:
                expert_pair(i, False, False)
            expert_pair(last_pair, False, True)


_INS = ['x', 'norm1_g', 'w_in', 'mu_rwkv', 'w0', 'w_decay2', 'a0', 'w_iclr2', 'w_gate2', 'k_k', 'k_a', 'r_k', 'lnx_g',
        'lnx_b', 'w_rwkv_o', 'conv_w', 'conv_b', 'dt_bias', 'a_log', 'd_skip', 'mnorm_g', 'w_mamba_o', 'w_out', 'norm2_g',
        'w_rg', 'b_rg', 'w_re', 'b_re', 'w_e1', 'w_e3', 'w_e2', 'final_g']


def kernel(**inputs):
    import numpy as np
    import concourse.bacc as bacc
    from concourse.bass_utils import run_bass_kernel_spmd

    nc = bacc.Bacc("TRN2", target_bir_lowering=False, num_devices=1)
    arrays, aps = {}, {}
    for name in _INS:
        arrays[f"in_{name}"] = np.ascontiguousarray(inputs[name])
        aps[name] = nc.dram_tensor(f"in_{name}", arrays[f"in_{name}"].shape, F32, kind="ExternalInput").ap()
    out = nc.dram_tensor("out_0", (1, SEQ, D_MODEL), F32, kind="ExternalOutput").ap()
    hybrid_block_kernel(nc, aps, out)
    r = run_bass_kernel_spmd(nc, [arrays], core_ids=[0])
    return r.results[0]["out_0"]
```
